# Optimizing a Trainium2 kernel written in Bass

```python
import jax, jax.numpy as jnp
from jax import lax
import numpy as np
import math

D_MODEL = 1024
BATCH = 1
SEQ = 512
DEPTH = 2

HEAD_DIM = 64
CONV_CH = D_MODEL // 4
CONV_WIDTH = 31
ATT_WIDTH = 3 * D_MODEL // 8
N_ATT_HEADS = ATT_WIDTH // HEAD_DIM
DILATION_PAIRS = ((128, 1), (512, 4), (2048, 16))
ATT_BLOCK = 128
ALIBI_MAX_EXP = 8.0
MASK_VALUE = -1e30
REC_WIDTH = 3 * D_MODEL // 8
REC_KEY_DIM = 64
REC_VAL_DIM = 64
N_REC_HEADS = REC_WIDTH // REC_VAL_DIM
REC_KEY_WIDTH = N_REC_HEADS * REC_KEY_DIM
REC_CHUNK = 64
F_TINY = 1e-30
MIX_WIDTH = CONV_CH + ATT_WIDTH + REC_WIDTH
IN_SPLITS = (CONV_CH, CONV_CH, ATT_WIDTH, ATT_WIDTH, ATT_WIDTH,
             REC_KEY_WIDTH, REC_KEY_WIDTH, REC_KEY_WIDTH, REC_WIDTH, REC_WIDTH)
IN_COLS = sum(IN_SPLITS)
D_FF = ((8 * D_MODEL // 3 + 127) // 128) * 128
FFN_CONV_WIDTH = 3
N_MOD = 6
EPS = 1e-6


def _rmsnorm(x, w):
    xf = x.astype(jnp.float32)
    y = xf * lax.rsqrt(jnp.mean(xf * xf, axis=-1, keepdims=True) + EPS)
    return (y * w.astype(jnp.float32)).astype(x.dtype)

def _layernorm(x, w, b):
    xf = x.astype(jnp.float32)
    mu = jnp.mean(xf, axis=-1, keepdims=True)
    var = jnp.mean(jnp.square(xf - mu), axis=-1, keepdims=True)
    y = (xf - mu) * lax.rsqrt(var + EPS)
    return (y * w.astype(jnp.float32) + b.astype(jnp.float32)).astype(x.dtype)

def _depthwise_conv(x, w, b=None):
    k_w, ch = w.shape
    y = lax.conv_general_dilated(
        x, w[:, None, :].astype(x.dtype), window_strides=(1,),
        padding=[(k_w // 2, k_w // 2)],
        dimension_numbers=('NWC', 'WIO', 'NWC'), feature_group_count=ch)
    if b is not None:
        y = y + b.astype(x.dtype)
    return y

def _dilated_window_attention(q, k, v, slopes, window, dilation):
    B, S, H, Dh = q.shape
    half = window // (2 * dilation)
    L = S // dilation

    def to_sub(t):
        return t.reshape(B, L, dilation, H, Dh).transpose(0, 2, 1, 3, 4).reshape(B * dilation, L, H, Dh)

    qs, ks, vs = to_sub(q), to_sub(k), to_sub(v)
    blk = min(ATT_BLOCK, L)
    nb = -(-L // blk)
    Lp = nb * blk
    span = blk + 2 * half
    qs = jnp.pad(qs, ((0, 0), (0, Lp - L), (0, 0), (0, 0)))
    pad_k = ((0, 0), (half, half + Lp - L), (0, 0), (0, 0))
    ks = jnp.pad(ks, pad_k)
    vs = jnp.pad(vs, pad_k)
    idx = (np.arange(nb) * blk)[:, None] + np.arange(span)[None, :]
    kb = ks[:, idx]
    vb = vs[:, idx]
    qb = qs.reshape(B * dilation, nb, blk, H, Dh)
    rel = np.arange(span)[None, :] - half - np.arange(blk)[:, None]
    key_pos = idx - half
    valid = ((np.abs(rel) <= half)[None]
             & (key_pos[:, None, :] >= 0) & (key_pos[:, None, :] < L))
    dist = jnp.asarray(np.abs(rel) * dilation, jnp.float32)
    scores = jnp.einsum('bnqhd,bnkhd->bnhqk', qb, kb) * (Dh ** -0.5)
    scores = scores - slopes[:, None, None] * dist
    scores = jnp.where(jnp.asarray(valid)[:, None], scores, MASK_VALUE)
    lse = jax.nn.logsumexp(scores, axis=-1)
    p = jnp.exp(scores - lse[..., None])
    o = jnp.einsum('bnhqk,bnkhd->bnqhd', p, vb).reshape(B * dilation, Lp, H, Dh)[:, :L]
    lse = lse.transpose(0, 1, 3, 2).reshape(B * dilation, Lp, H)[:, :L]

    def from_sub(t):
        t5 = t.reshape((B, dilation, L) + t.shape[2:])
        t5 = jnp.moveaxis(t5, 1, 2)
        return t5.reshape((B, S) + t5.shape[3:])

    return from_sub(o), from_sub(lse)

def _mixture_of_dilated_attention(q, k, v):
    slopes = jnp.asarray(2.0 ** (-ALIBI_MAX_EXP * np.arange(1, N_ATT_HEADS + 1) / N_ATT_HEADS), jnp.float32)
    outs, lses = [], []
    for window, dilation in DILATION_PAIRS:
        o_g, l_g = _dilated_window_attention(q, k, v, slopes, window, dilation)
        outs.append(o_g)
        lses.append(l_g)
    wts = jax.nn.softmax(jnp.stack(lses, 0), axis=0)
    return jnp.einsum('gbsh,gbshd->bshd', wts, jnp.stack(outs, 0))

def _hgrn2_scan(q, k, v, logf):
    B, S, H, dk = q.shape
    dv = v.shape[-1]
    n = S // REC_CHUNK

    def chunks(t):
        return t.reshape(B, n, REC_CHUNK, H, t.shape[-1]).transpose(1, 0, 3, 2, 4)

    qc, kc, vc = chunks(q), chunks(k), chunks(v)
    bc = jnp.cumsum(chunks(logf), axis=3)
    lower = jnp.asarray(np.tril(np.ones((REC_CHUNK, REC_CHUNK), bool)))[:, :, None]

    def step(state, inp):
        qt, kt, vt, bt = inp
        diff = bt[:, :, :, None, :] - bt[:, :, None, :, :]
        decay = jnp.where(lower, jnp.exp(jnp.where(lower, diff, 0.0)), 0.0)
        scores = jnp.einsum('bhtk,bhsk,bhtsk->bhts', qt, kt, decay)
        o = (jnp.einsum('bhts,bhsv->bhtv', scores, vt)
             + jnp.einsum('bhtk,bhkv->bhtv', qt * jnp.exp(bt), state))
        b_last = bt[:, :, -1:, :]
        state = (jnp.exp(b_last[:, :, 0, :])[..., None] * state
                 + jnp.einsum('bhsk,bhsv->bhkv', kt * jnp.exp(b_last - bt), vt))
        return state, o

    state0 = jnp.zeros((B, H, dk, dv), q.dtype)
    _, o = lax.scan(step, state0, (qc, kc, vc, bc))
    return o.transpose(1, 0, 3, 2, 4).reshape(B, S, H, dv)

def _hgrn2_gate(z, lb):
    f = lb + (1.0 - lb) * jax.nn.sigmoid(z)
    logf = jnp.log(jnp.maximum(f, F_TINY))
    k = (1.0 - lb) * jax.nn.sigmoid(-z)
    return logf, k

def _token_mixers(h, w_in, conv_w, conv_b, ln_w, ln_b, lb_fwd, lb_bwd, rec_norm_w, w_out):
    B, S, _ = h.shape
    f32 = jnp.float32
    proj = h @ w_in.astype(h.dtype)
    cuts = [int(c) for c in np.cumsum(IN_SPLITS)[:-1]]
    (a_val, a_gate, q_att, k_att, v_att,
     q_rec, z_fwd, z_bwd, i_rec, g_rec) = jnp.split(proj, cuts, axis=-1)

    a = a_val * jax.nn.sigmoid(a_gate)
    a = _depthwise_conv(a, conv_w, conv_b)
    a = jax.nn.silu(_layernorm(a, ln_w, ln_b))

    def heads(t, d):
        return t.astype(f32).reshape(B, S, -1, d)
    att = _mixture_of_dilated_attention(heads(q_att, HEAD_DIM), heads(k_att, HEAD_DIM), heads(v_att, HEAD_DIM))
    att = att.reshape(B, S, ATT_WIDTH).astype(h.dtype)

    qr = heads(jax.nn.silu(q_rec.astype(f32)), REC_KEY_DIM)
    vr = heads(i_rec, REC_VAL_DIM)
    logf_f, k_f = _hgrn2_gate(z_fwd.astype(f32), lb_fwd)
    logf_b, k_b = _hgrn2_gate(z_bwd.astype(f32), lb_bwd)
    o_f = _hgrn2_scan(qr, heads(k_f, REC_KEY_DIM), vr, heads(logf_f, REC_KEY_DIM))
    flip = lambda t: jnp.flip(t, axis=1)
    o_b = flip(_hgrn2_scan(flip(qr), flip(heads(k_b, REC_KEY_DIM)), flip(vr), flip(heads(logf_b, REC_KEY_DIM))))
    o_r = o_f + o_b
    o_r = o_r * lax.rsqrt(jnp.mean(o_r * o_r, axis=-1, keepdims=True) + EPS)
    o_r = o_r.reshape(B, S, REC_WIDTH) * rec_norm_w.astype(f32)
    rec = (o_r * jax.nn.silu(g_rec.astype(f32))).astype(h.dtype)

    mixed = jnp.concatenate([a, att, rec], axis=-1)
    return mixed @ w_out.astype(h.dtype)

def _conv_ffn(h, w_up, conv_w, w_down):
    u = h @ w_up.astype(h.dtype)
    u = _depthwise_conv(u, conv_w)
    gate, val = jnp.split(u, 2, axis=-1)
    return (jax.nn.gelu(gate, approximate=False) * val) @ w_down.astype(h.dtype)

def first_inputs(seed: int = 0) -> dict:
    key = jax.random.key(seed)
    ks = jax.random.split(key, 18)
    f32 = jnp.float32
    D = D_MODEL

    def nrm(k, shape, scale):
        return jax.random.normal(k, shape, f32) * scale

    return {
        "x": nrm(ks[0], (BATCH, SEQ, D), 1.0),
        "c": nrm(ks[1], (BATCH, D), 1.0),
        "w_ada": nrm(ks[2], (DEPTH, D, N_MOD * D), 0.5 * D ** -0.5),
        "b_ada": nrm(ks[3], (DEPTH, N_MOD * D), 0.02),
        "norm1_w": 1.0 + nrm(ks[4], (DEPTH, D), 0.05),
        "w_in": nrm(ks[5], (DEPTH, D, IN_COLS), D ** -0.5),
        "conv_a_w": nrm(ks[6], (DEPTH, CONV_WIDTH, CONV_CH), CONV_WIDTH ** -0.5),
        "conv_a_b": nrm(ks[7], (DEPTH, CONV_CH), 0.02),
        "ln_a_w": 1.0 + nrm(ks[8], (DEPTH, CONV_CH), 0.05),
        "ln_a_b": nrm(ks[9], (DEPTH, CONV_CH), 0.02),
        "lb_gamma": nrm(ks[10], (DEPTH, 2, REC_KEY_WIDTH), 1.0),
        "rec_norm_w": 1.0 + nrm(ks[11], (DEPTH, REC_WIDTH), 0.05),
        "w_out": nrm(ks[12], (DEPTH, MIX_WIDTH, D), MIX_WIDTH ** -0.5),
        "norm2_w": 1.0 + nrm(ks[13], (DEPTH, D), 0.05),
        "w_up": nrm(ks[14], (DEPTH, D, 2 * D_FF), D ** -0.5),
        "conv_f_w": nrm(ks[15], (DEPTH, FFN_CONV_WIDTH, 2 * D_FF), FFN_CONV_WIDTH ** -0.5),
        "w_down": nrm(ks[16], (DEPTH, D_FF, D), D_FF ** -0.5),
        "final_norm_w": 1.0 + nrm(ks[17], (D,), 0.05),
    }

def first_block(x, c, w_ada, b_ada, norm1_w, w_in, conv_a_w, conv_a_b, ln_a_w, ln_a_b,
              lb_gamma, rec_norm_w, w_out, norm2_w, w_up, conv_f_w, w_down, final_norm_w):
    p = jax.nn.softmax(lb_gamma.astype(jnp.float32), axis=0)
    lower_bounds = jnp.cumsum(p, axis=0) - p[0:1]
    cond = jax.nn.silu(c)
    for l in range(DEPTH):
        mod = (cond @ w_ada[l] + b_ada[l]).astype(x.dtype)[:, None, :]
        sh1, sc1, g1, sh2, sc2, g2 = jnp.split(mod, N_MOD, axis=-1)
        h = _rmsnorm(x, norm1_w[l]) * (1.0 + sc1) + sh1
        x = x + g1 * _token_mixers(h, w_in[l], conv_a_w[l], conv_a_b[l], ln_a_w[l], ln_a_b[l],
                                   lower_bounds[l, 0], lower_bounds[l, 1], rec_norm_w[l], w_out[l])
        h = _rmsnorm(x, norm2_w[l]) * (1.0 + sc2) + sh2
        x = x + g2 * _conv_ffn(h, w_up[l], conv_f_w[l], w_down[l])
    return _rmsnorm(x, final_norm_w)


CHUNK = 64
Q_BLOCK = 128
ATT_HEADS = 8
ATT_HEAD_DIM = 64
IDX_HEADS = 8
IDX_DIM = 64
TOPK_MAX = 256
ROPE_THETA = 500000.0
ROPE_FRACTION_DIV = 4
GLA_HEADS = 4
GLA_DK = 128
GLA_DV = 256
GLA_GATE_RANK = 16
GLA_TAU = 16.0
D_FF_2 = 2816
CONV_WIDTH_2 = 3
LN_EPS = 1e-5
DN_ALPHA = (2.0 * DEPTH) ** 0.25
DN_BETA = (8.0 * DEPTH) ** -0.25

ATT_WIDTH_2 = ATT_HEADS * ATT_HEAD_DIM
IDXQ_WIDTH = IDX_HEADS * IDX_DIM
GLA_K_WIDTH = GLA_HEADS * GLA_DK
GLA_V_WIDTH = GLA_HEADS * GLA_DV
IN_SPLITS_2 = (ATT_WIDTH_2, ATT_WIDTH_2, ATT_WIDTH_2,
             IDXQ_WIDTH, IDX_DIM, IDX_HEADS,
             GLA_K_WIDTH, GLA_K_WIDTH, GLA_V_WIDTH, GLA_GATE_RANK, GLA_V_WIDTH,
             D_MODEL, D_MODEL)
IN_WIDTH = sum(IN_SPLITS_2)


F32 = jnp.float32

def layer_norm(x, g, b):
    xf = x.astype(F32)
    mu = jnp.mean(xf, axis=-1, keepdims=True)
    var = jnp.mean(jnp.square(xf - mu), axis=-1, keepdims=True)
    return ((xf - mu) * lax.rsqrt(var + LN_EPS) * g.astype(F32) + b.astype(F32)).astype(x.dtype)

def partial_rope(x, pos):
    dh = x.shape[-1]
    rd = dh // ROPE_FRACTION_DIV
    half = rd // 2
    inv = ROPE_THETA ** (-jnp.arange(half, dtype=F32) * 2.0 / rd)
    ang = pos.astype(F32)[..., None] * inv
    cos = jnp.cos(ang)[:, :, None, :]
    sin = jnp.sin(ang)[:, :, None, :]
    xr = x[..., :rd].astype(F32)
    x1, x2 = xr[..., :half], xr[..., half:]
    rot = jnp.concatenate([x1 * cos - x2 * sin, x2 * cos + x1 * sin], axis=-1)
    return jnp.concatenate([rot.astype(x.dtype), x[..., rd:]], axis=-1)

def dsa_attention(q, k, v, q_idx, k_idx, w_idx):
    B, S, H, Dh = q.shape
    topk = min(TOPK_MAX, S // 4)
    nb = S // Q_BLOCK
    key_chunk = jnp.arange(S) // CHUNK
    k_idx32 = k_idx.astype(F32)

    def to_blocks(a):
        return jnp.moveaxis(a.reshape((B, nb, Q_BLOCK) + a.shape[2:]), 1, 0)

    def block(args):
        qb, qib, wb, start = args
        q_chunk = (start + jnp.arange(Q_BLOCK)) // CHUNK
        admissible = key_chunk[None, :] <= q_chunk[:, None]
        dots = jnp.einsum('bqhd,bsd->bqhs', qib.astype(F32), k_idx32) * (IDX_DIM ** -0.5)
        score = jnp.einsum('bqhs,bqh->bqs', jax.nn.relu(dots),
                           wb.astype(F32) * (IDX_HEADS ** -0.5))
        score = jnp.where(admissible[None], score, -jnp.inf)
        top_val, top_idx = lax.top_k(score, topk)
        valid = jnp.isfinite(top_val)
        k_sel = jax.vmap(lambda kk, ii: kk[ii])(k, top_idx)
        v_sel = jax.vmap(lambda vv, ii: vv[ii])(v, top_idx)
        logits = jnp.einsum('bqhd,bqkhd->bhqk', qb.astype(F32), k_sel.astype(F32)) * (Dh ** -0.5)
        logits = jnp.where(valid[:, None], logits, -jnp.inf)
        p = jax.nn.softmax(logits, axis=-1)
        return jnp.einsum('bhqk,bqkhd->bqhd', p, v_sel.astype(F32)).astype(q.dtype)

    starts = jnp.arange(nb) * Q_BLOCK
    out = lax.map(block, (to_blocks(q), to_blocks(q_idx), to_blocks(w_idx), starts))
    return jnp.moveaxis(out, 0, 1).reshape(B, S, H, Dh)

def gla_chunked(q, k, v, log_a):
    B, S, H, Dk = q.shape
    Dv = v.shape[-1]
    nc = S // CHUNK

    def chunks(a):
        return jnp.moveaxis(a.astype(F32).reshape((B, nc, CHUNK) + a.shape[2:]), 1, 0)

    def step(state, inp):
        qc, kc, vc, lac = inp
        cum = jnp.cumsum(lac, axis=1)
        total = cum[:, -1]
        k_dec = kc * jnp.exp(total[:, None] - cum)
        state = jnp.exp(total)[..., None] * state + jnp.einsum('bchk,bchv->bhkv', k_dec, vc)
        out = jnp.einsum('bchk,bhkv->bchv', qc, state)
        return state, out

    s0 = jnp.zeros((B, H, Dk, Dv), F32)
    _, o = lax.scan(step, s0, (chunks(q) * (Dk ** -0.5), chunks(k), chunks(v), chunks(log_a)))
    return jnp.moveaxis(o, 0, 1).reshape(B, S, H, Dv)

def hybrid_mixer(x, pos, w_in, gla_w_gate, gla_b_gate, gla_norm_g, p_attn, p_gla, w_out, b_out):
    B, S, _ = x.shape
    proj = x @ w_in
    offsets = np.cumsum(IN_SPLITS_2)[:-1].tolist()
    (aq, ak, av, iq, ik, iw, gq, gk, gv, g_lr, g_r, gate_a, gate_b) = jnp.split(proj, offsets, axis=-1)

    aq = partial_rope(aq.reshape(B, S, ATT_HEADS, ATT_HEAD_DIM), pos)
    ak = partial_rope(ak.reshape(B, S, ATT_HEADS, ATT_HEAD_DIM), pos)
    av = av.reshape(B, S, ATT_HEADS, ATT_HEAD_DIM)
    iq = partial_rope(iq.reshape(B, S, IDX_HEADS, IDX_DIM), pos)
    ik = partial_rope(ik[:, :, None, :], pos)[:, :, 0, :]
    ya = dsa_attention(aq, ak, av, iq, ik, iw).reshape(B, S, ATT_WIDTH_2) @ p_attn

    gate_logits = g_lr @ gla_w_gate + gla_b_gate
    log_a = jax.nn.log_sigmoid(gate_logits.astype(F32)) / GLA_TAU
    o = gla_chunked(gq.reshape(B, S, GLA_HEADS, GLA_DK),
                    gk.reshape(B, S, GLA_HEADS, GLA_DK),
                    gv.reshape(B, S, GLA_HEADS, GLA_DV),
                    log_a.reshape(B, S, GLA_HEADS, GLA_DK))
    mu = jnp.mean(o, axis=-1, keepdims=True)
    var = jnp.mean(jnp.square(o - mu), axis=-1, keepdims=True)
    o = (o - mu) * lax.rsqrt(var + LN_EPS) * gla_norm_g.astype(F32).reshape(GLA_HEADS, GLA_DV)
    o = o.reshape(B, S, GLA_V_WIDTH).astype(x.dtype) * jax.nn.silu(g_r)
    yb = o @ p_gla

    merged = jax.nn.sigmoid(gate_a) * ya + jax.nn.sigmoid(gate_b) * yb
    return merged @ w_out + b_out

def conv_ffn(x, w_up, conv_w, conv_b, w_down):
    u = x @ w_up
    c = u.shape[-1]
    u = lax.conv_general_dilated(u, conv_w[:, None, :], window_strides=(1,),
                                 padding=[(CONV_WIDTH_2 - 1, 0)],
                                 dimension_numbers=('NWC', 'WIO', 'NWC'),
                                 feature_group_count=c) + conv_b
    a, b = jnp.split(u, 2, axis=-1)
    return (jax.nn.gelu(a) * b) @ w_down

def second_inputs(seed: int = 0) -> dict:
    key = jax.random.key(seed)
    ks = jax.random.split(key, 20)
    L, D = DEPTH, D_MODEL
    nrm = lambda k, shape, s: jax.random.normal(k, shape, F32) * s
    x = jax.random.normal(ks[0], (BATCH, SEQ, D), F32)
    offs = jax.random.randint(ks[1], (BATCH, 1), 0, 64) * CHUNK
    positions = (offs + jnp.arange(SEQ, dtype=jnp.int32)[None, :]).astype(jnp.int32)
    return {
        "x": x,
        "positions": positions,
        "w_in": nrm(ks[2], (L, D, IN_WIDTH), D ** -0.5),
        "gla_w_gate": nrm(ks[3], (L, GLA_GATE_RANK, GLA_K_WIDTH), GLA_GATE_RANK ** -0.5),
        "gla_b_gate": nrm(ks[4], (L, GLA_K_WIDTH), 0.1) + 1.0,
        "gla_norm_g": 1.0 + nrm(ks[5], (L, GLA_V_WIDTH), 0.02),
        "p_attn": nrm(ks[6], (L, ATT_WIDTH_2, D), ATT_WIDTH_2 ** -0.5),
        "p_gla": nrm(ks[7], (L, GLA_V_WIDTH, D), GLA_V_WIDTH ** -0.5),
        "w_mix_out": nrm(ks[8], (L, D, D), DN_BETA * D ** -0.5),
        "b_mix_out": nrm(ks[9], (L, D), 0.02),
        "ln1_g": 1.0 + nrm(ks[10], (L, D), 0.02),
        "ln1_b": nrm(ks[11], (L, D), 0.02),
        "w_up": nrm(ks[12], (L, D, 2 * D_FF_2), D ** -0.5),
        "conv_w": nrm(ks[13], (L, CONV_WIDTH_2, 2 * D_FF_2), CONV_WIDTH_2 ** -0.5),
        "conv_b": nrm(ks[14], (L, 2 * D_FF_2), 0.02),
        "w_down": nrm(ks[15], (L, D_FF_2, D), DN_BETA * D_FF_2 ** -0.5),
        "ln2_g": 1.0 + nrm(ks[16], (L, D), 0.02),
        "ln2_b": nrm(ks[17], (L, D), 0.02),
    }

def second_block(x, positions, w_in, gla_w_gate, gla_b_gate, gla_norm_g, p_attn, p_gla,
              w_mix_out, b_mix_out, ln1_g, ln1_b, w_up, conv_w, conv_b, w_down, ln2_g, ln2_b):
    for l in range(DEPTH):
        y = hybrid_mixer(x, positions, w_in[l], gla_w_gate[l], gla_b_gate[l], gla_norm_g[l],
                         p_attn[l], p_gla[l], w_mix_out[l], b_mix_out[l])
        x = layer_norm(DN_ALPHA * x + y, ln1_g[l], ln1_b[l])
        y = conv_ffn(x, w_up[l], conv_w[l], conv_b[l], w_down[l])
        x = layer_norm(DN_ALPHA * x + y, ln2_g[l], ln2_b[l])
    return x


def setup_inputs(seed=0):
    out = dict(first_inputs(seed))
    for name, value in second_inputs(seed + 1).items():
        if name != "x":
            out[name + "_2"] = value
    return out


def reference(
    x, c, w_ada, b_ada, norm1_w, w_in, conv_a_w, conv_a_b, ln_a_w, ln_a_b, lb_gamma, rec_norm_w,
    w_out, norm2_w, w_up, conv_f_w, w_down, final_norm_w, positions_2, w_in_2, gla_w_gate_2,
    gla_b_gate_2, gla_norm_g_2, p_attn_2, p_gla_2, w_mix_out_2, b_mix_out_2, ln1_g_2, ln1_b_2,
    w_up_2, conv_w_2, conv_b_2, w_down_2, ln2_g_2, ln2_b_2,
):
    x = first_block(
        x, c, w_ada, b_ada, norm1_w, w_in, conv_a_w, conv_a_b, ln_a_w, ln_a_b, lb_gamma,
        rec_norm_w, w_out, norm2_w, w_up, conv_f_w, w_down, final_norm_w,
    )
    return second_block(
        x, positions_2, w_in_2, gla_w_gate_2, gla_b_gate_2, gla_norm_g_2, p_attn_2, p_gla_2,
        w_mix_out_2, b_mix_out_2, ln1_g_2, ln1_b_2, w_up_2, conv_w_2, conv_b_2, w_down_2,
        ln2_g_2, ln2_b_2,
    )


_drawn_inputs = setup_inputs


def setup_inputs(seed=0):
    import zlib

    import numpy as np

    out = dict(_drawn_inputs(seed))
    spreads = {}
    factors = {'norm1_w': 3.302,
     'conv_a_b': 8.0,
     'ln_a_w': 6.109,
     'ln_a_b': 8.0,
     'lb_gamma': 4.219,
     'rec_norm_w': 5.41,
     'gla_w_gate_2': 2.768,
     'gla_b_gate_2': 6.17,
     'gla_norm_g_2': 8.0,
     'b_mix_out_2': 2.726,
     'conv_b_2': 5.939,
     'norm2_w': 2.877}
    for name, (base, spread) in spreads.items():
        noise = np.random.default_rng([zlib.crc32(name.encode()), seed]).standard_normal(out[name].shape)
        drawn = base * np.exp(spread * noise) if base else spread * noise
        out[name] = __import__('jax').numpy.asarray(drawn.astype(out[name].dtype))
    for name, factor in factors.items():
        out[name] = (out[name] * factor).astype(out[name].dtype)
    return out
```

```python
from contextlib import ExitStack

import numpy as np

import concourse.bass as bass
from concourse import mybir

F32 = mybir.dt.float32
I32 = mybir.dt.int32
U8 = mybir.dt.uint8
ALU = mybir.AluOpType
ACT = mybir.ActivationFunctionType
AX = mybir.AxisListType

P = 128
D = 1024
S = 512
DEPTH = 2
KT = D // P
TT = S // P
EPS = 1e-6
LN_EPS = 1e-5
BIG = 1e30

CONV_CH, CONV_W = 256, 31
ATT_W = REC_W = 384
HD = 64
N_HEADS_1 = ATT_W // HD
RT = REC_W // P
D_FF = 2816
FT = D_FF // P
LEVELS = [1, 2, 4, 8, 16, 32, 64]
TABLE = S + 3 * P

N_HEADS_2 = 8
ATT_W2 = 512
TOPK = 128
CHUNK = 64
NCH = S // CHUNK
GLA_H, GLA_DK, GLA_DV = 4, 128, 256
GLA_RANK = 16
GLA_TAU = 16.0
ALPHA = (2.0 * DEPTH) ** 0.25

SLOT = 3072
NSLOT = 4


def cols(w, l, c0, n, kt=KT):
    return w[bass.ds(l, 1), 0:kt * P, c0:c0 + n].rearrange("o (k p) n -> p (o k) n", p=P)


class Ring:

    def __init__(self, nc, ctx, name):
        self.buf = ctx.enter_context(nc.sbuf_tensor(f"{name}_slots", [P, NSLOT, SLOT], F32))
        self.loaded = [ctx.enter_context(nc.semaphore(f"{name}_slot{s}_loaded")) for s in range(NSLOT)]
        self.full = ctx.enter_context(nc.semaphore(f"{name}_tiles_multiplied"))
        self.units = []
        self.tiles = 0
        self.used_at = []
        self.issued = 0

    def plan(self, sources):
        first = len(self.units)
        self.units += sources
        return first

    def view(self, i):
        _, kt, n = self.units[i]
        return self.buf[:, i % NSLOT, 0:kt * n].rearrange("p (k n) -> p k n", k=kt)

    def uses(self, unit, tiles):
        assert unit == len(self.used_at)
        before, self.tiles = self.tiles, self.tiles + tiles
        self.used_at.append(self.tiles)
        return before

    def load_until(self, sp, end):
        while self.issued < min(end + NSLOT, len(self.units)):
            i = self.issued
            src, _, _ = self.units[i]
            if i >= NSLOT:
                sp.wait_ge(self.full, self.used_at[i - NSLOT])
            sp.dma_start(self.view(i), src).then_inc(self.loaded[i % NSLOT], 16)
            self.issued += 1

    def arrived(self, pe, i):
        pe.wait_ge(self.loaded[i % NSLOT], 16 * (i // NSLOT + 1))


class Chain:

    def __init__(self, eng, sem):
        self.eng, self.sem, self.n = eng, sem, 0

    def add(self, ins):
        self.n += 1
        ins.then_inc(self.sem, 1)
        return self.n

    def wait(self, n=None):
        self.eng.wait_ge(self.sem, self.n if n is None else n)

    def link(self, ins):
        self.add(ins)
        self.wait()


class Core:

    def __init__(self, nc, ctx):
        self.nc = nc
        sb = lambda name, shape, dt=F32: ctx.enter_context(nc.sbuf_tensor(name, shape, dt))
        self.ps = ctx.enter_context(nc.psum_tensor("ps", [P, 8, 512], F32))
        self.x = sb("x_res", [P, KT, S])
        self.h = sb("h_norm", [P, KT, S])
        self.ident = sb("ident", [P, P])
        self.ones = sb("ones", [P, 6, P])
        self.eps = sb("eps", [P, 8])
        self.sems = []

    def sem(self, ctx, name):
        s = ctx.enter_context(self.nc.semaphore(name))
        self.sems.append(s)
        return s

    def clear(self, sems):
        nums = sorted(s.num for s in sems)
        start = prev = nums[0]
        runs = []
        for n in nums[1:]:
            if n != prev + 1:
                runs.append((start, prev + 1))
                start = n
            prev = n
        runs.append((start, prev + 1))
        for a, b in runs:
            self.nc.gpsimd.sem_clear(range(a, b))
        self.nc.all_engine_barrier()


def stage_start(core, ctx, args):
    nc, ps = core.nc, core.ps
    const_in, x_in = args["const_f"], args["x"]
    xin = ctx.enter_context(nc.sbuf_tensor("x_tokens", [P, TT, D], F32))
    loaded = core.sem(ctx, "start_loaded")
    turned = core.sem(ctx, "start_turned")
    kept = core.sem(ctx, "start_kept")
    with nc.Block() as block:
        @block.sync
        def _(sp):
            sp.dma_start(core.ident[:, :], const_in[:, 0:P]).then_inc(loaded, 16)
            sp.dma_start(core.ones[:, :, :].rearrange("p a b -> p (a b)"), const_in[:, P:7 * P]).then_inc(loaded, 16)
            sp.dma_start(core.eps[:, :], const_in[:, 7 * P:7 * P + 8]).then_inc(loaded, 16)
            sp.dma_start(xin[:, :, :], x_in.rearrange("o (t p) d -> p (o t) d", p=P)).then_inc(loaded, 16)

        @block.tensor
        def _(pe):
            pe.wait_ge(loaded, 64)
            for k in range(KT):
                for t in range(TT):
                    ins = pe.transpose(ps[:, k, t * P:(t + 1) * P], xin[:, t, k * P:(k + 1) * P], core.ident[:, :])
                ins.then_inc(turned, 1)

        @block.scalar
        def _(act):
            for k in range(KT):
                act.wait_ge(turned, k + 1)
                act.activation(core.x[:, k, :], ps[:, k, :], ACT.Copy).then_inc(kept, 1)


def stage_columns(core, ctx, name, rows, out, out2=None):
    nc, ps = core.nc, core.ps
    groups, g, n = [], [], 0
    for src, k in rows:
        if n + k > P:
            groups.append((g, n))
            g, n = [], 0
        g.append((src, k))
        n += k
    groups.append((g, n))
    stage = ctx.enter_context(nc.sbuf_tensor(f"{name}_rows", [P, len(groups), P], F32))
    loaded = core.sem(ctx, f"{name}_rows_loaded")
    turned = core.sem(ctx, f"{name}_rows_turned")
    kept = core.sem(ctx, f"{name}_columns_kept")
    with nc.Block() as block:
        @block.sync
        def _(sp):
            for i, (g, _) in enumerate(groups):
                r = 0
                for src, k in g:
                    sp.dma_start(stage[r:r + k, i, :], src).then_inc(loaded, 16)
                    r += k

        @block.tensor
        def _(pe):
            pe.wait_ge(loaded, 16 * len(rows))
            for i, (_, n) in enumerate(groups):
                pe.transpose(ps[:, i, 0:n], stage[0:n, i, :], core.ident[0:n, 0:n]).then_inc(turned, 1)

        @block.scalar
        def _(act):
            c = 0
            for i, (_, n) in enumerate(groups):
                act.wait_ge(turned, i + 1)
                act.activation(out[:, c:c + n], ps[:, i, 0:n], ACT.Copy).then_inc(kept, 1)
                c += n


def stage_project(core, ctx, name, ring, jobs, next_units, carrier="scalar"):
    nc, ps = core.nc, core.ps
    full, base = ring.full, ring.tiles
    free = core.sem(ctx, f"{name}_bank_free")
    banks = []
    for unit, kind, put, src in jobs:
        _, kt, n = ring.units[unit]
        if kind == "T":
            tiles = [(j * P, min(P, n - j * P)) for j in range(-(-n // P))]
            for j, (c, m) in enumerate(tiles):
                banks.append((unit, j == len(tiles) - 1, kind, kt, c, m, put, j, src))
        else:
            for j in range(TT):
                banks.append((unit, j == TT - 1, kind, kt, 0, n, put, j, src))
        ring.uses(unit, len(banks) - (ring.tiles - base))
    with nc.Block() as block:
        @block.sync
        def _(sp):
            ring.load_until(sp, next_units)

        @block.tensor
        def _(pe):
            for b, (unit, last, kind, kt, c, m, put, j, src) in enumerate(banks):
                if j == 0:
                    ring.arrived(pe, unit)
                if b >= 8:
                    pe.wait_ge(free, b - 7)
                w = ring.view(unit)
                for k in range(kt):
                    if kind == "T":
                        ins = pe.matmul(ps[0:m, b % 8, :], w[:, k, c:c + m], src[:, k, :],
                                        start=(k == 0), stop=(k == kt - 1))
                    else:
                        ins = pe.matmul(ps[:, b % 8, 0:m], src[:, k, j * P:(j + 1) * P], w[:, k, :],
                                        start=(k == 0), stop=(k == kt - 1))
                ins.then_inc(full, 1)

        @(block.scalar if carrier == "scalar" else block.vector)
        def _(act):
            for b, (unit, last, kind, kt, c, m, put, j, src) in enumerate(banks):
                act.wait_ge(full, base + b + 1)
                view = ps[0:m, b % 8, :] if kind == "T" else ps[:, b % 8, 0:m]
                put(act, view, j).then_inc(free, 1)


def stage_mod(core, ctx, ring, first, next_units, silu_c, b_cols, mod):
    nc, ps = core.nc, core.ps
    kept = core.sem(ctx, "mod_kept")
    per = 3
    for u in range(6 * KT // per):
        ring.uses(first + u, 1)
    with nc.Block() as block:
        @block.sync
        def _(sp):
            ring.load_until(sp, next_units)

        @block.tensor
        def _(pe):
            for u in range(6 * KT // per):
                ring.arrived(pe, first + u)
                w = ring.view(first + u)
                for j in range(per):
                    n = u * per + j
                    for k in range(KT):
                        ins = pe.matmul(ps[:, 0, n:n + 1], w[:, k, j * P:(j + 1) * P], silu_c[:, k:k + 1],
                                        start=(k == 0), stop=(k == KT - 1))
                ins.then_inc(ring.full, 1)

        @block.vector
        def _(dve):
            dve.wait_ge(ring.full, ring.tiles)
            dve.tensor_tensor(mod[:, :], ps[:, 0, 0:6 * KT], b_cols, ALU.add).then_inc(kept, 1)


def stage_rms(core, ctx, name, scale, shift, tmp, out):
    nc, ps = core.nc, core.ps
    squared = core.sem(ctx, f"{name}_squared")
    summed = core.sem(ctx, f"{name}_summed")
    rooted = core.sem(ctx, f"{name}_rooted")
    scaled = core.sem(ctx, f"{name}_scaled")
    shifted = core.sem(ctx, f"{name}_shifted")
    with nc.Block() as block:
        @block.scalar
        def _(act):
            for k in range(KT):
                if k >= 2:
                    act.wait_ge(summed, k - 1)
                act.activation(tmp[:, k % 2, :], core.x[:, k, :], ACT.Square).then_inc(squared, 1)
            act.wait_ge(summed, KT)
            act.activation(tmp[:, 2, :], ps[:, 0, :], ACT.Sqrt, bias=core.eps[:, 0:1]).then_inc(rooted, 1)
            if shift is not None:
                for k in range(KT):
                    act.wait_ge(scaled, k + 2)
                    act.activation(out[:, k, :], tmp[:, 4 + k % 2, :], ACT.Identity,
                                   bias=shift[:, k:k + 1]).then_inc(shifted, 1)

        @block.tensor
        def _(pe):
            for k in range(KT):
                pe.wait_ge(squared, k + 1)
                pe.matmul(ps[:, 0, :], core.ones[:, 0, :], tmp[:, k % 2, :],
                          start=(k == 0), stop=(k == KT - 1)).then_inc(summed, 1)

        @block.vector
        def _(dve):
            dve.wait_ge(rooted, 1)
            dve.reciprocal(tmp[:, 3, :], tmp[:, 2, :]).then_inc(scaled, 1)
            dve.wait_ge(scaled, 1)
            for k in range(KT):
                dst = out[:, k, :]
                if shift is not None:
                    dst = tmp[:, 4 + k % 2, :]
                    if k >= 2:
                        dve.wait_ge(shifted, k - 1)
                dve.scalar_tensor_tensor(dst, core.x[:, k, :], scale[:, k:k + 1], tmp[:, 3, :],
                                         ALU.mult, ALU.mult).then_inc(scaled, 1)


def stage_ffn(core, ctx, name, l, w_up, w_down, taps, bias, lead, gelu, put, bufs, src):
    nc, ps = core.nc, core.ps
    g, u, c, wup = bufs["g"], bufs["u"], bufs["c"], bufs["w"]
    nup, ndn = 2, 2
    PAD = S + 2
    up_loaded = [core.sem(ctx, f"{name}_up_slot{s}_loaded") for s in range(nup)]
    up_full = core.sem(ctx, f"{name}_up_full")
    edge = core.sem(ctx, f"{name}_edges_zero")
    u_kept = core.sem(ctx, f"{name}_u_kept")
    tap0 = core.sem(ctx, f"{name}_tap0")
    conv = core.sem(ctx, f"{name}_conv")
    act_g = core.sem(ctx, f"{name}_gelu")
    prod = core.sem(ctx, f"{name}_hidden")
    dn_loaded = [core.sem(ctx, f"{name}_down_slot{s}_loaded") for s in range(ndn)]
    dn_full = core.sem(ctx, f"{name}_down_full")
    dn_kept = core.sem(ctx, f"{name}_down_kept")
    HK = FT // 2

    def up_view(s):
        return wup[:, s, 0:KT * 2 * P].rearrange("p (k h c) -> p k h c", k=KT, h=2)

    def dn_view(s):
        return wup[:, nup + s, 0:HK * 2 * P].rearrange("p (k c) -> p k c", k=HK)

    up_src = w_up.rearrange("d (k p) (h n) -> d p k h n", p=P, h=2)
    dn_src = w_down.rearrange("d (k p) n -> d p k n", p=P)

    with nc.Block() as block:
        @block.sync
        def _(sp):
            for s in range(nup):
                for h in range(2):
                    sp.dma_start(up_view(s)[:, :, h, :], up_src[bass.ds(l, 1), :, :, h, s * P:(s + 1) * P]
                                 .rearrange("o p k n -> p (o k) n")).then_inc(up_loaded[s], 16)
            for s in range(ndn):
                sp.dma_start(dn_view(s), dn_src[bass.ds(l, 1), :, s * HK:(s + 1) * HK, 0:2 * P]
                             .rearrange("o p k n -> p (o k) n")).then_inc(dn_loaded[s], 16)
            with sp.Fori(1, FT // nup) as i:
                for s in range(nup):
                    sp.wait_ge(up_full, 4 * i + 2 * s - 2)
                    for h in range(2):
                        sp.dma_start(up_view(s)[:, :, h, :],
                                     up_src[bass.ds(l, 1), :, :, h, bass.ds(2 * P * i + s * P, P)]
                                     .rearrange("o p k n -> p (o k) n")).then_inc(up_loaded[s], 16)
            with sp.Fori(1, KT // 2) as i:
                for s in range(ndn):
                    sp.wait_ge(dn_full, 3 * i - (0 if s else 2))
                    sp.dma_start(dn_view(s), dn_src[bass.ds(l, 1), :, s * HK:(s + 1) * HK, bass.ds(2 * P * i, 2 * P)]
                                 .rearrange("o p k n -> p (o k) n")).then_inc(dn_loaded[s], 16)

        @block.tensor
        def _(pe):
            def pair(s, i, peeled=False):
                pe.wait_ge(up_loaded[s], 32 * i + 32)
                for h in range(2):
                    if not peeled:
                        pe.wait_ge(u_kept, 4 * i + 2 * s + h - 3)
                    for k in range(KT):
                        ins = pe.matmul(ps[:, 2 * s + h, :], up_view(s)[:, k, h, :], src[:, k, :],
                                        start=(k == 0), stop=(k == KT - 1))
                    ins.then_inc(up_full, 1)
            for s in range(nup):
                pair(s, 0, peeled=True)
            with pe.Fori(1, FT // nup) as i:
                for s in range(nup):
                    pair(s, i)
            def down(i, peeled=False):
                for s in range(ndn):
                    pe.wait_ge(dn_loaded[s], 16 * i + 16)
                    if s == 0 and not peeled:
                        pe.wait_ge(dn_kept, 2 * i)
                    for n in range(2):
                        for k in range(HK):
                            ins = pe.matmul(ps[:, 4 + n, :], dn_view(s)[:, k, n * P:(n + 1) * P],
                                            g[:, s * HK + k, :], start=(s == 0 and k == 0),
                                            stop=(s == 1 and k == HK - 1))
                        if n == 1 or s == 1:
                            ins.then_inc(dn_full, 1)
            pe.wait_ge(prod, FT)
            down(0, peeled=True)
            with pe.Fori(1, KT // 2) as i:
                down(i)

        @block.scalar
        def _(act):
            act.wait_ge(edge, 4)
            def pair(s, i, peeled=False):
                for h in range(2):
                    act.wait_ge(up_full, 4 * i + 2 * s + h + 1)
                    if not peeled:
                        act.wait_ge(conv, 4 * i + 2 * s + h - 3)
                    act.activation(u[:, 2 * s + h, lead:lead + S], ps[:, 2 * s + h, :], ACT.Copy)\
                        .then_inc(u_kept, 1)
                for h in range(2):
                    act.wait_ge(u_kept, 4 * i + 2 * s + h + 1)
                    if not peeled:
                        act.wait_ge(prod, 2 * i + s - 1)
                    j = nup * i + s + h * FT
                    act.activation(c[:, 2 * s + h, :], u[:, 2 * s + h, 0:S], ACT.Identity,
                                   bias=(bias[:, bass.ds(j, 1)] if bias is not None else core.eps[:, 3:4]),
                                   scale=taps[:, bass.ds(j, 1)]).then_inc(tap0, 1)
                act.wait_ge(conv, 4 * i + 2 * s + 1)
                act.activation(c[:, 2 * s, :], c[:, 2 * s, :], gelu).then_inc(act_g, 1)
            for s in range(nup):
                pair(s, 0, peeled=True)
            with act.Fori(1, FT // nup) as i:
                for s in range(nup):
                    pair(s, i)

        @block.vector
        def _(dve):
            for q in range(4):
                dve.memset(u[:, q, 0:PAD], 0.0).then_inc(edge, 1)
            step = Chain(dve, core.sem(ctx, f"{name}_taps_chain"))
            def pair(s, i, peeled=False):
                j = nup * i + s
                for h in range(2):
                    dve.wait_ge(tap0, 4 * i + 2 * s + h + 1)
                    cc = c[:, 2 * s + h, :]
                    uu = u[:, 2 * s + h, :]
                    t = [taps[:, bass.ds(j + h * FT + w * 2 * FT, 1)] for w in range(3)]
                    dve.scalar_tensor_tensor(cc, uu[:, 1:1 + S], t[1], cc, ALU.mult, ALU.add)\
                        .then_inc(step.sem, 1)
                    dve.wait_ge(step.sem, 4 * i + 2 * s + h + 1)
                    dve.scalar_tensor_tensor(cc, uu[:, 2:2 + S], t[2], cc, ALU.mult, ALU.add)\
                        .then_inc(conv, 1)
                dve.wait_ge(conv, 4 * i + 2 * s + 2)
                dve.wait_ge(act_g, 2 * i + s + 1)
                dve.tensor_tensor(g[:, bass.ds(j, 1), :], c[:, 2 * s:2 * s + 1, :], c[:, 2 * s + 1:2 * s + 2, :],
                                  ALU.mult).then_inc(prod, 1)
            for s in range(nup):
                pair(s, 0, peeled=True)
            with dve.Fori(1, FT // nup) as i:
                for s in range(nup):
                    pair(s, i)
            def out(i):
                for n in range(2):
                    dve.wait_ge(dn_full, 3 * i + 2 + n)
                    put(dve, 2 * i + n, ps[:, 4 + n:5 + n, :]).then_inc(dn_kept, 1)
            out(0)
            with dve.Fori(1, KT // 2) as i:
                out(i)


def stage_conv(core, ctx, a, gate, taps, cbias, ln_w, ln_b, out, tmp):
    nc, ps = core.nc, core.ps
    C2, half = CONV_CH // P, CONV_W // 2
    pad = ctx.enter_context(nc.sbuf_tensor("conv_pad", [P, C2, S + CONV_W - 1], F32))
    gated = core.sem(ctx, "conv_gated")
    tapped = core.sem(ctx, "conv_tapped")
    meaned = core.sem(ctx, "conv_mean")
    centred = core.sem(ctx, "conv_centred")
    squared = core.sem(ctx, "conv_squared")
    varied = core.sem(ctx, "conv_variance")
    rooted = core.sem(ctx, "conv_rooted")
    normed = core.sem(ctx, "conv_normed")
    acc = lambda k: tmp[:, k, :]
    with nc.Block() as block:
        @block.vector
        def _(dve):
            ch = Chain(dve, core.sem(ctx, "conv_chain"))
            ch.add(dve.memset(pad[:, :, :], 0.0))
            ch.wait()
            for k in range(C2):
                ch.add(dve.tensor_tensor(pad[:, k, half:half + S], a[:, k, :], gate[:, k, :], ALU.mult))
            ch.wait()
            for k in range(C2):
                ch.add(dve.tensor_scalar(acc(k), pad[:, k, 0:S], taps[:, k:k + 1], cbias[:, k:k + 1],
                                         ALU.mult, ALU.add))
            for w in range(1, CONV_W):
                for k in range(C2):
                    ch.wait(ch.n - C2 + 1)
                    ins = dve.scalar_tensor_tensor(acc(k), pad[:, k, w:w + S],
                                                   taps[:, C2 * w + k:C2 * w + k + 1], acc(k), ALU.mult, ALU.add)
                    if w == CONV_W - 1:
                        ins.then_inc(tapped, 1)
                    else:
                        ch.add(ins)
                        continue
                    if k == 0:
                        ch.wait()
            dve.wait_ge(meaned, C2)
            for k in range(C2):
                dve.tensor_tensor(tmp[:, 2 + k, :], acc(k), ps[:, 0, :], ALU.subtract).then_inc(centred, 1)
            dve.wait_ge(rooted, 1)
            ch.link(dve.reciprocal(tmp[:, 7, :], tmp[:, 6, :]))
            dve.wait_ge(centred, C2)
            for k in range(C2):
                dve.scalar_tensor_tensor(acc(k), tmp[:, 2 + k, :], ln_w[:, k:k + 1], tmp[:, 7, :],
                                         ALU.mult, ALU.mult).then_inc(normed, 1)

        @block.tensor
        def _(pe):
            pe.wait_ge(tapped, C2)
            for k in range(C2):
                pe.matmul(ps[:, 0, :], core.ones[:, 1, :], acc(k), start=(k == 0), stop=(k == C2 - 1))\
                    .then_inc(meaned, 1)
            for k in range(C2):
                pe.wait_ge(squared, k + 1)
                pe.matmul(ps[:, 1, :], core.ones[:, 1, :], tmp[:, 4 + k, :], start=(k == 0), stop=(k == C2 - 1))\
                    .then_inc(varied, 1)

        @block.scalar
        def _(act):
            for k in range(C2):
                act.wait_ge(centred, k + 1)
                act.activation(tmp[:, 4 + k, :], tmp[:, 2 + k, :], ACT.Square).then_inc(squared, 1)
            act.wait_ge(varied, C2)
            act.activation(tmp[:, 6, :], ps[:, 1, :], ACT.Sqrt, bias=core.eps[:, 0:1]).then_inc(rooted, 1)
            for k in range(C2):
                act.wait_ge(normed, k + 1)
                act.activation(out[:, k, :], acc(k), ACT.Silu, bias=ln_b[:, k:k + 1]).then_inc(squared, 1)


def stage_attention(core, ctx, name, heads, q, k, v, out, width, bias, prepare=None):
    nc, ps = core.nc, core.ps
    sp_ = ctx.enter_context(nc.sbuf_tensor(f"{name}_scores", [P, 3, S], F32))
    pt = ctx.enter_context(nc.sbuf_tensor(f"{name}_probs_turned", [P, 2, S], F32))
    st = ctx.enter_context(nc.sbuf_tensor(f"{name}_stats", [P, 3, 4], F32))
    scored = core.sem(ctx, f"{name}_scored")
    biased = core.sem(ctx, f"{name}_biased")
    maxed = core.sem(ctx, f"{name}_maxed")
    probbed = core.sem(ctx, f"{name}_exponentials")
    inverted = core.sem(ctx, f"{name}_inverted")
    normed = core.sem(ctx, f"{name}_normed")
    turned = core.sem(ctx, f"{name}_turned")
    turned_kept = core.sem(ctx, f"{name}_turned_kept")
    mixed = core.sem(ctx, f"{name}_mixed")
    kept = core.sem(ctx, f"{name}_kept")
    steps = [(h, t) for h in range(heads) for t in range(TT)]
    LAG = 1
    with nc.Block() as block:
        @block.tensor
        def _(pe):
            def scores(i):
                h, t = steps[i]
                w, r = width(t), HD * (h % 2)
                if i >= 2:
                    pe.wait_ge(biased, i - 1)
                pe.matmul(ps[:, i % 2, 0:w], q[r:r + HD, h // 2, t * P:(t + 1) * P], k[r:r + HD, h // 2, 0:w],
                          start=True, stop=True).then_inc(scored, 1)

            def values(i):
                h, t = steps[i]
                n, r = width(t) // P, HD * (h % 2)
                pe.wait_ge(normed, i + 1)
                if i >= 2:
                    pe.wait_ge(turned_kept, i - 1)
                for c in range(n):
                    ins = pe.transpose(ps[:, 2 + i % 2, c * P:(c + 1) * P], sp_[:, i % 3, c * P:(c + 1) * P],
                                       core.ident[:, :])
                ins.then_inc(turned, 1)

            def mix(i):
                h, t = steps[i]
                n, r = width(t) // P, HD * (h % 2)
                pe.wait_ge(turned_kept, i + 1)
                if i >= 2:
                    pe.wait_ge(kept, i - 1)
                for c in range(n):
                    ins = pe.matmul(ps[r:r + HD, 4 + i % 2, 0:P], v[:, c, h * HD:(h + 1) * HD],
                                    pt[:, i % 2, c * P:(c + 1) * P], start=(c == 0), stop=(c == n - 1))
                ins.then_inc(mixed, 1)
            for i in range(len(steps) + 2):
                if i < len(steps):
                    scores(i)
                if 1 <= i <= len(steps):
                    values(i - 1)
                if i >= 2:
                    mix(i - 2)

        @block.vector
        def _(dve):
            ch = Chain(dve, core.sem(ctx, f"{name}_chain"))

            def soft(i):
                h, t = steps[i]
                w = width(t)
                if t == 0 and prepare is not None:
                    prepare(dve, ch, h)
                dve.wait_ge(scored, i + 1)
                if i >= 3:
                    dve.wait_ge(turned, i - 2)
                dve.scalar_tensor_tensor(sp_[:, i % 3, 0:w], ps[:, i % 2, 0:w], HD ** -0.5, bias(h, t),
                                         ALU.mult, ALU.add).then_inc(biased, 1)
                dve.wait_ge(biased, i + 1)
                dve.tensor_reduce(st[:, i % 3, 0:1], sp_[:, i % 3, 0:w], AX.X, ALU.max, negate=True)\
                    .then_inc(maxed, 1)

            def norm(i):
                h, t = steps[i]
                w = width(t)
                dve.wait_ge(probbed, i + 1)
                dve.reciprocal(st[:, i % 3, 2:3], st[:, i % 3, 1:2]).then_inc(inverted, 1)
                dve.wait_ge(inverted, i + 1)
                dve.tensor_scalar(sp_[:, i % 3, 0:w], sp_[:, i % 3, 0:w], st[:, i % 3, 2:3], None, ALU.mult)\
                    .then_inc(normed, 1)
            for i in range(len(steps) + 1):
                if i < len(steps):
                    soft(i)
                if i >= 1:
                    norm(i - 1)

        @block.scalar
        def _(act):
            def exps(i):
                h, t = steps[i]
                w = width(t)
                act.wait_ge(maxed, i + 1)
                if i >= 3:
                    act.wait_ge(normed, i - 2)
                act.activation(sp_[:, i % 3, 0:w], sp_[:, i % 3, 0:w], ACT.Exp, bias=st[:, i % 3, 0:1],
                               accum_out=st[:, i % 3, 1:2]).then_inc(probbed, 1)

            def turn(i):
                h, t = steps[i]
                w = width(t)
                act.wait_ge(turned, i + 1)
                if i >= 2:
                    act.wait_ge(mixed, i - 1)
                act.activation(pt[:, i % 2, 0:w], ps[:, 2 + i % 2, 0:w], ACT.Copy).then_inc(turned_kept, 1)

            def keep(i):
                h, t = steps[i]
                r = HD * (h % 2)
                act.wait_ge(mixed, i + 1)
                act.activation(out[r:r + HD, h // 2, t * P:(t + 1) * P], ps[r:r + HD, 4 + i % 2, 0:P], ACT.Copy)\
                    .then_inc(kept, 1)
            for i in range(len(steps) + 2):
                if i < len(steps):
                    exps(i)
                if 1 <= i <= len(steps):
                    turn(i - 1)
                if i >= 2:
                    keep(i - 2)


def stage_recurrence(core, ctx, qr, kf, kb, ff, fb, v, masks, orec):
    nc, ps = core.nc, core.ps
    qf = ctx.enter_context(nc.sbuf_tensor("rec_q_fwd", [P, 2, S], F32))
    qb = ctx.enter_context(nc.sbuf_tensor("rec_q_bwd", [P, 2, S], F32))
    ks = ctx.enter_context(nc.sbuf_tensor("rec_k_sum", [P, 2, S], F32))
    tot = ctx.enter_context(nc.sbuf_tensor("rec_totals", [P, 2, S], F32))
    sc = ctx.enter_context(nc.sbuf_tensor("rec_scores", [P, 2, 5 * S], F32))
    started = core.sem(ctx, "rec_started")
    multiplied = core.sem(ctx, "rec_multiplied")
    copied = core.sem(ctx, "rec_copied")
    decayed = core.sem(ctx, "rec_decayed")
    across = core.sem(ctx, "rec_across")
    across_kept = core.sem(ctx, "rec_across_kept")
    mixed = core.sem(ctx, "rec_mixed")
    kept = core.sem(ctx, "rec_kept")
    NL = len(LEVELS)
    diag = lambda h: sc[:, h, :].rearrange("p (i c) -> p i c", c=S + P)[:, :, 0:P]
    full = lambda h: sc[:, h, 0:TT * S].rearrange("p (i t) -> p i t", i=TT)

    with nc.Block() as block:
        @block.tensor
        def _(pe):
            nb = 0
            for p in range(RT):
                pe.wait_ge(started, p + 1)
                for lv in range(NL + 1):
                    if lv >= 1:
                        if lv >= 2:
                            pe.wait_ge(decayed, p * (NL + 1) + lv - 1)
                    for h in range(2):
                        r = h * HD
                        if nb >= 4:
                            pe.wait_ge(copied, nb - 3)
                        bank = ps[:, nb % 4, :]
                        for i in range(TT):
                            if lv == 0:
                                ins = pe.matmul(bank[:, i * P:(i + 1) * P], ks[r:r + HD, p % 2, i * P:(i + 1) * P],
                                                qr[r:r + HD, p, i * P:(i + 1) * P], start=True, stop=True)
                                continue
                            m = LEVELS[lv - 1]
                            tile_q = lambda a: a[r:r + HD, p % 2, i * P:(i + 1) * P]\
                                .rearrange("k (n two m) -> k n two m", two=2, m=m)
                            pe.matmul(bank[:, i * P:i * P + P // 2], kf[r:r + HD, p, i * P:(i + 1) * P],
                                      tile_q(qf)[:, :, 1, :], start=True, stop=True)
                            ins = pe.matmul(bank[:, i * P + P // 2:(i + 1) * P], kb[r:r + HD, p, i * P:(i + 1) * P],
                                            tile_q(qb)[:, :, 0, :], start=True, stop=True)
                        ins.then_inc(multiplied, 1)
                        nb += 1
                for part in range(2):
                    pe.wait_ge(decayed, p * (NL + 1) + NL + part)
                    for h in range(2):
                        r = h * HD
                        if part == 0:
                            if p >= 1:
                                pe.wait_ge(kept, 2 * (p - 1) + h + 1)
                            for i in range(TT):
                                kk, qq = (kf, qf) if i % 2 == 0 else (kb, qb)
                                j = i ^ 1
                                ins = pe.matmul(ps[:, 4 + h, i * P:(i + 1) * P], kk[r:r + HD, p, i * P:(i + 1) * P],
                                                qq[r:r + HD, p % 2, j * P:(j + 1) * P], start=True, stop=True)
                            ins.then_inc(across, 1)
                        else:
                            for half in range(2):
                                kk, qq = (kf, qf) if half == 0 else (kb, qb)
                                q0 = S // 2 * (1 - half)
                                bank = 6 + half
                                if h == 1:
                                    pe.wait_ge(across_kept, 8 * p + 5 + half)
                                elif p >= 1:
                                    pe.wait_ge(across_kept, 8 * p)
                                for i in range(2):
                                    s0 = (2 * half + i) * P
                                    ins = pe.matmul(ps[:, bank, i * 256:(i + 1) * 256], kk[r:r + HD, p, s0:s0 + P],
                                                    qq[r:r + HD, p % 2, q0:q0 + S // 2], start=True, stop=True)
                                ins.then_inc(across, 1)
                pe.wait_ge(copied, nb)
                for h in range(2):
                    r = h * HD
                    pe.wait_ge(across_kept, 8 * p + 8)
                    for i in range(TT):
                        ins = pe.matmul(ps[r:r + HD, 4 + h, :], v[:, i, (2 * p + h) * HD:(2 * p + h + 1) * HD],
                                        full(h)[:, i, :], start=(i == 0), stop=(i == TT - 1))
                    ins.then_inc(mixed, 1)

        @block.vector
        def _(dve):
            ch = Chain(dve, core.sem(ctx, "rec_chain"))
            nb = 0
            for p in range(RT):
                w = p % 2
                if p >= 2:
                    dve.wait_ge(mixed, 2 * (p - 1))
                ch.add(dve.tensor_tensor(qf[:, w, :], qr[:, p, :], ff[:, p, :], ALU.mult))
                ch.add(dve.tensor_tensor(qb[:, w, :], qr[:, p, :], fb[:, p, :], ALU.mult))
                ch.add(dve.tensor_tensor(ks[:, w, :], kf[:, p, :], kb[:, p, :], ALU.add))
                ch.wait()
                dve.sem_inc(started, 1)
                prev_f, prev_b = ff[:, p, :], fb[:, p, :]
                at = 0
                for lv in range(NL + 1):
                    if lv >= 1:
                        m = LEVELS[lv - 1]
                        dve.wait_ge(multiplied, nb + 2)
                        n = S // (2 * m)
                        blk = lambda a: a.rearrange("p (n two m) -> p n two m", two=2, m=m)
                        tf = prev_f.rearrange("p (n two) -> p n two", two=2)
                        tb = prev_b.rearrange("p (n two) -> p n two", two=2)
                        last_f = tf[:, :, 0].unsqueeze(2).to_broadcast([P, n, m])
                        next_f = tf[:, :, 1].unsqueeze(2).to_broadcast([P, n, m])
                        last_b = tb[:, :, 0].unsqueeze(2).to_broadcast([P, n, m])
                        next_b = tb[:, :, 1].unsqueeze(2).to_broadcast([P, n, m])
                        for a, half, f in ((qf[:, w, :], 1, last_f), (qb[:, w, :], 0, next_b),
                                           (kf[:, p, :], 0, next_f), (kb[:, p, :], 1, last_b)):
                            ap = blk(a)[:, :, half, :]
                            ch.add(dve.tensor_tensor(ap, ap, f, ALU.mult))
                        if at + n <= S:
                            nf, nbk = tot[:, 0, at:at + n], tot[:, 1, at:at + n]
                            ch.add(dve.tensor_tensor(nf, tf[:, :, 0], tf[:, :, 1], ALU.mult))
                            ch.add(dve.tensor_tensor(nbk, tb[:, :, 0], tb[:, :, 1], ALU.mult))
                            prev_f, prev_b = nf, nbk
                            at += n
                        ch.wait()
                        dve.sem_inc(decayed, 1)
                    for h in range(2):
                        dve.wait_ge(multiplied, nb + 1)
                        if p >= 1 and lv == 0:
                            dve.wait_ge(mixed, 2 * (p - 1) + h + 1)
                        bank = ps[:, nb % 4, :]
                        if lv == 0:
                            dve.tensor_copy(diag(h), bank.rearrange("p (i c) -> p i c", i=TT)).then_inc(copied, 1)
                        else:
                            m = LEVELS[lv - 1]
                            dve.wait_ge(copied, nb)
                            for part, two in ((0, 1), (1, 0)):
                                for i in range(1):
                                    dst = diag(h).rearrange("p i (n two m) -> p i n two m", two=2, m=m)[:, :, :, two, :]
                                    src = bank.rearrange("p (i two n m) -> p i two n m", i=TT, two=2, m=m)[:, :, part]
                                    msk = masks[:, lv - 1, :].rearrange("p (i n two m) -> p i n two m", i=TT, two=2, m=m)[:, :, :, two, :]
                                    ins = dve.copy_predicated(dst, msk, src)
                                if part == 0:
                                    ch.add(ins)
                                    ch.wait()
                                else:
                                    ins.then_inc(copied, 1)
                        nb += 1
                dve.wait_ge(across, 6 * p + 2)
                m = P
                tf = prev_f
                tb = prev_b
                n = S // (2 * m)
                blk = lambda a: a.rearrange("p (n two m) -> p n two m", two=2, m=m)
                tf = prev_f.rearrange("p (n two) -> p n two", two=2)
                tb = prev_b.rearrange("p (n two) -> p n two", two=2)
                for a, half, f in ((qf[:, w, :], 1, tf[:, :, 0]), (qb[:, w, :], 0, tb[:, :, 1]),
                                   (kf[:, p, :], 0, tf[:, :, 1]), (kb[:, p, :], 1, tb[:, :, 0])):
                    ap = blk(a)[:, :, half, :]
                    ch.add(dve.tensor_tensor(ap, ap, f.unsqueeze(2).to_broadcast([P, n, m]), ALU.mult))
                ch.wait()
                dve.sem_inc(decayed, 1)

        @block.scalar
        def _(act):
            for p in range(RT):
                for h in range(2):
                    act.wait_ge(across, 6 * p + h + 1)
                    if p >= 1:
                        act.wait_ge(mixed, 2 * (p - 1) + h + 1)
                    bank = ps[:, 4 + h, :].rearrange("p (n two c) -> p n two c", two=2, c=P)
                    flat = sc[:, h, :].rearrange("p (n c) -> p n c", c=S * 5 // 2)
                    act.activation(flat[:, :, P:2 * P], bank[:, :, 0, :], ACT.Copy).then_inc(across_kept, 1)
                    act.activation(flat[:, :, S:S + P], bank[:, :, 1, :], ACT.Copy).then_inc(across_kept, 1)
                for h in range(2):
                    for half in range(2):
                        act.wait_ge(across, 6 * p + 3 + 2 * h + half)
                        q0 = S // 2 * (1 - half)
                        ins = act.activation(full(h)[:, 2 * half:2 * half + 2, q0:q0 + S // 2],
                                             ps[:, 6 + half, :].rearrange("p (i c) -> p i c", i=2), ACT.Copy)
                        ins.then_inc(across_kept, 1)
                for h in range(2):
                    r = h * HD
                    act.wait_ge(mixed, 2 * p + h + 1)
                    act.activation(orec[r:r + HD, p, :], ps[r:r + HD, 4 + h, :], ACT.Copy).then_inc(kept, 1)


def stage_rec_norm(core, ctx, o, w, gate, out, tmp):
    nc, ps = core.nc, core.ps
    squared = core.sem(ctx, "recn_squared")
    summed = core.sem(ctx, "recn_summed")
    rooted = core.sem(ctx, "recn_rooted")
    with nc.Block() as block:
        @block.scalar
        def _(act):
            for k in range(RT):
                act.activation(tmp[:, k, :], o[:, k, :], ACT.Square).then_inc(squared, 1)
            for k in range(RT):
                act.wait_ge(summed, k + 1)
                act.activation(tmp[:, 3 + k, :], ps[:, k, :], ACT.Sqrt, bias=core.eps[:, 0:1]).then_inc(rooted, 1)

        @block.tensor
        def _(pe):
            for k in range(RT):
                pe.wait_ge(squared, k + 1)
                pe.matmul(ps[:, k, :], core.ones[:, 2, :], tmp[:, k, :], start=True, stop=True).then_inc(summed, 1)

        @block.vector
        def _(dve):
            ch = Chain(dve, core.sem(ctx, "recn_chain"))
            for k in range(RT):
                dve.wait_ge(rooted, k + 1)
                ch.link(dve.reciprocal(tmp[:, 3 + k, :], tmp[:, 3 + k, :]))
                ch.link(dve.scalar_tensor_tensor(o[:, k, :], o[:, k, :], w[:, k:k + 1], tmp[:, 3 + k, :],
                                                 ALU.mult, ALU.mult))
                ch.add(dve.tensor_tensor(out[:, k, :], o[:, k, :], gate[:, k, :], ALU.mult))


def stage_gates(core, ctx, z_pos, z_neg, lb, one_minus):
    nc = core.nc
    with nc.Block() as block:
        @block.vector
        def _(dve):
            ch = Chain(dve, core.sem(ctx, "gates_chain"))
            for d in range(2):
                for k in range(RT):
                    j = d * RT + k
                    f, kk = z_pos[d][:, k, :], z_neg[d][:, k, :]
                    ch.add(dve.tensor_scalar(f, f, one_minus[:, j:j + 1], lb[:, j:j + 1], ALU.mult, ALU.add))
                    ch.add(dve.tensor_scalar(kk, kk, one_minus[:, j:j + 1], None, ALU.mult))
            ch.wait()
            for d in range(2):
                ch.add(dve.tensor_scalar(z_pos[d][:, :, :], z_pos[d][:, :, :], 1e-30, None, ALU.max))


def stage_small_1(core, ctx, l_is_one, vec, mod, s1, s2, lb, one_minus):
    nc = core.nc
    diff = core.sem(ctx, "bounds_difference")
    sig = core.sem(ctx, "bounds_sigmoid")
    with nc.Block() as block:
        @block.vector
        def _(dve):
            ch = Chain(dve, core.sem(ctx, "small1_chain"))
            dve.tensor_tensor(lb[:, :], vec[:, 28:34], vec[:, 22:28], ALU.subtract).then_inc(diff, 1)
            for s, m, n in ((s1, 8, 0), (s2, 32, 8)):
                ch.add(dve.scalar_tensor_tensor(s[:, :], mod[:, m:m + 8], 1.0, vec[:, n:n + 8], ALU.add, ALU.mult))
            dve.wait_ge(sig, 1)
            ch.link(dve.tensor_scalar(lb[:, :], lb[:, :], l_is_one, None, ALU.mult))
            ch.add(dve.tensor_scalar(one_minus[:, :], lb[:, :], -1.0, 1.0, ALU.mult, ALU.add))

        @block.scalar
        def _(act):
            act.wait_ge(diff, 1)
            act.activation(lb[:, :], lb[:, :], ACT.Sigmoid).then_inc(sig, 1)


def stack_one(core, nc, args):
    with ExitStack() as ctx:
        sb = lambda name, shape, dt=F32: ctx.enter_context(nc.sbuf_tensor(name, shape, dt))
        outer = len(core.sems)
        silu_c = sb("silu_c", [P, KT])
        layer_no = sb("layer_no", [P, 1])
        n_vec = 37
        vec = sb("vec1", [P, n_vec])
        b_ada = sb("b_ada_cols", [P, 6 * KT])
        mod = sb("mod", [P, 6 * KT])
        ctaps = sb("conv_a_taps", [P, 2 * CONV_W])
        ftaps = sb("conv_f_taps", [P, 3 * 2 * FT])
        s1, s2 = sb("scale1", [P, KT]), sb("scale2", [P, KT])
        lb, om = sb("lower_bound", [P, 2 * RT]), sb("one_minus_lb", [P, 2 * RT])
        dist_ln = sb("attn_tables", [P, 2, TABLE])
        masks = sb("rec_masks", [P, len(LEVELS), S], U8)

        with ExitStack() as c2:
            cols_c = c2.enter_context(nc.sbuf_tensor("c_cols", [P, KT], F32))
            sems0 = len(core.sems)
            stage_columns(core, c2, "c", [(args["c"].rearrange("o (n p) -> (o n) p", p=P), KT)], cols_c)
            wide = c2.enter_context(nc.sbuf_tensor("rec_masks_wide", [P, len(LEVELS), P], I32))
            tabs = core.sem(c2, "tables_loaded")
            got = core.sem(c2, "silu_c_ready")
            with nc.Block() as block:
                @block.sync
                def _(sp):
                    sp.dma_start(dist_ln[:, :, :].rearrange("p a b -> p (a b)"), args["const_attn"]).then_inc(tabs, 16)
                    sp.dma_start(wide[:, :, :].rearrange("p a b -> p (a b)"), args["const_mask"]).then_inc(tabs, 16)
                    sp.wait_ge(tabs, 32)

                @block.scalar
                def _(act):
                    act.activation(silu_c[:, :], cols_c[:, :], ACT.Silu).then_inc(got, 1)

                @block.vector
                def _(dve):
                    dve.memset(layer_no[:, :], 0.0).then_inc(got, 1)
                    dve.wait_ge(tabs, 32)
                    for i in range(TT):
                        dve.tensor_copy(masks[:, :, i * P:(i + 1) * P], wide[:, :, :]).then_inc(got, 1)
            core.clear(core.sems[sems0:])
            del core.sems[sems0:]

        with nc.Fori(0, DEPTH) as l:
          with ExitStack() as lc:
            first_sem = len(core.sems)
            lsb = lambda name, shape, dt=F32: lc.enter_context(nc.sbuf_tensor(name, shape, dt))
            ring_ctx = ExitStack()
            ring = Ring(nc, ring_ctx, "ring1")
            core.sems += ring.loaded + [ring.full]
            mod0 = ring.plan([(cols(args["w_ada"], l, 3 * P * u, 3 * P), KT, 3 * P) for u in range(16)])
            w_in, w_out = args["w_in"], args["w_out"]
            widths = [(0, 256), (256, 256)] + [(512 + 384 * i, 384) for i in range(8)]
            in0 = ring.plan([(cols(w_in, l, c, n), KT, n) for c, n in widths])
            out0 = ring.plan([(cols(w_out, l, 256 * i, 256), KT, 256) for i in range(4)])

            rows = lambda a, n: (a[bass.ds(l, 1), :].rearrange("o (n p) -> (o n) p", p=P), n)
            with ExitStack() as c2:
                stage_columns(core, c2, "vec1", [
                    rows(args["norm1_w"], 8), rows(args["norm2_w"], 8), rows(args["conv_a_b"], 2),
                    rows(args["ln_a_w"], 2), rows(args["ln_a_b"], 2),
                    (args["lb_gamma"].rearrange("d e (n p) -> (d e n) p", p=P), 12), rows(args["rec_norm_w"], 3)], vec)
                stage_columns(core, c2, "ada1", [rows(args["b_ada"], 48)], b_ada)
                stage_columns(core, c2, "ctap1", [(args["conv_a_w"][bass.ds(l, 1), :, :]
                              .rearrange("o w (n p) -> (o w n) p", p=P), 2 * CONV_W)], ctaps)
                stage_columns(core, c2, "ftap1", [(args["conv_f_w"][bass.ds(l, 1), w:w + 1, :]
                              .rearrange("o w (n p) -> (o w n) p", p=P), 2 * FT) for w in range(3)], ftaps)
            stage_mod(core, lc, ring, mod0, in0, silu_c, b_ada[:, :], mod)
            stage_small_1(core, lc, layer_no[:, 0:1], vec, mod, s1, s2, lb, om)
            with ExitStack() as c2:
                tmp = c2.enter_context(nc.sbuf_tensor("rms1_tmp", [P, 6, S], F32))
                stage_rms(core, lc, "rms1", s1, mod[:, 0:8], tmp, core.h)

            with ExitStack() as mx:
                msb = lambda name, shape, dt=F32: mx.enter_context(nc.sbuf_tensor(name, shape, dt))
                orec = msb("rec_out", [P, RT, S])
                g_rec = msb("g_rec", [P, RT, S])
                mixed = msb("mixed", [P, KT, S])
                rx = ExitStack()
                rsb = lambda name, shape, dt=F32: rx.enter_context(nc.sbuf_tensor(name, shape, dt))
                qr, i_rec = rsb("q_rec", [P, RT, S]), rsb("i_rec", [P, TT, REC_W])
                ff, fb = rsb("f_fwd", [P, RT, S]), rsb("f_bwd", [P, RT, S])
                kf, kb = rsb("k_fwd", [P, RT, S]), rsb("k_bwd", [P, RT, S])
                with ExitStack() as ax:
                    asb = lambda name, shape, dt=F32: ax.enter_context(nc.sbuf_tensor(name, shape, dt))
                    q, k = asb("q_att", [P, 3, S]), asb("k_att", [P, 3, S])
                    v = asb("v_att", [P, TT, ATT_W])
                    a, gate = asb("a_val", [P, 2, S]), asb("a_gate", [P, 2, S])
                    keep = lambda dst, f=ACT.Copy: (lambda act, view, j: act.activation(dst[:, j, :], view, f))

                    def keep_z(act, view, j, pos, neg):
                        act.activation(pos[:, j, :], view, ACT.Sigmoid).then_inc(z_kept, 1)
                        return act.activation(neg[:, j, :], view, ACT.Sigmoid, scale=-1.0)
                    z_kept = core.sem(lc, "z_gates_kept")
                    jobs = [(in0, "T", keep(a), core.h), (in0 + 1, "T", keep(gate, ACT.Sigmoid), core.h),
                            (in0 + 2, "T", keep(q), core.h), (in0 + 3, "T", keep(k), core.h),
                            (in0 + 4, "tok", keep(v), core.h), (in0 + 5, "T", keep(qr, ACT.Silu), core.h),
                            (in0 + 6, "T", lambda act, view, j: keep_z(act, view, j, ff, kf), core.h),
                            (in0 + 7, "T", lambda act, view, j: keep_z(act, view, j, fb, kb), core.h),
                            (in0 + 8, "tok", keep(i_rec), core.h), (in0 + 9, "T", keep(g_rec, ACT.Silu), core.h)]
                    stage_project(core, lc, "in1", ring, jobs, out0)
                    stage_gates(core, lc, (ff, fb), (kf, kb), lb, om)
                    with ExitStack() as c2:
                        stage_conv_tmp = core.h
                        stage_conv(core, c2, a, gate, ctaps, vec[:, 16:18], vec[:, 18:20], vec[:, 20:22],
                                   mixed[:, 0:2, :], stage_conv_tmp)
                    slopes = [2.0 ** (-8.0 * (h + 1) / N_HEADS_1) for h in range(N_HEADS_1)]
                    tab = core.h[:, 0:4, :].rearrange("p a b -> p (a b)")

                    def prepare(dve, ch, h):
                        if h >= 2:
                            ch.wait()
                        ch.link(dve.scalar_tensor_tensor(tab[:, (h % 2) * 1024:(h % 2) * 1024 + TABLE],
                                                         dist_ln[:, 0, :], -slopes[h], dist_ln[:, 1, :],
                                                         ALU.mult, ALU.add))
                    with ExitStack() as c2:
                        stage_attention(core, c2, "att1", N_HEADS_1, q, k, v, mixed[:, 2:5, :], lambda t: S,
                                        lambda h, t: tab[:, (h % 2) * 1024 + 3 * P - t * P:
                                                         (h % 2) * 1024 + 3 * P - t * P + S], prepare)
                with rx, ExitStack() as c2:
                    stage_recurrence(core, c2, qr, kf, kb, ff, fb, i_rec, masks, orec)
                stage_rec_norm(core, lc, orec, vec[:, 34:37], g_rec, mixed[:, 5:8, :], core.h)

                def add_out(g):
                    def put(dve, view, j, t0):
                        n = t0 + j
                        return dve.scalar_tensor_tensor(core.x[:, n, :], view, g[:, n:n + 1], core.x[:, n, :],
                                                        ALU.mult, ALU.add)
                    return put
                put1 = add_out(mod[:, 16:24])
                stage_project(core, lc, "out1", ring,
                              [(out0 + i, "T", (lambda dve, view, j, i=i: put1(dve, view, j, 2 * i)), mixed)
                               for i in range(4)], out0 + 4, carrier="vector")
            ring_ctx.close()
            with ExitStack() as c2:
                bufs = {"g": c2.enter_context(nc.sbuf_tensor("hidden1", [P, FT, S], F32)),
                        "u": c2.enter_context(nc.sbuf_tensor("u_pad1", [P, 4, S + 2], F32)),
                        "c": c2.enter_context(nc.sbuf_tensor("u_conv1", [P, 4, S], F32)),
                        "w": c2.enter_context(nc.sbuf_tensor("ffn_w1", [P, 4, FT // 2 * 2 * P], F32))}
                stage_rms(core, lc, "rms2", s2, mod[:, 24:32], bufs["g"][:, 0:6, :], core.h)

                def put(dve, n, view):
                    xn = core.x[:, bass.ds(n, 1), :]
                    return dve.scalar_tensor_tensor(xn, view, mod[:, bass.ds(n + 40, 1)], xn, ALU.mult, ALU.add)
                stage_ffn(core, lc, "ffn1", l, args["w_up"], args["w_down"], ftaps, None, 1, ACT.Gelu, put, bufs,
                          core.h)
            with nc.Block() as block:
                one = core.sem(lc, "layer_counted")

                @block.vector
                def _(dve):
                    dve.tensor_scalar(layer_no[:, :], layer_no[:, :], 1.0, None, ALU.add).then_inc(one, 1)
            core.clear(core.sems[first_sem:])
            del core.sems[first_sem:]

        with ExitStack() as c2:
            first_sem = len(core.sems)
            fin = c2.enter_context(nc.sbuf_tensor("final_norm_cols", [P, KT], F32))
            stage_columns(core, c2, "fin", [(args["final_norm_w"].rearrange("(n p) -> n p", p=P), KT)], fin)
            tmp = c2.enter_context(nc.sbuf_tensor("rms3_tmp", [P, 6, S], F32))
            stage_rms(core, c2, "rms3", fin, None, tmp, core.x)
            core.clear(core.sems[first_sem:])
            del core.sems[first_sem:]


def stage_layernorm(core, ctx, name, src, out, groups, avg, w, b, tmp):
    nc, ps = core.nc, core.ps
    meaned = core.sem(ctx, f"{name}_mean")
    centred = core.sem(ctx, f"{name}_centred")
    squared = core.sem(ctx, f"{name}_squared")
    varied = core.sem(ctx, f"{name}_variance")
    rooted = core.sem(ctx, f"{name}_rooted")
    inverted = core.sem(ctx, f"{name}_inverted")
    normed = core.sem(ctx, f"{name}_normed")
    shifted = core.sem(ctx, f"{name}_shifted")
    flat = [(g, k, k == tiles[0], k == tiles[-1]) for g, tiles in enumerate(groups) for k in tiles]
    with nc.Block() as block:
        @block.tensor
        def _(pe):
            for g, k, first, last in flat:
                pe.matmul(ps[:, g, :], core.ones[:, avg, :], src[:, k, :], start=first, stop=last)\
                    .then_inc(meaned, 1)
            for i, (g, k, first, last) in enumerate(flat):
                pe.wait_ge(squared, i + 1)
                pe.matmul(ps[:, 4 + g, :], core.ones[:, avg, :], tmp[:, i % 2, :], start=first, stop=last)\
                    .then_inc(varied, 1)

        @block.vector
        def _(dve):
            for i, (g, k, first, last) in enumerate(flat):
                dve.wait_ge(meaned, (g + 1) * len(groups[0]))
                dve.tensor_tensor(src[:, k, :], src[:, k, :], ps[:, g, :], ALU.subtract).then_inc(centred, 1)
            for g in range(len(groups)):
                dve.wait_ge(rooted, g + 1)
                dve.reciprocal(tmp[:, 2 + g, :], tmp[:, 2 + g, :]).then_inc(inverted, 1)
            for i, (g, k, first, last) in enumerate(flat):
                dve.wait_ge(inverted, g + 1)
                dve.wait_ge(squared, i + 1)
                dve.scalar_tensor_tensor(out[:, k, :], src[:, k, :], w[:, k:k + 1], tmp[:, 2 + g, :],
                                         ALU.mult, ALU.mult).then_inc(normed, 1)

        @block.scalar
        def _(act):
            for i, (g, k, first, last) in enumerate(flat):
                act.wait_ge(centred, i + 1)
                if i >= 2:
                    act.wait_ge(varied, i - 1)
                act.activation(tmp[:, i % 2, :], src[:, k, :], ACT.Square).then_inc(squared, 1)
            for g in range(len(groups)):
                act.wait_ge(varied, (g + 1) * len(groups[0]))
                act.activation(tmp[:, 2 + g, :], ps[:, 4 + g, :], ACT.Sqrt, bias=core.eps[:, 1:2])\
                    .then_inc(rooted, 1)
            if b is not None:
                for i, (g, k, first, last) in enumerate(flat):
                    act.wait_ge(normed, i + 1)
                    act.activation(out[:, k, :], out[:, k, :], ACT.Identity, bias=b[:, k:k + 1])\
                        .then_inc(shifted, 1)


def stage_angles(core, ctx, positions, cos, sin):
    nc = core.nc
    pos_i = ctx.enter_context(nc.sbuf_tensor("pos_int", [P, S], I32))
    w = ctx.enter_context(nc.sbuf_tensor("angle_work", [P, 4, S], F32))
    loaded = core.sem(ctx, "positions_loaded")
    reduced = core.sem(ctx, "angle_reduced")
    absed = core.sem(ctx, "angle_abs")
    done = core.sem(ctx, "angle_done")
    C1 = 6.28125
    C2 = float(np.float32(np.floor((2 * np.pi - C1) * 2.0 ** 21) / 2.0 ** 21))
    C3 = float(2 * np.pi - C1 - C2)
    ROUND = 12582912.0
    with nc.Block() as block:
        @block.sync
        def _(sp):
            sp.dma_start(pos_i[:, :], positions.partition_broadcast(P)).then_inc(loaded, 16)

        @block.vector
        def _(dve):
            ch = Chain(dve, core.sem(ctx, "angle_chain"))
            dve.wait_ge(loaded, 16)
            ch.link(dve.tensor_copy(w[:, 0, :], pos_i[:, :]))
            ch.link(dve.tensor_scalar(w[:, 1, :], w[:, 0, :], core.eps[:, 4:5], None, ALU.mult))
            ch.link(dve.tensor_scalar(w[:, 2, :], w[:, 1, :], 1.0 / (2 * np.pi), None, ALU.mult))
            ch.link(dve.tensor_scalar(w[:, 2, :], w[:, 2, :], ROUND, None, ALU.add))
            ch.link(dve.tensor_scalar(w[:, 2, :], w[:, 2, :], ROUND, None, ALU.subtract))
            for c in (C1, C2, C3):
                ch.link(dve.scalar_tensor_tensor(w[:, 1, :], w[:, 2, :], -c, w[:, 1, :], ALU.mult, ALU.add))
            dve.tensor_scalar(w[:, 1, :], w[:, 1, :], 3.1415925, -3.1415925, ALU.min, ALU.max).then_inc(reduced, 1)

        @block.scalar
        def _(act):
            act.wait_ge(reduced, 1)
            act.activation(w[:, 3, :], w[:, 1, :], ACT.Abs).then_inc(absed, 1)
            act.activation(sin[:, :], w[:, 1, :], ACT.Sin).then_inc(done, 1)
            act.wait_ge(absed, 1)
            act.activation(cos[:, :], w[:, 3, :], ACT.Sin, bias=core.eps[:, 5:6], scale=-1.0).then_inc(done, 1)


def stage_rope(core, ctx, tiles, ik_raw, ik, cos, sin, tmp):
    nc, ps = core.nc, core.ps
    rotated = core.sem(ctx, "rope_rotated")
    turned = core.sem(ctx, "rope_turned")
    n = len(tiles)
    with nc.Block() as block:
        @block.tensor
        def _(pe):
            for i, x in enumerate(tiles):
                if i >= 4:
                    pe.wait_ge(turned, i - 3)
                pe.matmul(ps[:, i % 4, :], core.ones[:, 3, :], x, start=True, stop=True).then_inc(rotated, 1)
            pe.matmul(ps[:, 4, :], core.ones[0:HD, 4, :], ik_raw, start=True, stop=True)
            pe.matmul(ps[:, 5, :], core.ones[0:HD, 5, :], ik_raw, start=True, stop=True).then_inc(rotated, 1)

        @block.vector
        def _(dve):
            ch = Chain(dve, core.sem(ctx, "rope_chain"))
            for i in range(n + 1):
                dve.wait_ge(rotated, i + 1)
                raw, rot, out = (tiles[i], ps[:, i % 4, :], tiles[i]) if i < n else (ps[:, 4, :], ps[:, 5, :], ik)
                t1, t2 = tmp[:, 2 * (i % 2), :], tmp[:, 2 * (i % 2) + 1, :]
                if i >= 2:
                    dve.wait_ge(turned, i - 1)
                ch.add(dve.tensor_tensor(t1, raw, cos[:, :], ALU.mult))
                ch.add(dve.tensor_tensor(t2, rot, sin[:, :], ALU.mult))
                ch.wait()
                dve.tensor_tensor(out, t1, t2, ALU.add).then_inc(turned, 1)


NEG = -3.0e38


def stage_select(core, ctx, iq, ik, iw, bias):
    nc, ps = core.nc, core.ps
    rl = ctx.enter_context(nc.sbuf_tensor("sel_relu", [P, 4, S], F32))
    sc = ctx.enter_context(nc.sbuf_tensor("sel_scores", [P, 2, S], F32))
    wk = ctx.enter_context(nc.sbuf_tensor("sel_work", [P, 3, S], F32))
    m8 = ctx.enter_context(nc.sbuf_tensor("sel_max8", [P, 8], F32))
    cn = ctx.enter_context(nc.sbuf_tensor("sel_counts", [P, 2], F32))
    dotted = core.sem(ctx, "sel_dotted")
    relued = core.sem(ctx, "sel_relued")
    summed = core.sem(ctx, "sel_summed")
    steps = [(t, h) for t in range(1, TT) for h in range(N_HEADS_2)]
    with nc.Block() as block:
        @block.tensor
        def _(pe):
            for i, (t, h) in enumerate(steps):
                w, r = P * (t + 1), HD * (h % 2)
                if i >= 4:
                    pe.wait_ge(relued, i - 3)
                pe.matmul(ps[:, i % 4, 0:w], iq[r:r + HD, h // 2, t * P:(t + 1) * P], ik[r:r + HD, 0:w],
                          start=True, stop=True).then_inc(dotted, 1)

        @block.scalar
        def _(act):
            for i, (t, h) in enumerate(steps):
                w = P * (t + 1)
                act.wait_ge(dotted, i + 1)
                if i >= 4:
                    act.wait_ge(summed, i - 3)
                act.activation(rl[:, i % 4, 0:w], ps[:, i % 4, 0:w], ACT.Relu, scale=HD ** -0.5).then_inc(relued, 1)

        @block.vector
        def _(dve):
            ch = Chain(dve, core.sem(ctx, "sel_chain"))
            ch.link(dve.memset(bias[:, 0, 0:P], 0.0))
            ch.add(dve.memset(bias[0:HD, 0, HD:P], -BIG))
            for i, (t, h) in enumerate(steps):
                w = P * (t + 1)
                acc = sc[:, t % 2, 0:w]
                dve.wait_ge(relued, i + 1)
                if h == 0:
                    dve.tensor_scalar(acc, rl[:, i % 4, 0:w], iw[:, t, h:h + 1], None, ALU.mult).then_inc(summed, 1)
                else:
                    dve.wait_ge(summed, i)
                    dve.scalar_tensor_tensor(acc, rl[:, i % 4, 0:w], iw[:, t, h:h + 1], acc, ALU.mult, ALU.add)\
                        .then_inc(summed, 1)
                if h < N_HEADS_2 - 1:
                    continue
                dve.wait_ge(summed, i + 1)
                ch.link(dve.memset(sc[0:HD, t % 2, w - CHUNK:w], NEG))
                work = wk[:, 0, 0:w]
                for r in range(TOPK // 8):
                    src = acc if r == 0 else work
                    ch.link(dve.max(m8[:, :], src))
                    if r < TOPK // 8 - 1:
                        ch.link(dve.match_replace(work, m8[:, :], src, NEG))
                least = m8[:, 7:8]
                above, equal = wk[:, 0, 0:w], wk[:, 1, 0:w]
                ch.add(dve.tensor_scalar(equal, acc, least, None, ALU.is_equal))
                ch.link(dve.tensor_scalar(above, acc, least, 0.0, ALU.is_gt, ALU.add, accum_out=cn[:, 0:1]))
                ch.link(dve.tensor_scalar(cn[:, 1:2], cn[:, 0:1], -1.0, float(TOPK), ALU.mult, ALU.add))
                ch.link(dve.tensor_tensor_scan(wk[:, 2, 0:w], equal, equal, 0.0, ALU.add, ALU.max))
                ch.link(dve.scalar_tensor_tensor(equal, wk[:, 2, 0:w], cn[:, 1:2], equal, ALU.is_le, ALU.mult))
                ch.link(dve.tensor_tensor(above, above, equal, ALU.add))
                ch.link(dve.tensor_scalar(bias[:, t, 0:w], above, BIG, -BIG, ALU.mult, ALU.add))


def stage_gla_gates(core, ctx, glr, wg, wg_src, b, gk, la, etot, tmp):
    nc, ps = core.nc, core.ps
    loaded = core.sem(ctx, "gla_w_loaded")
    full = core.sem(ctx, "gla_logits")
    logs = core.sem(ctx, "gla_log")
    steps = core.sem(ctx, "gla_act_chain")
    summed = core.sem(ctx, "gla_centred")
    decay = core.sem(ctx, "gla_decay")
    mask = tmp[:, 7, :]
    with nc.Block() as block:
        @block.sync
        def _(sp):
            sp.dma_start(wg[:, :], wg_src).then_inc(loaded, 16)

        @block.tensor
        def _(pe):
            pe.wait_ge(loaded, 16)
            for h in range(GLA_H):
                pe.matmul(ps[:, h, :], wg[:, h * P:(h + 1) * P], glr[0:GLA_RANK, 0, :], start=True, stop=True)\
                    .then_inc(full, 1)

        @block.scalar
        def _(act):
            ch = Chain(act, steps)
            for h in range(GLA_H):
                act.wait_ge(full, h + 1)
                ch.link(act.activation(tmp[:, 2 + h, :], ps[:, h, :], ACT.Identity, bias=b[:, h:h + 1]))
                ch.link(act.activation(tmp[:, h % 2, :], tmp[:, 2 + h, :], ACT.Abs))
                ch.link(act.activation(tmp[:, h % 2, :], tmp[:, h % 2, :], ACT.Exp, scale=-1.0))
                act.activation(la[:, h, :], tmp[:, h % 2, :], ACT.Ln, bias=core.eps[:, 2:3]).then_inc(logs, 1)
            for h in range(GLA_H):
                act.wait_ge(summed, h + 1)
                act.activation(tmp[:, 2 + h, :], tmp[:, 2 + h, :], ACT.Exp, scale=-1.0 / GLA_TAU).then_inc(decay, 1)
                act.activation(etot[:, h, :], la[:, h, CHUNK - 1:S:CHUNK], ACT.Exp, scale=1.0 / GLA_TAU)\
                    .then_inc(decay, 1)

        @block.vector
        def _(dve):
            ch = Chain(dve, core.sem(ctx, "gla_dve_chain"))
            ch.link(dve.memset(mask, 1.0))
            ch.add(dve.memset(mask.rearrange("p (n c) -> p n c", c=CHUNK)[:, :, 0:1], 0.0))
            for h in range(GLA_H):
                dve.wait_ge(logs, h + 1)
                ch.link(dve.tensor_scalar(tmp[:, 2 + h, :], tmp[:, 2 + h, :], 0.0, None, ALU.min))
                ch.link(dve.tensor_tensor(tmp[:, 6, :], tmp[:, 2 + h, :], la[:, h, :], ALU.subtract))
                ch.link(dve.tensor_tensor_scan(la[:, h, :], mask, tmp[:, 6, :], 0.0, ALU.mult, ALU.add))
                blk = lambda a: a.rearrange("p (n c) -> p n c", c=CHUNK)
                dve.tensor_tensor(blk(tmp[:, 2 + h, :]), blk(la[:, h, :]),
                                  blk(la[:, h, :])[:, :, CHUNK - 1:CHUNK].to_broadcast([P, NCH, CHUNK]),
                                  ALU.subtract).then_inc(summed, 1)
            for h in range(GLA_H):
                dve.wait_ge(decay, 2 * h + 2)
                ch.add(dve.tensor_tensor(gk[:, h, :], gk[:, h, :], tmp[:, 2 + h, :], ALU.mult))


def stage_gla(core, ctx, gq, gk, gv, etot, out):
    nc, ps = core.nc, core.ps
    kt = ctx.enter_context(nc.sbuf_tensor("gla_k_tokens", [P, 2, S], F32))
    st = ctx.enter_context(nc.sbuf_tensor("gla_states", [P, 2, NCH, GLA_DV], F32))
    turned = core.sem(ctx, "gla_turned")
    turned_kept = core.sem(ctx, "gla_turned_kept")
    outer = core.sem(ctx, "gla_outer_products")
    stated = core.sem(ctx, "gla_stated")
    read = core.sem(ctx, "gla_read")
    kept = core.sem(ctx, "gla_kept")
    with nc.Block() as block:
        @block.tensor
        def _(pe):
            def turn(h):
                if h >= 2:
                    pe.wait_ge(turned_kept, h - 1)
                for t in range(TT):
                    ins = pe.transpose(ps[:, h % 2, t * P:(t + 1) * P], gk[:, h, t * P:(t + 1) * P], core.ident[:, :])
                ins.then_inc(turned, 1)

            def product(n):
                h, c = divmod(n, NCH)
                if c == 0:
                    pe.wait_ge(turned_kept, h + 1)
                if n >= 2:
                    pe.wait_ge(stated, n - 1)
                r, t = CHUNK * (c % 2), c // 2
                pe.matmul(ps[:, 2 + n % 2, 0:GLA_DV], kt[r:r + CHUNK, h % 2, t * P:(t + 1) * P],
                          gv[r:r + CHUNK, t, h * GLA_DV:(h + 1) * GLA_DV], start=True, stop=True).then_inc(outer, 1)

            def query(n):
                h, c = divmod(n, NCH)
                if c == 0 and h >= 2:
                    pe.wait_ge(kept, 2 * (h - 1))
                pe.wait_ge(stated, n + 1)
                for half in range(2):
                    ins = pe.matmul(ps[:, 4 + 2 * (h % 2) + half, c * CHUNK:(c + 1) * CHUNK],
                                    st[:, h % 2, c, half * P:(half + 1) * P], gq[:, h, c * CHUNK:(c + 1) * CHUNK],
                                    start=True, stop=True)
                ins.then_inc(read, 1)
            turn(0)
            for n in range(GLA_H * NCH + 1):
                if n < GLA_H * NCH:
                    if n % NCH == 4 and n // NCH + 1 < GLA_H:
                        turn(n // NCH + 1)
                    product(n)
                if n >= 1:
                    query(n - 1)

        @block.vector
        def _(dve):
            for n in range(GLA_H * NCH):
                h, c = divmod(n, NCH)
                dve.wait_ge(outer, n + 1)
                if h >= 2 and c == 0:
                    dve.wait_ge(read, NCH * (h - 1))
                if c == 0:
                    dve.tensor_copy(st[:, h % 2, c, :], ps[:, 2 + n % 2, 0:GLA_DV]).then_inc(stated, 1)
                else:
                    dve.wait_ge(stated, n)
                    dve.scalar_tensor_tensor(st[:, h % 2, c, :], st[:, h % 2, c - 1, :], etot[:, h, c:c + 1],
                                             ps[:, 2 + n % 2, 0:GLA_DV], ALU.mult, ALU.add).then_inc(stated, 1)

        @block.scalar
        def _(act):
            def keep_turned(h):
                act.wait_ge(turned, h + 1)
                if h >= 2:
                    act.wait_ge(outer, NCH * (h - 1))
                act.activation(kt[:, h % 2, :], ps[:, h % 2, :], ACT.Copy).then_inc(turned_kept, 1)
            keep_turned(0)
            for h in range(GLA_H):
                if h + 1 < GLA_H:
                    keep_turned(h + 1)
                act.wait_ge(read, NCH * (h + 1))
                for half in range(2):
                    act.activation(out[:, 2 * h + half, :], ps[:, 4 + 2 * (h % 2) + half, :], ACT.Copy,
                                   scale=GLA_DK ** -0.5).then_inc(kept, 1)


def stage_merge(core, ctx, ring, first, next_units, x, att, gla, out):
    nc, ps = core.nc, core.ps
    sg = ctx.enter_context(nc.sbuf_tensor("merge_gates", [P, 4, S], F32))
    tm = ctx.enter_context(nc.sbuf_tensor("merge_part", [P, 2, S], F32))
    base = ring.tiles
    for u in range(16):
        ring.uses(first + u, 2)
    gated = core.sem(ctx, "merge_gated")
    half1 = core.sem(ctx, "merge_products")
    merged = core.sem(ctx, "merge_merged")
    srcs = [(x, KT), (att, ATT_W2 // P), (x, KT), (gla, KT)]
    with nc.Block() as block:
        @block.sync
        def _(sp):
            ring.load_until(sp, next_units)

        @block.tensor
        def _(pe):
            for n in range(4):
                for part, (src, kt) in enumerate(srcs):
                    u = first + 4 * n + part
                    ring.arrived(pe, u)
                    if n >= 1:
                        pe.wait_ge(half1 if part % 2 else gated, 4 * (n - 1) + part // 2 * 2 + 2)
                    for j in range(2):
                        for k in range(kt):
                            ins = pe.matmul(ps[:, 2 * part + j, :], ring.view(u)[:, k, j * P:(j + 1) * P], src[:, k, :],
                                            start=(k == 0), stop=(k == kt - 1))
                        ins.then_inc(ring.full, 1)

        @block.scalar
        def _(act):
            for n in range(4):
                for g in range(2):
                    for j in range(2):
                        act.wait_ge(ring.full, base + 8 * n + 4 * g + j + 1)
                        if n >= 1:
                            act.wait_ge(half1, 4 * (n - 1) + 2 * g + j + 1)
                        act.activation(sg[:, 2 * g + j, :], ps[:, 4 * g + j, :], ACT.Sigmoid).then_inc(gated, 1)

        @block.vector
        def _(dve):
            for n in range(4):
                for g in range(2):
                    for j in range(2):
                        dve.wait_ge(ring.full, base + 8 * n + 4 * g + 2 + j + 1)
                        dve.wait_ge(gated, 4 * n + 2 * g + j + 1)
                        if g == 1 and n >= 1:
                            dve.wait_ge(merged, 2 * (n - 1) + j + 1)
                        dst = out[:, 2 * n + j, :] if g == 0 else tm[:, j, :]
                        dve.tensor_tensor(dst, ps[:, 4 * g + 2 + j, :], sg[:, 2 * g + j, :], ALU.mult)\
                            .then_inc(half1, 1)
                for j in range(2):
                    dve.wait_ge(half1, 4 * n + 2 + j + 1)
                    dve.tensor_tensor(out[:, 2 * n + j, :], out[:, 2 * n + j, :], tm[:, j, :], ALU.add)\
                        .then_inc(merged, 1)


def stack_two(core, nc, args):
    with ExitStack() as ctx:
        sb = lambda name, shape, dt=F32: ctx.enter_context(nc.sbuf_tensor(name, shape, dt))
        cos, sin = sb("rope_cos", [P, S]), sb("rope_sin", [P, S])
        vec = sb("vec2", [P, 52])
        fbias = sb("conv_2_bias", [P, 2 * FT])
        ftaps = sb("conv_2_taps", [P, 3 * 2 * FT])
        with ExitStack() as c2:
            first_sem = len(core.sems)
            stage_angles(core, c2, args["positions_2"], cos, sin)
            core.clear(core.sems[first_sem:])
            del core.sems[first_sem:]

        with nc.Fori(0, DEPTH) as l:
          with ExitStack() as lc:
            first_sem = len(core.sems)
            ring_ctx = ExitStack()
            ring = Ring(nc, ring_ctx, "ring2")
            core.sems += ring.loaded + [ring.full]
            w_in = args["w_in_2"]
            at = dict(zip(("aq", "ak", "av", "iq", "ik", "iw", "gq", "gk", "gv", "glr", "g_r", "ga", "gb", "end"),
                          np.cumsum([0, 512, 512, 512, 512, 64, 8, 512, 512, 1024, 16, 1024, 1024, 1024]).tolist()))
            two = lambda name, n: [(cols(w_in, l, at[name] + 256 * i, 256), KT, 256) for i in range(n)]
            one = lambda name, n: [(cols(w_in, l, at[name], n), KT, n)]
            in0 = ring.plan(two("aq", 2) + two("ak", 2) + two("av", 2) + two("iq", 2) + one("ik", 64) + one("iw", 8))
            gla0 = ring.plan(two("gq", 2) + two("gk", 2) + two("gv", 4) + one("glr", GLA_RANK))
            gr0 = ring.plan(two("g_r", 4))
            mg0 = ring.plan([u for n in range(4) for u in (
                (cols(w_in, l, at["ga"] + 256 * n, 256), KT, 256),
                (cols(args["p_attn_2"], l, 256 * n, 256, kt=4), 4, 256),
                (cols(w_in, l, at["gb"] + 256 * n, 256), KT, 256),
                (cols(args["p_gla_2"], l, 256 * n, 256), KT, 256))])
            out0 = ring.plan([(cols(args["w_mix_out_2"], l, 256 * i, 256), KT, 256) for i in range(4)])

            rows = lambda a, n: (a[bass.ds(l, 1), :].rearrange("o (n p) -> (o n) p", p=P), n)
            with ExitStack() as c2:
                stage_columns(core, c2, "vec2", [rows(args[k + "_2"], n) for k, n in (
                    ("b_mix_out", 8), ("ln1_g", 8), ("ln1_b", 8), ("ln2_g", 8), ("ln2_b", 8),
                    ("gla_b_gate", 4), ("gla_norm_g", 8))], vec)
                stage_columns(core, c2, "fbias2", [rows(args["conv_b_2"], 2 * FT)], fbias)
                stage_columns(core, c2, "ftap2", [(args["conv_w_2"][bass.ds(l, 1), w:w + 1, :]
                              .rearrange("o w (n p) -> (o w n) p", p=P), 2 * FT) for w in range(3)], ftaps)

            x = core.x
            keep = lambda dst, f=ACT.Copy, t0=0, **kw: (
                lambda act, view, j: act.activation(dst[:, t0 + j, :], view, f, **kw))
            tok = lambda dst, c0: (lambda act, view, j: act.activation(dst[:, j, c0:c0 + 256], view, ACT.Copy))
            with ExitStack() as mx:
                att = mx.enter_context(nc.sbuf_tensor("att_out2", [P, 4, S], F32))
                with ExitStack() as ax:
                    asb = lambda name, shape, dt=F32: ax.enter_context(nc.sbuf_tensor(name, shape, dt))
                    aq, ak, iq = asb("aq", [P, 4, S]), asb("ak", [P, 4, S]), asb("iq", [P, 4, S])
                    av = asb("av", [P, TT, ATT_W2])
                    ikr, ik, iw = asb("ik_raw", [HD, S]), asb("ik", [P, S]), asb("iw", [P, TT, N_HEADS_2])
                    bias = asb("sel_bias", [P, TT, S])
                    jobs = []
                    for i, dst in enumerate((aq, ak)):
                        jobs += [(in0 + 2 * i + u, "T", keep(dst, t0=2 * u), x) for u in range(2)]
                    jobs += [(in0 + 4 + u, "tok", tok(av, 256 * u), x) for u in range(2)]
                    jobs += [(in0 + 6 + u, "T", keep(iq, t0=2 * u), x) for u in range(2)]
                    jobs += [(in0 + 8, "T", lambda act, view, j: act.activation(ikr[:, :], view, ACT.Copy), x),
                             (in0 + 9, "tok", keep(iw, scale=N_HEADS_2 ** -0.5), x)]
                    stage_project(core, lc, "in2", ring, jobs, gla0)
                    with ExitStack() as c2:
                        tiles = [a[:, k, :] for a in (iq, aq, ak) for k in range(4)]
                        stage_rope(core, c2, tiles, ikr[:, :], ik[:, :], cos, sin, core.h)
                    with ExitStack() as c2:
                        stage_select(core, c2, iq, ik, iw, bias)
                    with ExitStack() as c2:
                        stage_attention(core, c2, "att2", N_HEADS_2, aq, ak, av, att, lambda t: P * (t + 1),
                                        lambda h, t: bias[:, t, 0:P * (t + 1)])
                gla = mx.enter_context(nc.sbuf_tensor("gla_out", [P, KT, S], F32))
                with ExitStack() as gx:
                    gsb = lambda name, shape, dt=F32: gx.enter_context(nc.sbuf_tensor(name, shape, dt))
                    gq, gk, la = gsb("gq", [P, 4, S]), gsb("gk", [P, 4, S]), gsb("gla_log_sums", [P, 4, S])
                    gv = gsb("gv", [P, TT, GLA_H * GLA_DV])
                    glr, wg = gsb("glr", [GLA_RANK, 1, S]), gsb("gla_gate_w", [GLA_RANK, GLA_H * GLA_DK])
                    etot = gsb("gla_chunk_decay", [P, GLA_H, NCH])
                    jobs = []
                    for i, dst in enumerate((gq, gk)):
                        jobs += [(gla0 + 2 * i + u, "T", keep(dst, t0=2 * u), x) for u in range(2)]
                    jobs += [(gla0 + 4 + u, "tok", tok(gv, 256 * u), x) for u in range(4)]
                    jobs += [(gla0 + 8, "T", keep(glr), x)]
                    stage_project(core, lc, "gla_in", ring, jobs, gr0)
                    with ExitStack() as c2:
                        stage_gla_gates(core, c2, glr, wg,
                                        args["gla_w_gate_2"][bass.ds(l, 1), :, :].rearrange("o r n -> (o r) n"),
                                        vec[:, 40:44], gk, la, etot, core.h)
                    with ExitStack() as c2:
                        stage_gla(core, c2, gq, gk, gv, etot, gla)
                with ExitStack() as c2:
                    stage_layernorm(core, c2, "gla_ln", gla, gla, [[2 * h, 2 * h + 1] for h in range(GLA_H)], 1,
                                    vec[:, 44:52], None, core.h)
                stage_project(core, lc, "g_r", ring,
                              [(gr0 + i, "T", keep(core.h, ACT.Silu, t0=2 * i), x) for i in range(4)], mg0)
                with nc.Block() as block:
                    gsem = core.sem(lc, "gla_gated")

                    @block.vector
                    def _(dve):
                        for k in range(KT):
                            dve.tensor_tensor(gla[:, k, :], gla[:, k, :], core.h[:, k, :], ALU.mult).then_inc(gsem, 1)
                with ExitStack() as c2:
                    stage_merge(core, c2, ring, mg0, out0, x, att, gla, core.h)
                pre = core.sem(lc, "residual_scaled")

                def put1(dve, view, j, t0):
                    n = t0 + j
                    dve.tensor_scalar(x[:, n, :], x[:, n, :], ALPHA, vec[:, n:n + 1], ALU.mult, ALU.add)\
                        .then_inc(pre, 1)
                    dve.wait_ge(pre, n + 1)
                    return dve.tensor_tensor(x[:, n, :], view, x[:, n, :], ALU.add)
                stage_project(core, lc, "out2", ring,
                              [(out0 + i, "T", (lambda dve, view, j, i=i: put1(dve, view, j, 2 * i)), core.h)
                               for i in range(4)], out0 + 4, carrier="vector")
            ring_ctx.close()
            with ExitStack() as c2:
                bufs = {"g": c2.enter_context(nc.sbuf_tensor("hidden2", [P, FT, S], F32)),
                        "u": c2.enter_context(nc.sbuf_tensor("u_pad2", [P, 4, S + 2], F32)),
                        "c": c2.enter_context(nc.sbuf_tensor("u_conv2", [P, 4, S], F32)),
                        "w": c2.enter_context(nc.sbuf_tensor("ffn_w2", [P, 4, FT // 2 * 2 * P], F32))}
                stage_layernorm(core, lc, "ln1", x, x, [list(range(KT))], 0, vec[:, 8:16], vec[:, 16:24], bufs["g"])

                def put(dve, n, view):
                    xn = x[:, bass.ds(n, 1), :]
                    return dve.scalar_tensor_tensor(xn, xn, ALPHA, view, ALU.mult, ALU.add)
                stage_ffn(core, lc, "ffn2", l, args["w_up_2"], args["w_down_2"], ftaps, fbias, 2,
                          ACT.Gelu_apprx_tanh, put, bufs, x)
                stage_layernorm(core, lc, "ln2", x, x, [list(range(KT))], 0, vec[:, 24:32], vec[:, 32:40], bufs["g"])
            core.clear(core.sems[first_sem:])
            del core.sems[first_sem:]


def stage_finish(core, ctx, out):
    nc, ps = core.nc, core.ps
    xo = ctx.enter_context(nc.sbuf_tensor("x_out", [P, TT, D], F32))
    turned = core.sem(ctx, "finish_turned")
    kept = core.sem(ctx, "finish_kept")
    stored = core.sem(ctx, "finish_stored")
    with nc.Block() as block:
        @block.tensor
        def _(pe):
            for t in range(TT):
                for g in range(2):
                    for k in range(4):
                        ins = pe.transpose(ps[:, 2 * t + g, k * P:(k + 1) * P],
                                           core.x[:, 4 * g + k, t * P:(t + 1) * P], core.ident[:, :])
                    ins.then_inc(turned, 1)

        @block.scalar
        def _(act):
            for t in range(TT):
                for g in range(2):
                    act.wait_ge(turned, 2 * t + g + 1)
                    act.activation(xo[:, t, g * 512:(g + 1) * 512], ps[:, 2 * t + g, :], ACT.Copy).then_inc(kept, 1)

        @block.sync
        def _(sp):
            for t in range(TT):
                sp.wait_ge(kept, 2 * t + 2)
                sp.dma_start(out[0, t * P:(t + 1) * P, :], xo[:, t, :]).then_inc(stored, 16)
            sp.wait_ge(stored, 16 * TT)


def build(nc, args, out):
    with ExitStack() as ctx:
        core = Core(nc, ctx)
        with ExitStack() as c2:
            stage_start(core, c2, args)
            core.clear(core.sems)
            core.sems.clear()
        stack_one(core, nc, args)
        stack_two(core, nc, args)
        with ExitStack() as c2:
            stage_finish(core, c2, out)


def constants():
    f = np.zeros((P, 7 * P + 8), np.float32)
    f[:, 0:P] = np.eye(P)
    f[:, P:2 * P] = 1.0 / D
    f[:, 2 * P:3 * P] = 1.0 / 256
    f[0:HD, 3 * P:3 * P + HD] = f[HD:P, 3 * P + HD:4 * P] = 1.0 / HD
    for b in (0, HD):
        for i in range(8):
            f[b + i + 8, 4 * P + b + i] = -1.0
            f[b + i, 4 * P + b + i + 8] = 1.0
    f[0:HD, 5 * P:5 * P + HD] = f[0:HD, 5 * P + HD:6 * P] = np.eye(HD)
    f[0:HD, 6 * P:6 * P + HD] = f[0:HD, 6 * P + HD:7 * P] = f[0:HD, 4 * P:4 * P + HD]
    f[:, 7 * P:7 * P + 4] = [EPS, LN_EPS, 1.0, 0.0]
    inv = (np.float32(500000.0) ** (-np.arange(8, dtype=np.float32) * np.float32(2.0) / np.float32(16)))
    for b in (0, 8, HD, HD + 8):
        f[b:b + 8, 7 * P + 4] = inv
    f[:, 7 * P + 5] = np.pi / 2
    d = np.abs(np.arange(TABLE)[None, :] - 3 * P - np.arange(P)[:, None])
    times = (d <= 64) * 1 + ((d % 4 == 0) & (d <= 256)) * 1 + (d % 16 == 0) * 1
    attn = np.stack([d.astype(np.float64), np.where(times > 0, np.log(np.maximum(times, 1)), -BIG)], 1)
    t = np.arange(P)
    masks = np.stack([((t[:, None] // m) ^ (t[None, :] // m)) == 1 for m in LEVELS], 1)
    return {"const_f": f, "const_attn": attn.astype(np.float32).reshape(P, -1),
            "const_mask": masks.astype(np.int32).reshape(P, -1)}


_OUT = (1, S, D)


def kernel(**inputs):
    import concourse.bacc as _bacc
    from concourse.bass_utils import run_bass_kernel_spmd as _run

    nc = _bacc.Bacc("TRN2", target_bir_lowering=False, num_devices=1)
    arrays, args = {}, {}
    for name, a in {**inputs, **constants()}.items():
        a = np.ascontiguousarray(a)
        arrays[f"in_{name}"] = a
        args[name] = nc.dram_tensor(f"in_{name}", a.shape, mybir.dt.from_np(a.dtype), kind="ExternalInput").ap()
    out = nc.dram_tensor("out_x", _OUT, F32, kind="ExternalOutput").ap()
    build(nc, args, out)
    r = _run(nc, [arrays], core_ids=[0])
    return r.results[0]["out_x"]
```

```python
from contextlib import ExitStack

import numpy as np

import concourse.bass as bass
from concourse import mybir

F32 = mybir.dt.float32
F32R = mybir.dt.float32r
I32 = mybir.dt.int32
U8 = mybir.dt.uint8
ALU = mybir.AluOpType
ACT = mybir.ActivationFunctionType
AX = mybir.AxisListType

P = 128
D = 1024
S = 512
DEPTH = 2
KT = D // P
TT = S // P
EPS = 1e-6
LN_EPS = 1e-5
BIG = 1e30

CONV_CH, CONV_W = 256, 31
ATT_W = REC_W = 384
HD = 64
N_HEADS_1 = ATT_W // HD
RT = REC_W // P
D_FF = 2816
FT = D_FF // P
LEVELS = [1, 2, 4, 8, 16, 32, 64]
TABLE = S + 3 * P

N_HEADS_2 = 8
ATT_W2 = 512
TOPK = 128
CHUNK = 64
NCH = S // CHUNK
GLA_H, GLA_DK, GLA_DV = 4, 128, 256
GLA_RANK = 16
GLA_TAU = 16.0
ALPHA = (2.0 * DEPTH) ** 0.25

SLOT = 2048
NSLOT = 2


def cols(w, l, c0, n, kt=KT):
    return w[bass.ds(l, 1), 0:kt * P, c0:c0 + n].rearrange("o (k p) n -> p (o k) n", p=P)


def products(pe, out, w_hi, w_lo, x_hi, x_lo, first, last):
    pe.matmul(out, w_lo, x_hi, start=first, stop=False)
    pe.matmul(out, w_hi, x_hi, start=False, stop=False)
    return pe.matmul(out, w_hi, x_lo, start=False, stop=last)


class Ring:

    def __init__(self, core, ctx, name):
        nc = core.nc
        self.core = core
        self.loaded = [ctx.enter_context(nc.semaphore(f"{name}_slot{s}_loaded")) for s in range(NSLOT)]
        self.hi_ready = ctx.enter_context(nc.semaphore(f"{name}_hi_ready"))
        self.lo_ready = ctx.enter_context(nc.semaphore(f"{name}_lo_ready"))
        self.full = ctx.enter_context(nc.semaphore(f"{name}_tiles_multiplied"))
        core.sems += self.loaded + [self.hi_ready, self.lo_ready, self.full]
        self.units = []
        self.tiles = 0
        self.used_at = []
        self.issued = self.highs = self.lows = 0

    def plan(self, sources):
        first = len(self.units)
        self.units += sources
        return first

    def view(self, buf, i):
        _, kt, n = self.units[i]
        return buf[:, i % NSLOT, 0:kt * n].rearrange("p (k n) -> p k n", k=kt)

    def flat(self, buf, i):
        _, kt, n = self.units[i]
        return buf[:, i % NSLOT, 0:kt * n]

    def hi(self, i):
        return self.view(self.core.w_hi, i)

    def lo(self, i):
        return self.view(self.core.w_lo, i)

    def uses(self, unit, tiles):
        assert unit == len(self.used_at)
        before, self.tiles = self.tiles, self.tiles + tiles
        self.used_at.append(self.tiles)
        return before

    def load_to(self, sp, end):
        while self.issued < min(end, len(self.units)):
            i = self.issued
            if i >= NSLOT:
                sp.wait_ge(self.lo_ready, i - NSLOT + 1)
            sp.dma_start(self.view(self.core.w_raw, i), self.units[i][0]).then_inc(self.loaded[i % NSLOT], 16)
            self.issued += 1

    def high_to(self, act, end):
        while self.highs < min(end, len(self.units)):
            i = self.highs
            act.wait_ge(self.loaded[i % NSLOT], 16 * (i // NSLOT + 1))
            if i >= NSLOT:
                act.wait_ge(self.full, self.used_at[i - NSLOT])
            act.activation(self.flat(self.core.w_hi, i), self.flat(self.core.w_raw, i), ACT.Copy)\
                .then_inc(self.hi_ready, 1)
            self.highs += 1

    def low_to(self, dve, end):
        while self.lows < min(end, len(self.units)):
            i = self.lows
            dve.wait_ge(self.hi_ready, i + 1)
            dve.tensor_tensor(self.flat(self.core.w_lo, i), self.flat(self.core.w_raw, i),
                              self.flat(self.core.w_hi, i).bitcast(F32), ALU.subtract).then_inc(self.lo_ready, 1)
            self.lows += 1

    def arrived(self, pe, i):
        pe.wait_ge(self.lo_ready, i + 1)


class Chain:

    def __init__(self, eng, sem):
        self.eng, self.sem, self.n = eng, sem, 0

    def add(self, ins):
        self.n += 1
        ins.then_inc(self.sem, 1)
        return self.n

    def wait(self, n=None):
        self.eng.wait_ge(self.sem, self.n if n is None else n)

    def link(self, ins):
        self.add(ins)
        self.wait()


class Core:

    def __init__(self, nc, ctx):
        self.nc = nc
        sb = lambda name, shape, dt=F32: ctx.enter_context(nc.sbuf_tensor(name, shape, dt))
        self.ps = ctx.enter_context(nc.psum_tensor("ps", [P, 8, 512], F32))
        self.x = sb("x_res", [P, KT, S])
        self.w_raw = sb("weights_raw", [P, NSLOT, SLOT])
        self.w_hi = sb("weights_hi", [P, NSLOT, SLOT], F32R)
        self.w_lo = sb("weights_lo", [P, NSLOT, SLOT], F32R)
        self.ident = sb("ident", [P, P])
        self.ones = sb("ones", [P, 6, P])
        self.eps = sb("eps", [P, 8])
        self.sems = []

    def sem(self, ctx, name):
        s = ctx.enter_context(self.nc.semaphore(name))
        self.sems.append(s)
        return s

    def clear(self, sems):
        nums = sorted(s.num for s in sems)
        start = prev = nums[0]
        runs = []
        for n in nums[1:]:
            if n != prev + 1:
                runs.append((start, prev + 1))
                start = n
            prev = n
        runs.append((start, prev + 1))
        for a, b in runs:
            self.nc.gpsimd.sem_clear(range(a, b))
        self.nc.all_engine_barrier()


def stage_start(core, ctx, args):
    nc, ps = core.nc, core.ps
    const_in, x_in = args["const_f"], args["x"]
    xin = ctx.enter_context(nc.sbuf_tensor("x_tokens", [P, TT, D], F32))
    loaded = core.sem(ctx, "start_loaded")
    turned = core.sem(ctx, "start_turned")
    kept = core.sem(ctx, "start_kept")
    with nc.Block() as block:
        @block.sync
        def _(sp):
            sp.dma_start(core.ident[:, :], const_in[:, 0:P]).then_inc(loaded, 16)
            sp.dma_start(core.ones[:, :, :].rearrange("p a b -> p (a b)"), const_in[:, P:7 * P]).then_inc(loaded, 16)
            sp.dma_start(core.eps[:, :], const_in[:, 7 * P:7 * P + 8]).then_inc(loaded, 16)
            sp.dma_start(xin[:, :, :], x_in.rearrange("o (t p) d -> p (o t) d", p=P)).then_inc(loaded, 16)

        @block.tensor
        def _(pe):
            pe.wait_ge(loaded, 64)
            for k in range(KT):
                for t in range(TT):
                    ins = pe.transpose(ps[:, k, t * P:(t + 1) * P], xin[:, t, k * P:(k + 1) * P], core.ident[:, :])
                ins.then_inc(turned, 1)

        @block.scalar
        def _(act):
            for k in range(KT):
                act.wait_ge(turned, k + 1)
                act.activation(core.x[:, k, :], ps[:, k, :], ACT.Copy).then_inc(kept, 1)


def stage_columns(core, ctx, name, rows, outs):
    nc, ps = core.nc, core.ps
    groups, g, n = [], [], 0
    for src, k in rows:
        if n + k > P:
            groups.append((g, n))
            g, n = [], 0
        g.append((src, k))
        n += k
    groups.append((g, n))
    stage = ctx.enter_context(nc.sbuf_tensor(f"{name}_rows", [P, len(groups), P], F32))
    loaded = core.sem(ctx, f"{name}_rows_loaded")
    turned = core.sem(ctx, f"{name}_rows_turned")
    kept = core.sem(ctx, f"{name}_columns_kept")
    with nc.Block() as block:
        @block.sync
        def _(sp):
            for i, (g, _) in enumerate(groups):
                r = 0
                for src, k in g:
                    sp.dma_start(stage[r:r + k, i, :], src).then_inc(loaded, 16)
                    r += k

        @block.tensor
        def _(pe):
            pe.wait_ge(loaded, 16 * len(rows))
            for i, (_, n) in enumerate(groups):
                pe.transpose(ps[:, i, 0:n], stage[0:n, i, :], core.ident[0:n, 0:n]).then_inc(turned, 1)

        @block.scalar
        def _(act):
            todo, c = list(outs), 0
            for i, (_, n) in enumerate(groups):
                act.wait_ge(turned, i + 1)
                r = 0
                while r < n:
                    k = min(n - r, todo[0].shape[1] - c)
                    act.activation(todo[0][:, c:c + k], ps[:, i, r:r + k], ACT.Copy).then_inc(kept, 1)
                    r, c = r + k, c + k
                    if c == todo[0].shape[1]:
                        todo, c = todo[1:], 0


def stage_split(core, ctx, name, src, hi, lo, n):
    nc = core.nc
    high = core.sem(ctx, f"{name}_hi")
    low = core.sem(ctx, f"{name}_lo")
    with nc.Block() as block:
        @block.scalar
        def _(act):
            for k in range(n):
                act.activation(hi[:, k, :], src[:, k, :], ACT.Copy).then_inc(high, 1)

        @block.vector
        def _(dve):
            for k in range(n):
                dve.wait_ge(high, k + 1)
                dve.tensor_tensor(lo[:, k, :], src[:, k, :], hi[:, k, :].bitcast(F32), ALU.subtract)\
                    .then_inc(low, 1)


def stage_project(core, ctx, name, ring, jobs, carrier="scalar", mod=None):
    nc, ps = core.nc, core.ps
    full, base = ring.full, ring.tiles
    free = core.sem(ctx, f"{name}_bank_free")
    NB = 7
    banks = []
    for unit, kind, put, src in jobs:
        _, kt, n = ring.units[unit]
        k0 = len(banks)
        if kind == "T":
            assert n % P == 0
            banks += [(unit, False, kind, kt, j * P, P, put, j, src) for j in range(n // P)]
        else:
            banks += [(unit, False, kind, kt, 0, n, put, j, src) for j in range(TT)]
        banks[-1] = banks[-1][:1] + (True,) + banks[-1][2:]
        ring.uses(unit, len(banks) - k0)
    first, end = jobs[0][0], jobs[-1][0] + 1
    with nc.Block() as block:
        @block.sync
        def _(sp):
            if mod is not None:
                mod.load_to(sp, 2)
                for i in range(first, end):
                    ring.load_to(sp, i + 1)
                    mod.load_to(sp, i - first - 1)
                mod.load_to(sp, mod.n)
            ring.load_to(sp, end + 2 * NSLOT)

        @block.tensor
        def _(pe):
            for b, (unit, last, kind, kt, c, m, put, j, (hi, lo)) in enumerate(banks):
                if j == 0:
                    ring.arrived(pe, unit)
                if b >= NB:
                    pe.wait_ge(free, b - NB + 1)
                wh, wl = ring.hi(unit), ring.lo(unit)
                for k in range(kt):
                    if kind == "T":
                        ins = products(pe, ps[:, b % NB, :], wh[:, k, c:c + m], wl[:, k, c:c + m],
                                       hi[:, k, :], lo[:, k, :], k == 0, k == kt - 1)
                    else:
                        t = slice(j * P, (j + 1) * P)
                        ins = products(pe, ps[:, b % NB, 0:m], hi[:, k, t], lo[:, k, t],
                                       wh[:, k, :], wl[:, k, :], k == 0, k == kt - 1)
                ins.then_inc(full, 1)
                if last and mod is not None:
                    mod.fold(pe, unit - first - 2)
            if mod is not None:
                mod.fold(pe, mod.n - 1)

        def carry(eng, highs=None, lows=None):
            for b, (unit, last, kind, kt, c, m, put, j, src) in enumerate(banks):
                if put is not None:
                    eng.wait_ge(full, base + b + 1)
                    put(eng, ps[:, b % NB, 0:m if kind == "tok" else S], j).then_inc(free, 1)
                if last:
                    (highs or lows)(eng, unit + NSLOT + 1)
                    if mod is not None and lows is not None:
                        mod.sum(eng, unit - first)

        @block.scalar
        def _(act):
            ring.high_to(act, first + NSLOT)
            if carrier == "scalar":
                carry(act, highs=ring.high_to)
            ring.high_to(act, end + NSLOT)

        @block.vector
        def _(dve):
            ring.low_to(dve, first + NSLOT)
            if carrier == "vector":
                carry(dve, lows=ring.low_to)
            else:
                for unit in range(first, end):
                    ring.low_to(dve, unit + NSLOT + 1)
                    if mod is not None:
                        mod.sum(dve, unit - first)
            ring.low_to(dve, end + NSLOT)
            if mod is not None:
                mod.finish(dve)


class ModJob:

    def __init__(self, core, ctx, name, w_ada, l, first, n, slots, acc, silu_c, b_cols, mod):
        self.core, self.n, self.first, self.l = core, n, first, l
        self.w_ada, self.silu_c, self.b_cols, self.mod = w_ada, silu_c, b_cols, mod
        self.slots = slots.rearrange("p a b -> p (a b)").rearrange("p (s k n) -> p s k n", s=2, k=KT)
        self.acc = acc
        self.loaded = [core.sem(ctx, f"{name}_slot{s}_loaded") for s in range(2)]
        self.chain = core.sem(ctx, f"{name}_partial_sums")
        self.folded = core.sem(ctx, f"{name}_folded")
        self.done = core.sem(ctx, f"{name}_done")
        self.issued = self.folds = 0

    def load_to(self, sp, end):
        while self.issued < min(end, self.n):
            m = self.issued
            if m >= 2:
                sp.wait_ge(self.chain, KT * (m - 1))
            sp.dma_start(self.slots[:, m % 2], cols(self.w_ada, self.l, 2 * P * (self.first + m), 2 * P))\
                .then_inc(self.loaded[m % 2], 16)
            self.issued += 1

    def sum(self, eng, m):
        if m >= self.n:
            return
        eng.wait_ge(self.loaded[m % 2], 16 * (m // 2 + 1))
        if m >= 2:
            eng.wait_ge(self.folded, m - 1)
        acc = self.acc[:, m % 2, :]
        for k in range(KT):
            w, c = self.slots[:, m % 2, k, :], self.silu_c[:, k:k + 1]
            if k == 0:
                eng.tensor_scalar(acc, w, c, None, ALU.mult).then_inc(self.chain, 1)
            else:
                eng.wait_ge(self.chain, KT * m + k)
                eng.scalar_tensor_tensor(acc, w, c, acc, ALU.mult, ALU.add).then_inc(self.chain, 1)

    def fold(self, pe, to):
        while self.folds <= min(to, self.n - 1):
            m = self.folds
            pe.wait_ge(self.chain, KT * (m + 1))
            for j in range(2):
                ins = pe.matmul(self.core.ps[:, 7, 2 * m + j:2 * m + j + 1], self.acc[:, m % 2, j * P:(j + 1) * P],
                                self.core.eps[:, 2:3], start=True, stop=True)
            ins.then_inc(self.folded, 1)
            self.folds += 1

    def finish(self, dve):
        dve.wait_ge(self.folded, self.n)
        a, b = 2 * self.first, 2 * (self.first + self.n)
        dve.tensor_tensor(self.mod[:, a:b], self.core.ps[:, 7, 0:b - a], self.b_cols[:, a:b], ALU.add)\
            .then_inc(self.done, 1)


def stage_mod(core, job):
    with core.nc.Block() as block:
        @block.sync
        def _(sp):
            job.load_to(sp, job.n)

        @block.vector
        def _(dve):
            for m in range(job.n):
                job.sum(dve, m)
            job.finish(dve)

        @block.tensor
        def _(pe):
            job.fold(pe, job.n - 1)


def stage_rms(core, ctx, name, scale, shift, tmp, out, parts=None):
    nc, ps = core.nc, core.ps
    squared = core.sem(ctx, f"{name}_squared")
    summed = core.sem(ctx, f"{name}_summed")
    rooted = core.sem(ctx, f"{name}_rooted")
    scaled = core.sem(ctx, f"{name}_scaled")
    high = core.sem(ctx, f"{name}_hi")
    low = core.sem(ctx, f"{name}_lo")
    with nc.Block() as block:
        @block.scalar
        def _(act):
            for k in range(KT):
                if k >= 2:
                    act.wait_ge(summed, k - 1)
                act.activation(tmp[:, k % 2, :], core.x[:, k, :], ACT.Square).then_inc(squared, 1)
            act.wait_ge(summed, KT)
            act.activation(tmp[:, 2, :], ps[:, 0, :], ACT.Sqrt, bias=core.eps[:, 0:1]).then_inc(rooted, 1)
            if shift is not None:
                for k in range(KT):
                    act.wait_ge(scaled, k + 2)
                    act.activation(parts[0][:, k, :], tmp[:, 4 + k % 2, :], ACT.Identity,
                                   bias=shift[:, k:k + 1]).then_inc(high, 1)

        @block.tensor
        def _(pe):
            for k in range(KT):
                pe.wait_ge(squared, k + 1)
                pe.matmul(ps[:, 0, :], core.ones[:, 0, :], tmp[:, k % 2, :],
                          start=(k == 0), stop=(k == KT - 1)).then_inc(summed, 1)

        @block.vector
        def _(dve):
            def lower(k):
                dve.wait_ge(high, k + 1)
                dve.scalar_tensor_tensor(parts[1][:, k, :], tmp[:, 4 + k % 2, :], shift[:, k:k + 1],
                                         parts[0][:, k, :].bitcast(F32), ALU.add, ALU.subtract).then_inc(low, 1)
            dve.wait_ge(rooted, 1)
            dve.reciprocal(tmp[:, 3, :], tmp[:, 2, :]).then_inc(scaled, 1)
            dve.wait_ge(scaled, 1)
            for k in range(KT):
                dst = out[:, k, :] if shift is None else tmp[:, 4 + k % 2, :]
                if shift is not None and k >= 2:
                    dve.wait_ge(low, k - 1)
                dve.scalar_tensor_tensor(dst, core.x[:, k, :], scale[:, k:k + 1], tmp[:, 3, :],
                                         ALU.mult, ALU.mult).then_inc(scaled, 1)
                if shift is not None and k >= 1:
                    lower(k - 1)
            if shift is not None:
                lower(KT - 1)


def stage_ffn(core, ctx, name, l, w_up, w_down, taps, bias, lead, gelu, put, bufs, src):
    nc, ps = core.nc, core.ps
    gh, gl, u, c = bufs["gh"], bufs["gl"], bufs["u"], bufs["c"]
    sh, sl = src
    HK = FT // 2
    NP = FT // 2
    NO = KT // 2
    up_loaded = [core.sem(ctx, f"{name}_up_slot{s}_loaded") for s in range(2)]
    up_hi = core.sem(ctx, f"{name}_up_hi")
    up_lo = core.sem(ctx, f"{name}_up_lo")
    up_full = core.sem(ctx, f"{name}_up_full")
    edge = core.sem(ctx, f"{name}_edges_zero")
    u_kept = core.sem(ctx, f"{name}_u_kept")
    tap0 = core.sem(ctx, f"{name}_tap0")
    tap1 = core.sem(ctx, f"{name}_tap1")
    conv = core.sem(ctx, f"{name}_conv")
    act_g = core.sem(ctx, f"{name}_gelu")
    prod = core.sem(ctx, f"{name}_gated")
    g_hi = core.sem(ctx, f"{name}_hidden_hi")
    g_lo = core.sem(ctx, f"{name}_hidden_lo")
    dn_loaded = [core.sem(ctx, f"{name}_down_slot{s}_loaded") for s in range(2)]
    dn_hi = core.sem(ctx, f"{name}_down_hi")
    dn_lo = core.sem(ctx, f"{name}_down_lo")
    dn_full = core.sem(ctx, f"{name}_down_units")
    dn_kept = core.sem(ctx, f"{name}_down_kept")
    UW, DW = KT * 2 * P, HK * P

    up_view = lambda buf, s: buf[:, s, 0:UW].rearrange("p (k h c) -> p k h c", k=KT, h=2)
    dn_view = lambda buf, s: buf[:, s, 0:DW].rearrange("p (k c) -> p k c", k=HK)
    up_src = w_up.rearrange("d (k p) (h n) -> d p k h n", p=P, h=2)
    dn_src = w_down.rearrange("d (k p) n -> d p k n", p=P)

    with nc.Block() as block:
        @block.sync
        def _(sp):
            def up(s, i, peeled=False):
                if not peeled:
                    sp.wait_ge(up_lo, 2 * i + s - 1)
                for h in range(2):
                    sp.dma_start(up_view(core.w_raw, s)[:, :, h, :],
                                 up_src[bass.ds(l, 1), :, :, h, bass.ds(2 * P * i + s * P, P)]
                                 .rearrange("o p k n -> p (o k) n")).then_inc(up_loaded[s], 16)

            def down(s, n, first=False):
                if first:
                    sp.wait_ge(up_lo, FT - 1 + s)
                else:
                    sp.wait_ge(dn_lo, 2 * n + s - 1)
                sp.dma_start(dn_view(core.w_raw, s), dn_src[bass.ds(l, 1), :, s * HK:(s + 1) * HK, bass.ds(P * n, P)]
                             .rearrange("o p k n -> p (o k) n")).then_inc(dn_loaded[s], 16)
            for s in range(2):
                up(s, 0, peeled=True)
            with sp.Fori(1, NP) as i:
                for s in range(2):
                    up(s, i)
            for s in range(2):
                down(s, 0, first=True)
            with sp.Fori(1, KT) as n:
                for s in range(2):
                    down(s, n)

        @block.tensor
        def _(pe):
            def pair(s, i, peeled=False):
                pe.wait_ge(up_lo, 2 * i + s + 1)
                for h in range(2):
                    if not peeled:
                        pe.wait_ge(u_kept, 4 * i + 2 * s + h - 3)
                    for k in range(KT):
                        ins = products(pe, ps[:, 2 * s + h, :], up_view(core.w_hi, s)[:, k, h, :],
                                       up_view(core.w_lo, s)[:, k, h, :], sh[:, k, :], sl[:, k, :],
                                       k == 0, k == KT - 1)
                    ins.then_inc(up_full, 1)
            for s in range(2):
                pair(s, 0, peeled=True)
            with pe.Fori(1, NP) as i:
                for s in range(2):
                    pair(s, i)

            def down(i, peeled=False):
                for b in range(2):
                    if not peeled:
                        pe.wait_ge(dn_kept, 2 * i + b - 1)
                    for s in range(2):
                        pe.wait_ge(dn_lo, 4 * i + 2 * b + s + 1)
                        for k in range(HK):
                            j = s * HK + k
                            ins = products(pe, ps[:, 4 + b, :], dn_view(core.w_hi, s)[:, k, :],
                                           dn_view(core.w_lo, s)[:, k, :], gh[:, j, :], gl[:, j, :],
                                           j == 0, j == FT - 1)
                        ins.then_inc(dn_full, 1)
            pe.wait_ge(g_lo, FT)
            down(0, peeled=True)
            with pe.Fori(1, NO) as i:
                down(i)

        @block.scalar
        def _(act):
            def high_up(s, i, peeled=False):
                act.wait_ge(up_loaded[s], 32 * i + 32)
                if not peeled:
                    act.wait_ge(up_full, 4 * i + 2 * s - 2)
                act.activation(core.w_hi[:, s, 0:UW], core.w_raw[:, s, 0:UW], ACT.Copy).then_inc(up_hi, 1)

            def high_down(s, n, first=False):
                act.wait_ge(dn_loaded[s], 16 * n + 16)
                if first:
                    act.wait_ge(up_full, 2 * (FT - 1 + s))
                else:
                    act.wait_ge(dn_full, 2 * n + s - 1)
                act.activation(core.w_hi[:, s, 0:DW], core.w_raw[:, s, 0:DW], ACT.Copy).then_inc(dn_hi, 1)

            def pair(s, i, ahead, peeled=False):
                for h in range(2):
                    act.wait_ge(up_full, 4 * i + 2 * s + h + 1)
                    if not peeled:
                        act.wait_ge(conv, 4 * i + 2 * s + h - 3)
                    act.activation(u[:, 2 * s + h, lead:lead + S], ps[:, 2 * s + h, :], ACT.Copy)\
                        .then_inc(u_kept, 1)
                for h in range(2):
                    act.wait_ge(u_kept, 4 * i + 2 * s + h + 1)
                    if not peeled:
                        act.wait_ge(g_lo, 2 * i + s - 1)
                    j = 2 * i + s + h * FT
                    act.activation(c[:, 2 * s + h, :], u[:, 2 * s + h, 0:S], ACT.Identity,
                                   bias=(bias[:, bass.ds(j, 1)] if bias is not None else core.eps[:, 3:4]),
                                   scale=taps[:, bass.ds(j, 1)]).then_inc(tap0, 1)
                ahead()
                act.wait_ge(conv, 4 * i + 2 * s + 1)
                act.activation(c[:, 2 * s, :], c[:, 2 * s, :], gelu).then_inc(act_g, 1)
            act.wait_ge(edge, 4)
            for s in range(2):
                high_up(s, 0, peeled=True)
            for s in range(2):
                pair(s, 0, lambda: high_up(s, 1), peeled=True)
            with act.Fori(1, NP - 1) as i:
                for s in range(2):
                    pair(s, i, lambda: high_up(s, i + 1))
            for s in range(2):
                pair(s, NP - 1, lambda: high_down(s, 0, first=True))
            with act.Fori(1, KT) as n:
                for s in range(2):
                    high_down(s, n)

        @block.vector
        def _(dve):
            def low_up(s, i):
                dve.wait_ge(up_hi, 2 * i + s + 1)
                dve.tensor_tensor(core.w_lo[:, s, 0:UW], core.w_raw[:, s, 0:UW],
                                  core.w_hi[:, s, 0:UW].bitcast(F32), ALU.subtract).then_inc(up_lo, 1)

            def low_down(s, n):
                dve.wait_ge(dn_hi, 2 * n + s + 1)
                dve.tensor_tensor(core.w_lo[:, s, 0:DW], core.w_raw[:, s, 0:DW],
                                  core.w_hi[:, s, 0:DW].bitcast(F32), ALU.subtract).then_inc(dn_lo, 1)

            def pair(s, i, ahead):
                j = 2 * i + s
                for h in range(2):
                    dve.wait_ge(tap0, 4 * i + 2 * s + h + 1)
                    cc = c[:, 2 * s + h, :]
                    uu = u[:, 2 * s + h, :]
                    t = [taps[:, bass.ds(j + h * FT + w * 2 * FT, 1)] for w in range(3)]
                    dve.scalar_tensor_tensor(cc, uu[:, 1:1 + S], t[1], cc, ALU.mult, ALU.add).then_inc(tap1, 1)
                    dve.wait_ge(tap1, 4 * i + 2 * s + h + 1)
                    dve.scalar_tensor_tensor(cc, uu[:, 2:2 + S], t[2], cc, ALU.mult, ALU.add).then_inc(conv, 1)
                ahead()
                dve.wait_ge(conv, 4 * i + 2 * s + 2)
                dve.wait_ge(act_g, 2 * i + s + 1)
                cg = c[:, 2 * s:2 * s + 1, :]
                dve.tensor_tensor(cg, cg, c[:, 2 * s + 1:2 * s + 2, :], ALU.mult).then_inc(prod, 1)
                dve.wait_ge(prod, 2 * i + s + 1)
                dve.tensor_copy(gh[:, bass.ds(j, 1), :], cg).then_inc(g_hi, 1)
                dve.wait_ge(g_hi, 2 * i + s + 1)
                dve.tensor_tensor(gl[:, bass.ds(j, 1), :], cg, gh[:, bass.ds(j, 1), :].bitcast(F32), ALU.subtract)\
                    .then_inc(g_lo, 1)
            for q in range(4):
                dve.memset(u[:, q, 0:S + 2], 0.0).then_inc(edge, 1)
            for s in range(2):
                low_up(s, 0)
            for s in range(2):
                pair(s, 0, lambda: low_up(s, 1))
            with dve.Fori(1, NP - 1) as i:
                for s in range(2):
                    pair(s, i, lambda: low_up(s, i + 1))
            for s in range(2):
                pair(s, NP - 1, lambda: low_down(s, 0))

            def out(i, last=False):
                for b in range(2):
                    n = 2 * i + b
                    if not (last and b == 1):
                        for s in range(2):
                            low_down(s, n + 1)
                    dve.wait_ge(dn_full, 2 * n + 2)
                    put(dve, n, ps[:, 4 + b:5 + b, :]).then_inc(dn_kept, 1)
            with dve.Fori(0, NO - 1) as i:
                out(i)
            out(NO - 1, last=True)


def stage_conv(core, ctx, a, gate, taps, cbias, ln_w, ln_b, out, tmp):
    nc, ps = core.nc, core.ps
    C2, half = CONV_CH // P, CONV_W // 2
    pad = ctx.enter_context(nc.sbuf_tensor("conv_pad", [P, C2, S + CONV_W - 1], F32))
    gated = core.sem(ctx, "conv_gated")
    tapped = core.sem(ctx, "conv_tapped")
    meaned = core.sem(ctx, "conv_mean")
    centred = core.sem(ctx, "conv_centred")
    squared = core.sem(ctx, "conv_squared")
    varied = core.sem(ctx, "conv_variance")
    rooted = core.sem(ctx, "conv_rooted")
    normed = core.sem(ctx, "conv_normed")
    acc = lambda k: tmp[:, k, :]
    with nc.Block() as block:
        @block.vector
        def _(dve):
            ch = Chain(dve, core.sem(ctx, "conv_chain"))
            ch.add(dve.memset(pad[:, :, :], 0.0))
            ch.wait()
            for k in range(C2):
                ch.add(dve.tensor_tensor(pad[:, k, half:half + S], a[:, k, :], gate[:, k, :], ALU.mult))
            ch.wait()
            for k in range(C2):
                ch.add(dve.tensor_scalar(acc(k), pad[:, k, 0:S], taps[:, k:k + 1], cbias[:, k:k + 1],
                                         ALU.mult, ALU.add))
            for w in range(1, CONV_W):
                for k in range(C2):
                    ch.wait(ch.n - C2 + 1)
                    ins = dve.scalar_tensor_tensor(acc(k), pad[:, k, w:w + S],
                                                   taps[:, C2 * w + k:C2 * w + k + 1], acc(k), ALU.mult, ALU.add)
                    if w == CONV_W - 1:
                        ins.then_inc(tapped, 1)
                    else:
                        ch.add(ins)
                        continue
                    if k == 0:
                        ch.wait()
            dve.wait_ge(meaned, C2)
            for k in range(C2):
                dve.tensor_tensor(tmp[:, 2 + k, :], acc(k), ps[:, 0, :], ALU.subtract).then_inc(centred, 1)
            dve.wait_ge(rooted, 1)
            ch.link(dve.reciprocal(tmp[:, 7, :], tmp[:, 6, :]))
            dve.wait_ge(centred, C2)
            for k in range(C2):
                dve.scalar_tensor_tensor(acc(k), tmp[:, 2 + k, :], ln_w[:, k:k + 1], tmp[:, 7, :],
                                         ALU.mult, ALU.mult).then_inc(normed, 1)

        @block.tensor
        def _(pe):
            pe.wait_ge(tapped, C2)
            for k in range(C2):
                pe.matmul(ps[:, 0, :], core.ones[:, 1, :], acc(k), start=(k == 0), stop=(k == C2 - 1))\
                    .then_inc(meaned, 1)
            for k in range(C2):
                pe.wait_ge(squared, k + 1)
                pe.matmul(ps[:, 1, :], core.ones[:, 1, :], tmp[:, 4 + k, :], start=(k == 0), stop=(k == C2 - 1))\
                    .then_inc(varied, 1)

        @block.scalar
        def _(act):
            for k in range(C2):
                act.wait_ge(centred, k + 1)
                act.activation(tmp[:, 4 + k, :], tmp[:, 2 + k, :], ACT.Square).then_inc(squared, 1)
            act.wait_ge(varied, C2)
            act.activation(tmp[:, 6, :], ps[:, 1, :], ACT.Sqrt, bias=core.eps[:, 0:1]).then_inc(rooted, 1)
            for k in range(C2):
                act.wait_ge(normed, k + 1)
                act.activation(out[:, k, :], acc(k), ACT.Silu, bias=ln_b[:, k:k + 1]).then_inc(squared, 1)


def stage_attention(core, ctx, name, heads, q, k, v, out, width, bias, prepare=None, preload=None):
    nc, ps = core.nc, core.ps
    sp_ = ctx.enter_context(nc.sbuf_tensor(f"{name}_scores", [P, 3, S], F32))
    pt = ctx.enter_context(nc.sbuf_tensor(f"{name}_probs_turned", [P, 2, S], F32))
    st = ctx.enter_context(nc.sbuf_tensor(f"{name}_stats", [P, 3, 4], F32))
    scored = core.sem(ctx, f"{name}_scored")
    biased = core.sem(ctx, f"{name}_biased")
    maxed = core.sem(ctx, f"{name}_maxed")
    probbed = core.sem(ctx, f"{name}_exponentials")
    inverted = core.sem(ctx, f"{name}_inverted")
    normed = core.sem(ctx, f"{name}_normed")
    turned = core.sem(ctx, f"{name}_turned")
    turned_kept = core.sem(ctx, f"{name}_turned_kept")
    mixed = core.sem(ctx, f"{name}_mixed")
    kept = core.sem(ctx, f"{name}_kept")
    steps = [(h, t) for h in range(heads) for t in range(TT)]
    with nc.Block() as block:
        if preload is not None:
            block.sync(preload)

        @block.tensor
        def _(pe):
            def scores(i):
                h, t = steps[i]
                w, r = width(t), HD * (h % 2)
                if i >= 2:
                    pe.wait_ge(biased, i - 1)
                pe.matmul(ps[:, i % 2, 0:w], q[r:r + HD, h // 2, t * P:(t + 1) * P], k[r:r + HD, h // 2, 0:w],
                          start=True, stop=True).then_inc(scored, 1)

            def values(i):
                h, t = steps[i]
                n, r = width(t) // P, HD * (h % 2)
                pe.wait_ge(normed, i + 1)
                if i >= 2:
                    pe.wait_ge(turned_kept, i - 1)
                for c in range(n):
                    ins = pe.transpose(ps[:, 2 + i % 2, c * P:(c + 1) * P], sp_[:, i % 3, c * P:(c + 1) * P],
                                       core.ident[:, :])
                ins.then_inc(turned, 1)

            def mix(i):
                h, t = steps[i]
                n, r = width(t) // P, HD * (h % 2)
                pe.wait_ge(turned_kept, i + 1)
                if i >= 2:
                    pe.wait_ge(kept, i - 1)
                for c in range(n):
                    ins = pe.matmul(ps[r:r + HD, 4 + i % 2, 0:P], v[:, c, h * HD:(h + 1) * HD],
                                    pt[:, i % 2, c * P:(c + 1) * P], start=(c == 0), stop=(c == n - 1))
                ins.then_inc(mixed, 1)
            for i in range(len(steps) + 2):
                if i < len(steps):
                    scores(i)
                if 1 <= i <= len(steps):
                    values(i - 1)
                if i >= 2:
                    mix(i - 2)

        @block.vector
        def _(dve):
            ch = Chain(dve, core.sem(ctx, f"{name}_chain"))

            def soft(i):
                h, t = steps[i]
                w = width(t)
                if t == 0 and prepare is not None:
                    prepare(dve, ch, h)
                dve.wait_ge(scored, i + 1)
                if i >= 3:
                    dve.wait_ge(turned, i - 2)
                dve.scalar_tensor_tensor(sp_[:, i % 3, 0:w], ps[:, i % 2, 0:w], HD ** -0.5, bias(h, t),
                                         ALU.mult, ALU.add).then_inc(biased, 1)
                dve.wait_ge(biased, i + 1)
                dve.tensor_reduce(st[:, i % 3, 0:1], sp_[:, i % 3, 0:w], AX.X, ALU.max, negate=True)\
                    .then_inc(maxed, 1)

            def norm(i):
                h, t = steps[i]
                w = width(t)
                dve.wait_ge(probbed, i + 1)
                dve.reciprocal(st[:, i % 3, 2:3], st[:, i % 3, 1:2]).then_inc(inverted, 1)
                dve.wait_ge(inverted, i + 1)
                dve.tensor_scalar(sp_[:, i % 3, 0:w], sp_[:, i % 3, 0:w], st[:, i % 3, 2:3], None, ALU.mult)\
                    .then_inc(normed, 1)
            for i in range(len(steps) + 1):
                if i < len(steps):
                    soft(i)
                if i >= 1:
                    norm(i - 1)

        @block.scalar
        def _(act):
            def exps(i):
                h, t = steps[i]
                w = width(t)
                act.wait_ge(maxed, i + 1)
                if i >= 3:
                    act.wait_ge(normed, i - 2)
                act.activation(sp_[:, i % 3, 0:w], sp_[:, i % 3, 0:w], ACT.Exp, bias=st[:, i % 3, 0:1],
                               accum_out=st[:, i % 3, 1:2]).then_inc(probbed, 1)

            def turn(i):
                h, t = steps[i]
                w = width(t)
                act.wait_ge(turned, i + 1)
                if i >= 2:
                    act.wait_ge(mixed, i - 1)
                act.activation(pt[:, i % 2, 0:w], ps[:, 2 + i % 2, 0:w], ACT.Copy).then_inc(turned_kept, 1)

            def keep(i):
                h, t = steps[i]
                r = HD * (h % 2)
                act.wait_ge(mixed, i + 1)
                act.activation(out[r:r + HD, h // 2, t * P:(t + 1) * P], ps[r:r + HD, 4 + i % 2, 0:P], ACT.Copy)\
                    .then_inc(kept, 1)
            for i in range(len(steps) + 2):
                if i < len(steps):
                    exps(i)
                if 1 <= i <= len(steps):
                    turn(i - 1)
                if i >= 2:
                    keep(i - 2)


def stage_recurrence(core, ctx, qr, kf, kb, ff, fb, v, masks, orec, masks_wide, masks_src):
    nc, ps = core.nc, core.ps
    qf = ctx.enter_context(nc.sbuf_tensor("rec_q_fwd", [P, 2, S], F32))
    qb = ctx.enter_context(nc.sbuf_tensor("rec_q_bwd", [P, 2, S], F32))
    ks = ctx.enter_context(nc.sbuf_tensor("rec_k_sum", [P, 2, S], F32))
    tot = ctx.enter_context(nc.sbuf_tensor("rec_totals", [P, 2, S], F32))
    sc = ctx.enter_context(nc.sbuf_tensor("rec_scores", [P, 2, 5 * S], F32))
    started = core.sem(ctx, "rec_started")
    multiplied = core.sem(ctx, "rec_multiplied")
    copied = core.sem(ctx, "rec_copied")
    decayed = core.sem(ctx, "rec_decayed")
    across = core.sem(ctx, "rec_across")
    across_kept = core.sem(ctx, "rec_across_kept")
    mixed = core.sem(ctx, "rec_mixed")
    kept = core.sem(ctx, "rec_kept")
    NL = len(LEVELS)
    diag = lambda h: sc[:, h, :].rearrange("p (i c) -> p i c", c=S + P)[:, :, 0:P]
    full = lambda h: sc[:, h, 0:TT * S].rearrange("p (i t) -> p i t", i=TT)

    masks_in = core.sem(ctx, "rec_masks_loaded")
    with nc.Block() as block:
        @block.sync
        def _(sp):
            sp.dma_start(masks_wide[:, :, :].rearrange("p a b -> p (a b)"), masks_src).then_inc(masks_in, 16)

        @block.tensor
        def _(pe):
            nb = 0
            for p in range(RT):
                pe.wait_ge(started, p + 1)
                for lv in range(NL + 1):
                    if lv >= 1:
                        if lv >= 2:
                            pe.wait_ge(decayed, p * (NL + 1) + lv - 1)
                    for h in range(2):
                        r = h * HD
                        if nb >= 4:
                            pe.wait_ge(copied, nb - 3)
                        bank = ps[:, nb % 4, :]
                        for i in range(TT):
                            if lv == 0:
                                ins = pe.matmul(bank[:, i * P:(i + 1) * P], ks[r:r + HD, p % 2, i * P:(i + 1) * P],
                                                qr[r:r + HD, p, i * P:(i + 1) * P], start=True, stop=True)
                                continue
                            m = LEVELS[lv - 1]
                            tile_q = lambda a: a[r:r + HD, p % 2, i * P:(i + 1) * P]\
                                .rearrange("k (n two m) -> k n two m", two=2, m=m)
                            pe.matmul(bank[:, i * P:i * P + P // 2], kf[r:r + HD, p, i * P:(i + 1) * P],
                                      tile_q(qf)[:, :, 1, :], start=True, stop=True)
                            ins = pe.matmul(bank[:, i * P + P // 2:(i + 1) * P], kb[r:r + HD, p, i * P:(i + 1) * P],
                                            tile_q(qb)[:, :, 0, :], start=True, stop=True)
                        ins.then_inc(multiplied, 1)
                        nb += 1
                for part in range(2):
                    pe.wait_ge(decayed, p * (NL + 1) + NL + part)
                    for h in range(2):
                        r = h * HD
                        if part == 0:
                            if p >= 1:
                                pe.wait_ge(kept, 2 * (p - 1) + h + 1)
                            for i in range(TT):
                                kk, qq = (kf, qf) if i % 2 == 0 else (kb, qb)
                                j = i ^ 1
                                ins = pe.matmul(ps[:, 4 + h, i * P:(i + 1) * P], kk[r:r + HD, p, i * P:(i + 1) * P],
                                                qq[r:r + HD, p % 2, j * P:(j + 1) * P], start=True, stop=True)
                            ins.then_inc(across, 1)
                        else:
                            for half in range(2):
                                kk, qq = (kf, qf) if half == 0 else (kb, qb)
                                q0 = S // 2 * (1 - half)
                                bank = 6 + half
                                if h == 1:
                                    pe.wait_ge(across_kept, 8 * p + 5 + half)
                                elif p >= 1:
                                    pe.wait_ge(across_kept, 8 * p)
                                for i in range(2):
                                    s0 = (2 * half + i) * P
                                    ins = pe.matmul(ps[:, bank, i * 256:(i + 1) * 256], kk[r:r + HD, p, s0:s0 + P],
                                                    qq[r:r + HD, p % 2, q0:q0 + S // 2], start=True, stop=True)
                                ins.then_inc(across, 1)
                pe.wait_ge(copied, nb)
                for h in range(2):
                    r = h * HD
                    pe.wait_ge(across_kept, 8 * p + 8)
                    for i in range(TT):
                        ins = pe.matmul(ps[r:r + HD, 4 + h, :], v[:, i, (2 * p + h) * HD:(2 * p + h + 1) * HD],
                                        full(h)[:, i, :], start=(i == 0), stop=(i == TT - 1))
                    ins.then_inc(mixed, 1)

        @block.vector
        def _(dve):
            ch = Chain(dve, core.sem(ctx, "rec_chain"))
            nb = 0
            for p in range(RT):
                w = p % 2
                if p >= 2:
                    dve.wait_ge(mixed, 2 * (p - 1))
                ch.add(dve.tensor_tensor(qf[:, w, :], qr[:, p, :], ff[:, p, :], ALU.mult))
                ch.add(dve.tensor_tensor(qb[:, w, :], qr[:, p, :], fb[:, p, :], ALU.mult))
                ch.add(dve.tensor_tensor(ks[:, w, :], kf[:, p, :], kb[:, p, :], ALU.add))
                ch.wait()
                dve.sem_inc(started, 1)
                if p == 0:
                    dve.wait_ge(masks_in, 16)
                    for i in range(TT):
                        ch.add(dve.tensor_copy(masks[:, :, i * P:(i + 1) * P], masks_wide[:, :, :]))
                    ch.wait()
                prev_f, prev_b = ff[:, p, :], fb[:, p, :]
                at = 0
                for lv in range(NL + 1):
                    if lv >= 1:
                        m = LEVELS[lv - 1]
                        dve.wait_ge(multiplied, nb + 2)
                        n = S // (2 * m)
                        blk = lambda a: a.rearrange("p (n two m) -> p n two m", two=2, m=m)
                        tf = prev_f.rearrange("p (n two) -> p n two", two=2)
                        tb = prev_b.rearrange("p (n two) -> p n two", two=2)
                        last_f = tf[:, :, 0].unsqueeze(2).to_broadcast([P, n, m])
                        next_f = tf[:, :, 1].unsqueeze(2).to_broadcast([P, n, m])
                        last_b = tb[:, :, 0].unsqueeze(2).to_broadcast([P, n, m])
                        next_b = tb[:, :, 1].unsqueeze(2).to_broadcast([P, n, m])
                        for a, half, f in ((qf[:, w, :], 1, last_f), (qb[:, w, :], 0, next_b),
                                           (kf[:, p, :], 0, next_f), (kb[:, p, :], 1, last_b)):
                            ap = blk(a)[:, :, half, :]
                            ch.add(dve.tensor_tensor(ap, ap, f, ALU.mult))
                        if at + n <= S:
                            nf, nbk = tot[:, 0, at:at + n], tot[:, 1, at:at + n]
                            ch.add(dve.tensor_tensor(nf, tf[:, :, 0], tf[:, :, 1], ALU.mult))
                            ch.add(dve.tensor_tensor(nbk, tb[:, :, 0], tb[:, :, 1], ALU.mult))
                            prev_f, prev_b = nf, nbk
                            at += n
                        ch.wait()
                        dve.sem_inc(decayed, 1)
                    for h in range(2):
                        dve.wait_ge(multiplied, nb + 1)
                        if p >= 1 and lv == 0:
                            dve.wait_ge(mixed, 2 * (p - 1) + h + 1)
                        bank = ps[:, nb % 4, :]
                        if lv == 0:
                            dve.tensor_copy(diag(h), bank.rearrange("p (i c) -> p i c", i=TT)).then_inc(copied, 1)
                        else:
                            m = LEVELS[lv - 1]
                            dve.wait_ge(copied, nb)
                            for part, two in ((0, 1), (1, 0)):
                                for i in range(1):
                                    dst = diag(h).rearrange("p i (n two m) -> p i n two m", two=2, m=m)[:, :, :, two, :]
                                    src = bank.rearrange("p (i two n m) -> p i two n m", i=TT, two=2, m=m)[:, :, part]
                                    msk = masks[:, lv - 1, :].rearrange("p (i n two m) -> p i n two m", i=TT, two=2, m=m)[:, :, :, two, :]
                                    ins = dve.copy_predicated(dst, msk, src)
                                if part == 0:
                                    ch.add(ins)
                                    ch.wait()
                                else:
                                    ins.then_inc(copied, 1)
                        nb += 1
                dve.wait_ge(across, 6 * p + 2)
                m = P
                tf = prev_f
                tb = prev_b
                n = S // (2 * m)
                blk = lambda a: a.rearrange("p (n two m) -> p n two m", two=2, m=m)
                tf = prev_f.rearrange("p (n two) -> p n two", two=2)
                tb = prev_b.rearrange("p (n two) -> p n two", two=2)
                for a, half, f in ((qf[:, w, :], 1, tf[:, :, 0]), (qb[:, w, :], 0, tb[:, :, 1]),
                                   (kf[:, p, :], 0, tf[:, :, 1]), (kb[:, p, :], 1, tb[:, :, 0])):
                    ap = blk(a)[:, :, half, :]
                    ch.add(dve.tensor_tensor(ap, ap, f.unsqueeze(2).to_broadcast([P, n, m]), ALU.mult))
                ch.wait()
                dve.sem_inc(decayed, 1)

        @block.scalar
        def _(act):
            for p in range(RT):
                for h in range(2):
                    act.wait_ge(across, 6 * p + h + 1)
                    if p >= 1:
                        act.wait_ge(mixed, 2 * (p - 1) + h + 1)
                    bank = ps[:, 4 + h, :].rearrange("p (n two c) -> p n two c", two=2, c=P)
                    flat = sc[:, h, :].rearrange("p (n c) -> p n c", c=S * 5 // 2)
                    act.activation(flat[:, :, P:2 * P], bank[:, :, 0, :], ACT.Copy).then_inc(across_kept, 1)
                    act.activation(flat[:, :, S:S + P], bank[:, :, 1, :], ACT.Copy).then_inc(across_kept, 1)
                for h in range(2):
                    for half in range(2):
                        act.wait_ge(across, 6 * p + 3 + 2 * h + half)
                        q0 = S // 2 * (1 - half)
                        ins = act.activation(full(h)[:, 2 * half:2 * half + 2, q0:q0 + S // 2],
                                             ps[:, 6 + half, :].rearrange("p (i c) -> p i c", i=2), ACT.Copy)
                        ins.then_inc(across_kept, 1)
                for h in range(2):
                    r = h * HD
                    act.wait_ge(mixed, 2 * p + h + 1)
                    act.activation(orec[r:r + HD, p, :], ps[r:r + HD, 4 + h, :], ACT.Copy).then_inc(kept, 1)


def stage_rec_norm(core, ctx, o, w, gate, out, tmp):
    nc, ps = core.nc, core.ps
    squared = core.sem(ctx, "recn_squared")
    summed = core.sem(ctx, "recn_summed")
    rooted = core.sem(ctx, "recn_rooted")
    with nc.Block() as block:
        @block.scalar
        def _(act):
            for k in range(RT):
                act.activation(tmp[:, k, :], o[:, k, :], ACT.Square).then_inc(squared, 1)
            for k in range(RT):
                act.wait_ge(summed, k + 1)
                act.activation(tmp[:, 3 + k, :], ps[:, k, :], ACT.Sqrt, bias=core.eps[:, 0:1]).then_inc(rooted, 1)

        @block.tensor
        def _(pe):
            for k in range(RT):
                pe.wait_ge(squared, k + 1)
                pe.matmul(ps[:, k, :], core.ones[:, 2, :], tmp[:, k, :], start=True, stop=True).then_inc(summed, 1)

        @block.vector
        def _(dve):
            ch = Chain(dve, core.sem(ctx, "recn_chain"))
            for k in range(RT):
                dve.wait_ge(rooted, k + 1)
                ch.link(dve.reciprocal(tmp[:, 3 + k, :], tmp[:, 3 + k, :]))
                ch.link(dve.scalar_tensor_tensor(o[:, k, :], o[:, k, :], w[:, k:k + 1], tmp[:, 3 + k, :],
                                                 ALU.mult, ALU.mult))
                ch.add(dve.tensor_tensor(out[:, k, :], o[:, k, :], gate[:, k, :], ALU.mult))


def stage_gates(core, ctx, z_pos, z_neg, lb, one_minus, mod, vec, s2):
    nc = core.nc
    with nc.Block() as block:
        @block.vector
        def _(dve):
            ch = Chain(dve, core.sem(ctx, "gates_chain"))
            ch.add(dve.scalar_tensor_tensor(s2[:, :], mod[:, 32:40], 1.0, vec[:, 8:16], ALU.add, ALU.mult))
            for d in range(2):
                for k in range(RT):
                    j = d * RT + k
                    f, kk = z_pos[d][:, k, :], z_neg[d][:, k, :]
                    ch.add(dve.tensor_scalar(f, f, one_minus[:, j:j + 1], lb[:, j:j + 1], ALU.mult, ALU.add))
                    ch.add(dve.tensor_scalar(kk, kk, one_minus[:, j:j + 1], None, ALU.mult))
            ch.wait()
            for d in range(2):
                ch.add(dve.tensor_scalar(z_pos[d][:, :, :], z_pos[d][:, :, :], 1e-30, None, ALU.max))


def stage_small_1(core, ctx, l_is_one, vec, mod, s1, lb, one_minus):
    nc = core.nc
    diff = core.sem(ctx, "bounds_difference")
    sig = core.sem(ctx, "bounds_sigmoid")
    with nc.Block() as block:
        @block.vector
        def _(dve):
            ch = Chain(dve, core.sem(ctx, "small1_chain"))
            dve.tensor_tensor(lb[:, :], vec[:, 28:34], vec[:, 22:28], ALU.subtract).then_inc(diff, 1)
            ch.add(dve.scalar_tensor_tensor(s1[:, :], mod[:, 8:16], 1.0, vec[:, 0:8], ALU.add, ALU.mult))
            dve.wait_ge(sig, 1)
            ch.link(dve.tensor_scalar(lb[:, :], lb[:, :], l_is_one, None, ALU.mult))
            ch.add(dve.tensor_scalar(one_minus[:, :], lb[:, :], -1.0, 1.0, ALU.mult, ALU.add))

        @block.scalar
        def _(act):
            act.wait_ge(diff, 1)
            act.activation(lb[:, :], lb[:, :], ACT.Sigmoid).then_inc(sig, 1)


def stack_one(core, nc, args):
    with ExitStack() as ctx:
        sb = lambda name, shape, dt=F32: ctx.enter_context(nc.sbuf_tensor(name, shape, dt))
        silu_c = sb("silu_c", [P, KT])
        layer_no = sb("layer_no", [P, 1])
        vec = sb("vec1", [P, 37])
        b_ada = sb("b_ada_cols", [P, 6 * KT])
        mod = sb("mod", [P, 6 * KT])
        ctaps = sb("conv_a_taps", [P, 2 * CONV_W])
        ftaps = sb("conv_f_taps", [P, 3 * 2 * FT])
        s1, s2 = sb("scale1", [P, KT]), sb("scale2", [P, KT])
        lb, om = sb("lower_bound", [P, 2 * RT]), sb("one_minus_lb", [P, 2 * RT])

        with ExitStack() as c2:
            cols_c = c2.enter_context(nc.sbuf_tensor("c_cols", [P, KT], F32))
            first_sem = len(core.sems)
            stage_columns(core, c2, "c", [(args["c"].rearrange("o (n p) -> (o n) p", p=P), KT)], (cols_c,))
            got = core.sem(c2, "silu_c_ready")
            with nc.Block() as block:
                @block.scalar
                def _(act):
                    act.activation(silu_c[:, :], cols_c[:, :], ACT.Silu).then_inc(got, 1)

                @block.vector
                def _(dve):
                    dve.memset(layer_no[:, :], 0.0).then_inc(got, 1)
            core.clear(core.sems[first_sem:])
            del core.sems[first_sem:]

        with nc.Fori(0, DEPTH) as l:
          with ExitStack() as lc:
            first_sem = len(core.sems)
            ring = Ring(core, lc, "ring1")
            w_in, w_out = args["w_in"], args["w_out"]
            plan = [(0, 256, "T"), (256, 256, "T")] + [(512 + 256 * i, 256, "T") for i in range(3)]
            plan += [(1280, 192, "tok"), (1472, 192, "tok")] + [(1664 + 256 * i, 256, "T") for i in range(4)]
            plan += [(2688, 128, "T"), (2816, 192, "tok"), (3008, 192, "tok"), (3200, 256, "T"), (3456, 128, "T")]
            in0 = ring.plan([(cols(w_in, l, c, n), KT, n) for c, n, _ in plan])
            out0 = ring.plan([(cols(w_out, l, 256 * i, 256), KT, 256) for i in range(4)])

            rows = lambda a, n: (a[bass.ds(l, 1), :].rearrange("o (n p) -> (o n) p", p=P), n)
            with ExitStack() as c2:
                stage_columns(core, c2, "vec1", [
                    rows(args["norm1_w"], 8), rows(args["norm2_w"], 8), rows(args["conv_a_b"], 2),
                    rows(args["ln_a_w"], 2), rows(args["ln_a_b"], 2),
                    (args["lb_gamma"].rearrange("d e (n p) -> (d e n) p", p=P), 12), rows(args["rec_norm_w"], 3),
                    rows(args["b_ada"], 48)], (vec, b_ada))
                stage_columns(core, c2, "taps1", [(args["conv_a_w"][bass.ds(l, 1), :, :]
                              .rearrange("o w (n p) -> (o w n) p", p=P), 2 * CONV_W)] +
                              [(args["conv_f_w"][bass.ds(l, 1), w:w + 1, :]
                                .rearrange("o w (n p) -> (o w n) p", p=P), 2 * FT) for w in range(3)], (ctaps, ftaps))
            with ExitStack() as mx:
                msb = lambda name, shape, dt=F32: mx.enter_context(nc.sbuf_tensor(name, shape, dt))
                orec = msb("rec_out", [P, RT, S])
                g_rec = msb("g_rec", [P, RT, S])
                mixed = msb("mixed", [P, KT, S])
                acc = msb("mod_partial", [P, 2, 2 * P])
                stage_mod(core, ModJob(core, lc, "mod_a", args["w_ada"], l, 0, 8, mixed[:, :, :], acc, silu_c, b_ada, mod))
                rx = ExitStack()
                rsb = lambda name, shape, dt=F32: rx.enter_context(nc.sbuf_tensor(name, shape, dt))
                qr, i_rec = rsb("q_rec", [P, RT, S]), rsb("i_rec", [P, TT, REC_W])
                ff, fb = rsb("f_fwd", [P, RT, S]), rsb("f_bwd", [P, RT, S])
                kf, kb = rsb("k_fwd", [P, RT, S]), rsb("k_bwd", [P, RT, S])
                ax = ExitStack()
                asb = lambda name, shape, dt=F32: ax.enter_context(nc.sbuf_tensor(name, shape, dt))
                q, k = asb("q_att", [P, 3, S]), asb("k_att", [P, 3, S])
                v = asb("v_att", [P, TT, ATT_W])
                a, gate = asb("a_val", [P, 2, S]), asb("a_gate", [P, 2, S])
                with ExitStack() as hx:
                    hi, lo = (hx.enter_context(nc.sbuf_tensor(f"h1_{n}", [P, KT, S], F32R)) for n in ("hi", "lo"))
                    with ExitStack() as c2:
                        tmp = mixed
                        stage_small_1(core, lc, layer_no[:, 0:1], vec, mod, s1, lb, om)
                        stage_rms(core, lc, "rms1", s1, mod[:, 0:8], tmp, None, (hi, lo))
                    z_kept = core.sem(lc, "z_gates_kept")

                    def into(tiles):
                        def put(act, view, j):
                            dst, n, f = tiles[j]
                            if f is None:
                                act.activation(dst[0][:, n, :], view, ACT.Sigmoid).then_inc(z_kept, 1)
                                return act.activation(dst[1][:, n, :], view, ACT.Sigmoid, scale=-1.0)
                            return act.activation(dst[:, n, :], view, f)
                        return put
                    order = [(a, 0, ACT.Copy), (a, 1, ACT.Copy), (gate, 0, ACT.Sigmoid), (gate, 1, ACT.Sigmoid)]
                    order += [(q, n, ACT.Copy) for n in range(3)] + [(k, n, ACT.Copy) for n in range(3)]
                    order += [None] * 3 + [(qr, n, ACT.Silu) for n in range(3)]
                    order += [((ff, kf), n, None) for n in range(3)] + [((fb, kb), n, None) for n in range(3)]
                    order += [None] * 3 + [(g_rec, n, ACT.Silu) for n in range(3)]
                    tok = {5: (v, 0), 6: (v, 192), 12: (i_rec, 0), 13: (i_rec, 192)}
                    jobs = []
                    for i, (c, n, kind) in enumerate(plan):
                        if kind == "tok":
                            dst, c0 = tok[i]
                            put = lambda act, view, j, dst=dst, c0=c0: \
                                act.activation(dst[:, j, c0:c0 + 192], view, ACT.Copy)
                        else:
                            put = into(order[c // P:(c + n) // P])
                        jobs.append((in0 + i, kind, put, (hi, lo)))
                    stage_project(core, lc, "in1", ring, jobs,
                                  mod=ModJob(core, lc, "mod_b", args["w_ada"], l, 8, 16, mixed[:, :, :], acc,
                                             silu_c, b_ada, mod))
                stage_gates(core, lc, (ff, fb), (kf, kb), lb, om, mod, vec, s2)
                with ExitStack() as c2:
                    scratch = c2.enter_context(nc.sbuf_tensor("conv_scratch", [P, KT, S], F32))
                    stage_conv(core, c2, a, gate, ctaps, vec[:, 16:18], vec[:, 18:20], vec[:, 20:22],
                               mixed[:, 0:2, :], scratch)
                slopes = [2.0 ** (-8.0 * (h + 1) / N_HEADS_1) for h in range(N_HEADS_1)]
                with ax, ExitStack() as c2:
                    dist_ln = c2.enter_context(nc.sbuf_tensor("attn_tables", [P, 2, TABLE], F32))
                    tab = c2.enter_context(nc.sbuf_tensor("attn_bias", [P, 2, TABLE], F32))
                    tab_in = core.sem(lc, "attn_tables_loaded")

                    def prepare(dve, ch, h):
                        if h == 0:
                            dve.wait_ge(tab_in, 16)
                        ch.link(dve.scalar_tensor_tensor(tab[:, h % 2, :], dist_ln[:, 0, :], -slopes[h],
                                                         dist_ln[:, 1, :], ALU.mult, ALU.add))
                    stage_attention(core, c2, "att1", N_HEADS_1, q, k, v, mixed[:, 2:5, :], lambda t: S,
                                    lambda h, t: tab[:, h % 2, 3 * P - t * P:3 * P - t * P + S], prepare,
                                    lambda sp: sp.dma_start(dist_ln[:, :, :].rearrange("p a b -> p (a b)"),
                                                            args["const_attn"]).then_inc(tab_in, 16))
                with rx, ExitStack() as c2:
                    wide = c2.enter_context(nc.sbuf_tensor("rec_masks_wide", [P, len(LEVELS), P], I32))
                    masks = c2.enter_context(nc.sbuf_tensor("rec_masks", [P, len(LEVELS), S], U8))
                    stage_recurrence(core, c2, qr, kf, kb, ff, fb, i_rec, masks, orec, wide, args["const_mask"])
                hi, lo = (msb(f"mixed_{n}", [P, KT, S], F32R) for n in ("hi", "lo"))
                with ExitStack() as c2:
                    scratch = c2.enter_context(nc.sbuf_tensor("rec_norm_scratch", [P, 6, S], F32))
                    stage_rec_norm(core, lc, orec, vec[:, 34:37], g_rec, mixed[:, 5:8, :], scratch)
                stage_split(core, lc, "mixed", mixed, hi, lo, KT)

                def put1(dve, view, n):
                    return dve.scalar_tensor_tensor(core.x[:, n, :], view, mod[:, 16 + n:17 + n], core.x[:, n, :],
                                                    ALU.mult, ALU.add)
                stage_project(core, lc, "out1", ring,
                              [(out0 + i, "T", (lambda dve, view, j, i=i: put1(dve, view, 2 * i + j)), (hi, lo))
                               for i in range(4)], carrier="vector")
            with ExitStack() as c2:
                hi, lo = (c2.enter_context(nc.sbuf_tensor(f"h2_{n}", [P, KT, S], F32R)) for n in ("hi", "lo"))
                with ExitStack() as c3:
                    tmp = c3.enter_context(nc.sbuf_tensor("rms2_tmp", [P, 6, S], F32))
                    stage_rms(core, lc, "rms2", s2, mod[:, 24:32], tmp, None, (hi, lo))

                def put(dve, n, view):
                    xn = core.x[:, bass.ds(n, 1), :]
                    return dve.scalar_tensor_tensor(xn, view, mod[:, bass.ds(n + 40, 1)], xn, ALU.mult, ALU.add)
                stage_ffn(core, lc, "ffn1", l, args["w_up"], args["w_down"], ftaps, None, 1, ACT.Gelu, put,
                          ffn_buffers(nc, c2, "one"), (hi, lo))
            with nc.Block() as block:
                one = core.sem(lc, "layer_counted")

                @block.vector
                def _(dve):
                    dve.tensor_scalar(layer_no[:, :], layer_no[:, :], 1.0, None, ALU.add).then_inc(one, 1)
            core.clear(core.sems[first_sem:])
            del core.sems[first_sem:]

        with ExitStack() as c2:
            first_sem = len(core.sems)
            fin = c2.enter_context(nc.sbuf_tensor("final_norm_cols", [P, KT], F32))
            stage_columns(core, c2, "fin", [(args["final_norm_w"].rearrange("(n p) -> n p", p=P), KT)], (fin,))
            tmp = c2.enter_context(nc.sbuf_tensor("rms3_tmp", [P, 6, S], F32))
            stage_rms(core, c2, "rms3", fin, None, tmp, core.x)
            core.clear(core.sems[first_sem:])
            del core.sems[first_sem:]


def ffn_buffers(nc, ctx, which):
    sb = lambda name, shape, dt=F32: ctx.enter_context(nc.sbuf_tensor(f"{name}_{which}", shape, dt))
    return {"gh": sb("hidden_hi", [P, FT, S], F32R), "gl": sb("hidden_lo", [P, FT, S], F32R),
            "u": sb("u_padded", [P, 4, S + 2]), "c": sb("u_convolved", [P, 4, S])}


def stage_layernorm(core, ctx, name, src, out, groups, avg, w, b, tmp):
    nc, ps = core.nc, core.ps
    meaned = core.sem(ctx, f"{name}_mean")
    centred = core.sem(ctx, f"{name}_centred")
    squared = core.sem(ctx, f"{name}_squared")
    varied = core.sem(ctx, f"{name}_variance")
    rooted = core.sem(ctx, f"{name}_rooted")
    inverted = core.sem(ctx, f"{name}_inverted")
    normed = core.sem(ctx, f"{name}_normed")
    shifted = core.sem(ctx, f"{name}_shifted")
    flat = [(g, k, k == tiles[0], k == tiles[-1]) for g, tiles in enumerate(groups) for k in tiles]
    with nc.Block() as block:
        @block.tensor
        def _(pe):
            for g, k, first, last in flat:
                pe.matmul(ps[:, g, :], core.ones[:, avg, :], src[:, k, :], start=first, stop=last)\
                    .then_inc(meaned, 1)
            for i, (g, k, first, last) in enumerate(flat):
                pe.wait_ge(squared, i + 1)
                pe.matmul(ps[:, 4 + g, :], core.ones[:, avg, :], tmp[:, i % 2, :], start=first, stop=last)\
                    .then_inc(varied, 1)

        @block.vector
        def _(dve):
            for i, (g, k, first, last) in enumerate(flat):
                dve.wait_ge(meaned, (g + 1) * len(groups[0]))
                dve.tensor_tensor(src[:, k, :], src[:, k, :], ps[:, g, :], ALU.subtract).then_inc(centred, 1)
            for g in range(len(groups)):
                dve.wait_ge(rooted, g + 1)
                dve.reciprocal(tmp[:, 2 + g, :], tmp[:, 2 + g, :]).then_inc(inverted, 1)
            for i, (g, k, first, last) in enumerate(flat):
                dve.wait_ge(inverted, g + 1)
                dve.wait_ge(squared, i + 1)
                dve.scalar_tensor_tensor(out[:, k, :], src[:, k, :], w[:, k:k + 1], tmp[:, 2 + g, :],
                                         ALU.mult, ALU.mult).then_inc(normed, 1)

        @block.scalar
        def _(act):
            for i, (g, k, first, last) in enumerate(flat):
                act.wait_ge(centred, i + 1)
                if i >= 2:
                    act.wait_ge(varied, i - 1)
                act.activation(tmp[:, i % 2, :], src[:, k, :], ACT.Square).then_inc(squared, 1)
            for g in range(len(groups)):
                act.wait_ge(varied, (g + 1) * len(groups[0]))
                act.activation(tmp[:, 2 + g, :], ps[:, 4 + g, :], ACT.Sqrt, bias=core.eps[:, 1:2])\
                    .then_inc(rooted, 1)
            if b is not None:
                for i, (g, k, first, last) in enumerate(flat):
                    act.wait_ge(normed, i + 1)
                    act.activation(out[:, k, :], out[:, k, :], ACT.Identity, bias=b[:, k:k + 1])\
                        .then_inc(shifted, 1)


def stage_angles(core, ctx, positions, cos, sin):
    nc = core.nc
    pos_i = ctx.enter_context(nc.sbuf_tensor("pos_int", [P, S], I32))
    w = ctx.enter_context(nc.sbuf_tensor("angle_work", [P, 4, S], F32))
    loaded = core.sem(ctx, "positions_loaded")
    reduced = core.sem(ctx, "angle_reduced")
    absed = core.sem(ctx, "angle_abs")
    done = core.sem(ctx, "angle_done")
    C1 = 6.28125
    C2 = float(np.float32(np.floor((2 * np.pi - C1) * 2.0 ** 21) / 2.0 ** 21))
    C3 = float(2 * np.pi - C1 - C2)
    ROUND = 12582912.0
    with nc.Block() as block:
        @block.sync
        def _(sp):
            sp.dma_start(pos_i[:, :], positions.partition_broadcast(P)).then_inc(loaded, 16)

        @block.vector
        def _(dve):
            ch = Chain(dve, core.sem(ctx, "angle_chain"))
            dve.wait_ge(loaded, 16)
            ch.link(dve.tensor_copy(w[:, 0, :], pos_i[:, :]))
            ch.link(dve.tensor_scalar(w[:, 1, :], w[:, 0, :], core.eps[:, 4:5], None, ALU.mult))
            ch.link(dve.tensor_scalar(w[:, 2, :], w[:, 1, :], 1.0 / (2 * np.pi), None, ALU.mult))
            ch.link(dve.tensor_scalar(w[:, 2, :], w[:, 2, :], ROUND, None, ALU.add))
            ch.link(dve.tensor_scalar(w[:, 2, :], w[:, 2, :], ROUND, None, ALU.subtract))
            for c in (C1, C2, C3):
                ch.link(dve.scalar_tensor_tensor(w[:, 1, :], w[:, 2, :], -c, w[:, 1, :], ALU.mult, ALU.add))
            dve.tensor_scalar(w[:, 1, :], w[:, 1, :], 3.1415925, -3.1415925, ALU.min, ALU.max).then_inc(reduced, 1)

        @block.scalar
        def _(act):
            act.wait_ge(reduced, 1)
            act.activation(w[:, 3, :], w[:, 1, :], ACT.Abs).then_inc(absed, 1)
            act.activation(sin[:, :], w[:, 1, :], ACT.Sin).then_inc(done, 1)
            act.wait_ge(absed, 1)
            act.activation(cos[:, :], w[:, 3, :], ACT.Sin, bias=core.eps[:, 5:6], scale=-1.0).then_inc(done, 1)


def stage_rope(core, ctx, tiles, ik_raw, ik, cos, sin, tmp):
    nc, ps = core.nc, core.ps
    rotated = core.sem(ctx, "rope_rotated")
    turned = core.sem(ctx, "rope_turned")
    n = len(tiles)
    with nc.Block() as block:
        @block.tensor
        def _(pe):
            for i, x in enumerate(tiles):
                if i >= 4:
                    pe.wait_ge(turned, i - 3)
                pe.matmul(ps[:, i % 4, :], core.ones[:, 3, :], x, start=True, stop=True).then_inc(rotated, 1)
            pe.matmul(ps[:, 4, :], core.ones[0:HD, 4, :], ik_raw, start=True, stop=True)
            pe.matmul(ps[:, 5, :], core.ones[0:HD, 5, :], ik_raw, start=True, stop=True).then_inc(rotated, 1)

        @block.vector
        def _(dve):
            ch = Chain(dve, core.sem(ctx, "rope_chain"))
            for i in range(n + 1):
                dve.wait_ge(rotated, i + 1)
                raw, rot, out = (tiles[i], ps[:, i % 4, :], tiles[i]) if i < n else (ps[:, 4, :], ps[:, 5, :], ik)
                t1, t2 = tmp[:, 2 * (i % 2), :], tmp[:, 2 * (i % 2) + 1, :]
                if i >= 2:
                    dve.wait_ge(turned, i - 1)
                ch.add(dve.tensor_tensor(t1, raw, cos[:, :], ALU.mult))
                ch.add(dve.tensor_tensor(t2, rot, sin[:, :], ALU.mult))
                ch.wait()
                dve.tensor_tensor(out, t1, t2, ALU.add).then_inc(turned, 1)


NEG = -3.0e38


def stage_select(core, ctx, iq, ik, iw, bias):
    nc, ps = core.nc, core.ps
    rl = ctx.enter_context(nc.sbuf_tensor("sel_relu", [P, 4, S], F32))
    sc = ctx.enter_context(nc.sbuf_tensor("sel_scores", [P, 2, S], F32))
    wk = ctx.enter_context(nc.sbuf_tensor("sel_work", [P, 3, S], F32))
    m8 = ctx.enter_context(nc.sbuf_tensor("sel_max8", [P, 8], F32))
    cn = ctx.enter_context(nc.sbuf_tensor("sel_counts", [P, 2], F32))
    dotted = core.sem(ctx, "sel_dotted")
    relued = core.sem(ctx, "sel_relued")
    summed = core.sem(ctx, "sel_summed")
    steps = [(t, h) for t in range(1, TT) for h in range(N_HEADS_2)]
    with nc.Block() as block:
        @block.tensor
        def _(pe):
            for i, (t, h) in enumerate(steps):
                w, r = P * (t + 1), HD * (h % 2)
                if i >= 4:
                    pe.wait_ge(relued, i - 3)
                pe.matmul(ps[:, i % 4, 0:w], iq[r:r + HD, h // 2, t * P:(t + 1) * P], ik[r:r + HD, 0:w],
                          start=True, stop=True).then_inc(dotted, 1)

        @block.scalar
        def _(act):
            for i, (t, h) in enumerate(steps):
                w = P * (t + 1)
                act.wait_ge(dotted, i + 1)
                if i >= 4:
                    act.wait_ge(summed, i - 3)
                act.activation(rl[:, i % 4, 0:w], ps[:, i % 4, 0:w], ACT.Relu, scale=HD ** -0.5).then_inc(relued, 1)

        @block.vector
        def _(dve):
            ch = Chain(dve, core.sem(ctx, "sel_chain"))
            ch.link(dve.memset(bias[:, 0, 0:P], 0.0))
            ch.add(dve.memset(bias[0:HD, 0, HD:P], -BIG))
            for i, (t, h) in enumerate(steps):
                w = P * (t + 1)
                acc = sc[:, t % 2, 0:w]
                dve.wait_ge(relued, i + 1)
                if h == 0:
                    dve.tensor_scalar(acc, rl[:, i % 4, 0:w], iw[:, t, h:h + 1], None, ALU.mult).then_inc(summed, 1)
                else:
                    dve.wait_ge(summed, i)
                    dve.scalar_tensor_tensor(acc, rl[:, i % 4, 0:w], iw[:, t, h:h + 1], acc, ALU.mult, ALU.add)\
                        .then_inc(summed, 1)
                if h < N_HEADS_2 - 1:
                    continue
                dve.wait_ge(summed, i + 1)
                ch.link(dve.memset(sc[0:HD, t % 2, w - CHUNK:w], NEG))
                work = wk[:, 0, 0:w]
                for r in range(TOPK // 8):
                    src = acc if r == 0 else work
                    ch.link(dve.max(m8[:, :], src))
                    if r < TOPK // 8 - 1:
                        ch.link(dve.match_replace(work, m8[:, :], src, NEG))
                least = m8[:, 7:8]
                above, equal = wk[:, 0, 0:w], wk[:, 1, 0:w]
                ch.add(dve.tensor_scalar(equal, acc, least, None, ALU.is_equal))
                ch.link(dve.tensor_scalar(above, acc, least, 0.0, ALU.is_gt, ALU.add, accum_out=cn[:, 0:1]))
                ch.link(dve.tensor_scalar(cn[:, 1:2], cn[:, 0:1], -1.0, float(TOPK), ALU.mult, ALU.add))
                ch.link(dve.tensor_tensor_scan(wk[:, 2, 0:w], equal, equal, 0.0, ALU.add, ALU.max))
                ch.link(dve.scalar_tensor_tensor(equal, wk[:, 2, 0:w], cn[:, 1:2], equal, ALU.is_le, ALU.mult))
                ch.link(dve.tensor_tensor(above, above, equal, ALU.add))
                ch.link(dve.tensor_scalar(bias[:, t, 0:w], above, BIG, -BIG, ALU.mult, ALU.add))


def stage_gla_gates(core, ctx, glr, wg, wg_src, b, gk, la, etot, tmp):
    nc, ps = core.nc, core.ps
    loaded = core.sem(ctx, "gla_w_loaded")
    full = core.sem(ctx, "gla_logits")
    logs = core.sem(ctx, "gla_log")
    steps = core.sem(ctx, "gla_act_chain")
    summed = core.sem(ctx, "gla_centred")
    decay = core.sem(ctx, "gla_decay")
    mask = tmp[:, 7, :]
    with nc.Block() as block:
        @block.sync
        def _(sp):
            sp.dma_start(wg[:, :], wg_src).then_inc(loaded, 16)

        @block.tensor
        def _(pe):
            pe.wait_ge(loaded, 16)
            for h in range(GLA_H):
                pe.matmul(ps[:, h, :], wg[:, h * P:(h + 1) * P], glr[0:GLA_RANK, 0, :], start=True, stop=True)\
                    .then_inc(full, 1)

        @block.scalar
        def _(act):
            ch = Chain(act, steps)
            for h in range(GLA_H):
                act.wait_ge(full, h + 1)
                ch.link(act.activation(tmp[:, 2 + h, :], ps[:, h, :], ACT.Identity, bias=b[:, h:h + 1]))
                ch.link(act.activation(tmp[:, h % 2, :], tmp[:, 2 + h, :], ACT.Abs))
                ch.link(act.activation(tmp[:, h % 2, :], tmp[:, h % 2, :], ACT.Exp, scale=-1.0))
                act.activation(la[:, h, :], tmp[:, h % 2, :], ACT.Ln, bias=core.eps[:, 2:3]).then_inc(logs, 1)
            for h in range(GLA_H):
                act.wait_ge(summed, h + 1)
                act.activation(tmp[:, 2 + h, :], tmp[:, 2 + h, :], ACT.Exp, scale=-1.0 / GLA_TAU).then_inc(decay, 1)
                act.activation(etot[:, h, :], la[:, h, CHUNK - 1:S:CHUNK], ACT.Exp, scale=1.0 / GLA_TAU)\
                    .then_inc(decay, 1)

        @block.vector
        def _(dve):
            ch = Chain(dve, core.sem(ctx, "gla_dve_chain"))
            ch.link(dve.memset(mask, 1.0))
            ch.add(dve.memset(mask.rearrange("p (n c) -> p n c", c=CHUNK)[:, :, 0:1], 0.0))
            for h in range(GLA_H):
                dve.wait_ge(logs, h + 1)
                ch.link(dve.tensor_scalar(tmp[:, 2 + h, :], tmp[:, 2 + h, :], 0.0, None, ALU.min))
                ch.link(dve.tensor_tensor(tmp[:, 6, :], tmp[:, 2 + h, :], la[:, h, :], ALU.subtract))
                ch.link(dve.tensor_tensor_scan(la[:, h, :], mask, tmp[:, 6, :], 0.0, ALU.mult, ALU.add))
                blk = lambda a: a.rearrange("p (n c) -> p n c", c=CHUNK)
                dve.tensor_tensor(blk(tmp[:, 2 + h, :]), blk(la[:, h, :]),
                                  blk(la[:, h, :])[:, :, CHUNK - 1:CHUNK].to_broadcast([P, NCH, CHUNK]),
                                  ALU.subtract).then_inc(summed, 1)
            for h in range(GLA_H):
                dve.wait_ge(decay, 2 * h + 2)
                ch.add(dve.tensor_tensor(gk[:, h, :], gk[:, h, :], tmp[:, 2 + h, :], ALU.mult))


def stage_gla(core, ctx, gq, gk, gv, etot, out):
    nc, ps = core.nc, core.ps
    kt = ctx.enter_context(nc.sbuf_tensor("gla_k_tokens", [P, 2, S], F32))
    st = ctx.enter_context(nc.sbuf_tensor("gla_states", [P, 2, NCH, GLA_DV], F32))
    turned = core.sem(ctx, "gla_turned")
    turned_kept = core.sem(ctx, "gla_turned_kept")
    outer = core.sem(ctx, "gla_outer_products")
    stated = core.sem(ctx, "gla_stated")
    read = core.sem(ctx, "gla_read")
    kept = core.sem(ctx, "gla_kept")
    with nc.Block() as block:
        @block.tensor
        def _(pe):
            def turn(h):
                if h >= 2:
                    pe.wait_ge(turned_kept, h - 1)
                for t in range(TT):
                    ins = pe.transpose(ps[:, h % 2, t * P:(t + 1) * P], gk[:, h, t * P:(t + 1) * P], core.ident[:, :])
                ins.then_inc(turned, 1)

            def product(n):
                h, c = divmod(n, NCH)
                if c == 0:
                    pe.wait_ge(turned_kept, h + 1)
                if n >= 2:
                    pe.wait_ge(stated, n - 1)
                r, t = CHUNK * (c % 2), c // 2
                pe.matmul(ps[:, 2 + n % 2, 0:GLA_DV], kt[r:r + CHUNK, h % 2, t * P:(t + 1) * P],
                          gv[r:r + CHUNK, t, h * GLA_DV:(h + 1) * GLA_DV], start=True, stop=True).then_inc(outer, 1)

            def query(n):
                h, c = divmod(n, NCH)
                if c == 0 and h >= 2:
                    pe.wait_ge(kept, 2 * (h - 1))
                pe.wait_ge(stated, n + 1)
                for half in range(2):
                    ins = pe.matmul(ps[:, 4 + 2 * (h % 2) + half, c * CHUNK:(c + 1) * CHUNK],
                                    st[:, h % 2, c, half * P:(half + 1) * P], gq[:, h, c * CHUNK:(c + 1) * CHUNK],
                                    start=True, stop=True)
                ins.then_inc(read, 1)
            turn(0)
            for n in range(GLA_H * NCH + 1):
                if n < GLA_H * NCH:
                    if n % NCH == 4 and n // NCH + 1 < GLA_H:
                        turn(n // NCH + 1)
                    product(n)
                if n >= 1:
                    query(n - 1)

        @block.vector
        def _(dve):
            for n in range(GLA_H * NCH):
                h, c = divmod(n, NCH)
                dve.wait_ge(outer, n + 1)
                if h >= 2 and c == 0:
                    dve.wait_ge(read, NCH * (h - 1))
                if c == 0:
                    dve.tensor_copy(st[:, h % 2, c, :], ps[:, 2 + n % 2, 0:GLA_DV]).then_inc(stated, 1)
                else:
                    dve.wait_ge(stated, n)
                    dve.scalar_tensor_tensor(st[:, h % 2, c, :], st[:, h % 2, c - 1, :], etot[:, h, c:c + 1],
                                             ps[:, 2 + n % 2, 0:GLA_DV], ALU.mult, ALU.add).then_inc(stated, 1)

        @block.scalar
        def _(act):
            def keep_turned(h):
                act.wait_ge(turned, h + 1)
                if h >= 2:
                    act.wait_ge(outer, NCH * (h - 1))
                act.activation(kt[:, h % 2, :], ps[:, h % 2, :], ACT.Copy).then_inc(turned_kept, 1)
            keep_turned(0)
            for h in range(GLA_H):
                if h + 1 < GLA_H:
                    keep_turned(h + 1)
                act.wait_ge(read, NCH * (h + 1))
                for half in range(2):
                    act.activation(out[:, 2 * h + half, :], ps[:, 4 + 2 * (h % 2) + half, :], ACT.Copy,
                                   scale=GLA_DK ** -0.5).then_inc(kept, 1)


def stage_merge(core, ctx, ring, first, x, att, gla, out):
    nc, ps = core.nc, core.ps
    sg = ctx.enter_context(nc.sbuf_tensor("merge_gates", [P, 4, S], F32))
    tm = ctx.enter_context(nc.sbuf_tensor("merge_part", [P, 2, S], F32))
    base = ring.tiles
    for u in range(16):
        ring.uses(first + u, 2)
    gated = core.sem(ctx, "merge_gated")
    half1 = core.sem(ctx, "merge_products")
    merged = core.sem(ctx, "merge_merged")
    srcs = [(x, KT), (att, ATT_W2 // P), (x, KT), (gla, KT)]
    with nc.Block() as block:
        @block.sync
        def _(sp):
            ring.load_to(sp, first + 16 + 2 * NSLOT)

        @block.tensor
        def _(pe):
            for n in range(4):
                for part, ((hi, lo), kt) in enumerate(srcs):
                    u = first + 4 * n + part
                    ring.arrived(pe, u)
                    if n >= 1:
                        pe.wait_ge(half1 if part % 2 else gated, 4 * (n - 1) + part // 2 * 2 + 2)
                    for j in range(2):
                        for k in range(kt):
                            ins = products(pe, ps[:, 2 * part + j, :], ring.hi(u)[:, k, j * P:(j + 1) * P],
                                           ring.lo(u)[:, k, j * P:(j + 1) * P], hi[:, k, :], lo[:, k, :],
                                           k == 0, k == kt - 1)
                        ins.then_inc(ring.full, 1)

        @block.scalar
        def _(act):
            ring.high_to(act, first + NSLOT)
            for n in range(4):
                for g in range(2):
                    for j in range(2):
                        act.wait_ge(ring.full, base + 8 * n + 4 * g + j + 1)
                        if n >= 1:
                            act.wait_ge(half1, 4 * (n - 1) + 2 * g + j + 1)
                        act.activation(sg[:, 2 * g + j, :], ps[:, 4 * g + j, :], ACT.Sigmoid).then_inc(gated, 1)
                    ring.high_to(act, first + 4 * n + 2 * g + 4)
            ring.high_to(act, first + 16 + NSLOT)

        @block.vector
        def _(dve):
            ring.low_to(dve, first + NSLOT + 1)
            for n in range(4):
                for g in range(2):
                    for j in range(2):
                        dve.wait_ge(ring.full, base + 8 * n + 4 * g + 2 + j + 1)
                        dve.wait_ge(gated, 4 * n + 2 * g + j + 1)
                        if g == 1 and n >= 1:
                            dve.wait_ge(merged, 2 * (n - 1) + j + 1)
                        dst = out[:, 2 * n + j, :] if g == 0 else tm[:, j, :]
                        dve.tensor_tensor(dst, ps[:, 4 * g + 2 + j, :], sg[:, 2 * g + j, :], ALU.mult)\
                            .then_inc(half1, 1)
                    ring.low_to(dve, first + min(4 * n + 2 * g + 5, 16 + NSLOT))
                for j in range(2):
                    dve.wait_ge(half1, 4 * n + 2 + j + 1)
                    dve.tensor_tensor(out[:, 2 * n + j, :], out[:, 2 * n + j, :], tm[:, j, :], ALU.add)\
                        .then_inc(merged, 1)
            ring.low_to(dve, first + 16 + NSLOT)


def stack_two(core, nc, args):
    with ExitStack() as ctx:
        sb = lambda name, shape, dt=F32: ctx.enter_context(nc.sbuf_tensor(name, shape, dt))
        vec = sb("vec2", [P, 52])
        fbias = sb("conv_2_bias", [P, 2 * FT])
        ftaps = sb("conv_2_taps", [P, 3 * 2 * FT])
        x = core.x

        with nc.Fori(0, DEPTH) as l:
          with ExitStack() as lc:
            first_sem = len(core.sems)
            ring = Ring(core, lc, "ring2")
            w_in = args["w_in_2"]
            at = dict(zip(("aq", "ak", "av", "iq", "ik", "iw", "gq", "gk", "gv", "glr", "g_r", "ga", "gb", "end"),
                          np.cumsum([0, 512, 512, 512, 512, 64, 8, 512, 512, 1024, 16, 1024, 1024, 1024]).tolist()))
            two = lambda name, n: [(cols(w_in, l, at[name] + 256 * i, 256), KT, 256) for i in range(n)]
            one = lambda name, n: [(cols(w_in, l, at[name], n), KT, n)]
            in0 = ring.plan(two("aq", 2) + two("ak", 2) + two("av", 2) + two("iq", 2) + one("ik", P) + one("iw", 8))
            gla0 = ring.plan(two("gq", 2) + two("gk", 2) + two("gv", 4) + one("glr", P))
            gr0 = ring.plan(two("g_r", 4))
            mg0 = ring.plan([u for n in range(4) for u in (
                (cols(w_in, l, at["ga"] + 256 * n, 256), KT, 256),
                (cols(args["p_attn_2"], l, 256 * n, 256, kt=4), 4, 256),
                (cols(w_in, l, at["gb"] + 256 * n, 256), KT, 256),
                (cols(args["p_gla_2"], l, 256 * n, 256), KT, 256))])
            out0 = ring.plan([(cols(args["w_mix_out_2"], l, 256 * i, 256), KT, 256) for i in range(4)])

            rows = lambda a, n: (a[bass.ds(l, 1), :].rearrange("o (n p) -> (o n) p", p=P), n)
            with ExitStack() as c2:
                stage_columns(core, c2, "vec2", [rows(args[k + "_2"], n) for k, n in (
                    ("b_mix_out", 8), ("ln1_g", 8), ("ln1_b", 8), ("ln2_g", 8), ("ln2_b", 8),
                    ("gla_b_gate", 4), ("gla_norm_g", 8), ("conv_b", 2 * FT))] + [
                        (args["conv_w_2"][bass.ds(l, 1), w:w + 1, :].rearrange("o w (n p) -> (o w n) p", p=P), 2 * FT)
                        for w in range(3)], (vec, fbias, ftaps))

            keep = lambda dst, f=ACT.Copy, t0=0, **kw: (
                lambda act, view, j: act.activation(dst[:, t0 + j, :], view, f, **kw))
            tok = lambda dst, c0: (lambda act, view, j: act.activation(dst[:, j, c0:c0 + 256], view, ACT.Copy))
            with ExitStack() as mx:
                msb = lambda name, shape, dt=F32: mx.enter_context(nc.sbuf_tensor(name, shape, dt))
                xp = [msb(f"x_{n}", [P, KT, S], F32R) for n in ("hi", "lo")]
                stage_split(core, lc, "x", x, *xp, KT)
                att = msb("att_out2", [P, 4, S])
                with ExitStack() as ax:
                    asb = lambda name, shape, dt=F32: ax.enter_context(nc.sbuf_tensor(name, shape, dt))
                    aq, ak, iq = asb("aq", [P, 4, S]), asb("ak", [P, 4, S]), asb("iq", [P, 4, S])
                    av = asb("av", [P, TT, ATT_W2])
                    ikr, ik, iw = asb("ik_raw", [HD, S]), asb("ik", [P, S]), asb("iw", [P, TT, N_HEADS_2])
                    bias = asb("sel_bias", [P, TT, S])
                    jobs = []
                    for i, dst in enumerate((aq, ak)):
                        jobs += [(in0 + 2 * i + u, "T", keep(dst, t0=2 * u), xp) for u in range(2)]
                    jobs += [(in0 + 4 + u, "tok", tok(av, 256 * u), xp) for u in range(2)]
                    jobs += [(in0 + 6 + u, "T", keep(iq, t0=2 * u), xp) for u in range(2)]
                    jobs += [(in0 + 8, "T", lambda act, view, j: act.activation(ikr[:, :], view[0:HD, :], ACT.Copy), xp),
                             (in0 + 9, "tok", keep(iw, scale=N_HEADS_2 ** -0.5), xp)]
                    stage_project(core, lc, "in2", ring, jobs)
                    with ExitStack() as c2:
                        csb = lambda name, shape: c2.enter_context(nc.sbuf_tensor(name, shape, F32))
                        cos, sin = csb("rope_cos", [P, S]), csb("rope_sin", [P, S])
                        with ExitStack() as c3:
                            stage_angles(core, c3, args["positions_2"], cos, sin)
                        tiles = [a[:, k, :] for a in (iq, aq, ak) for k in range(4)]
                        stage_rope(core, c2, tiles, ikr[:, :], ik[:, :], cos, sin, csb("rope_tmp", [P, 4, S]))
                    with ExitStack() as c2:
                        stage_select(core, c2, iq, ik, iw, bias)
                    with ExitStack() as c2:
                        stage_attention(core, c2, "att2", N_HEADS_2, aq, ak, av, att, lambda t: P * (t + 1),
                                        lambda h, t: bias[:, t, 0:P * (t + 1)])
                gla = msb("gla_out", [P, KT, S])
                with ExitStack() as gx:
                    gsb = lambda name, shape, dt=F32: gx.enter_context(nc.sbuf_tensor(name, shape, dt))
                    gq, gk = gsb("gq", [P, 4, S]), gsb("gk", [P, 4, S])
                    gv = gsb("gv", [P, TT, GLA_H * GLA_DV])
                    etot = gsb("gla_chunk_decay", [P, GLA_H, NCH])
                    glr = gsb("glr", [GLA_RANK, 1, S])
                    jobs = []
                    for i, dst in enumerate((gq, gk)):
                        jobs += [(gla0 + 2 * i + u, "T", keep(dst, t0=2 * u), xp) for u in range(2)]
                    jobs += [(gla0 + 4 + u, "tok", tok(gv, 256 * u), xp) for u in range(4)]
                    jobs += [(gla0 + 8, "T", lambda act, view, j: act.activation(glr[:, 0, :], view[0:GLA_RANK, :],
                                                                                 ACT.Copy), xp)]
                    stage_project(core, lc, "gla_in", ring, jobs)
                    with ExitStack() as c2:
                        csb = lambda name, shape: c2.enter_context(nc.sbuf_tensor(name, shape, F32))
                        stage_gla_gates(core, c2, glr, csb("gla_gate_w", [GLA_RANK, GLA_H * GLA_DK]),
                                        args["gla_w_gate_2"][bass.ds(l, 1), :, :].rearrange("o r n -> (o r) n"),
                                        vec[:, 40:44], gk, csb("gla_log_sums", [P, 4, S]), etot, gla)
                    with ExitStack() as c2:
                        stage_gla(core, c2, gq, gk, gv, etot, gla)
                with ExitStack() as c2:
                    gr = c2.enter_context(nc.sbuf_tensor("g_r", [P, KT, S], F32))
                    stage_layernorm(core, c2, "gla_ln", gla, gla, [[2 * h, 2 * h + 1] for h in range(GLA_H)], 1,
                                    vec[:, 44:52], None, gr)
                    stage_project(core, lc, "g_r", ring,
                                  [(gr0 + i, "T", keep(gr, ACT.Silu, t0=2 * i), xp) for i in range(4)])
                    with nc.Block() as block:
                        gsem = core.sem(lc, "gla_gated")

                        @block.vector
                        def _(dve):
                            for k in range(KT):
                                dve.tensor_tensor(gla[:, k, :], gla[:, k, :], gr[:, k, :], ALU.mult).then_inc(gsem, 1)
                with ExitStack() as c2:
                    csb = lambda name, n: c2.enter_context(nc.sbuf_tensor(name, [P, n, S], F32R))
                    ap = [csb(f"att_{n}", 4) for n in ("hi", "lo")]
                    gp = [csb(f"gla_{n}", KT) for n in ("hi", "lo")]
                    stage_split(core, lc, "att", att, *ap, 4)
                    stage_split(core, lc, "gla", gla, *gp, KT)
                    stage_merge(core, c2, ring, mg0, xp, ap, gp, gla)
                with ExitStack() as c2:
                    csb = lambda name, n: c2.enter_context(nc.sbuf_tensor(name, [P, n, S], F32R))
                    hp = [csb(f"merged_{n}", KT) for n in ("hi", "lo")]
                    stage_split(core, lc, "merged", gla, *hp, KT)
                    pre = core.sem(lc, "residual_scaled")

                    def put1(dve, view, n):
                        dve.tensor_scalar(x[:, n, :], x[:, n, :], ALPHA, vec[:, n:n + 1], ALU.mult, ALU.add)\
                            .then_inc(pre, 1)
                        dve.wait_ge(pre, n + 1)
                        return dve.tensor_tensor(x[:, n, :], view, x[:, n, :], ALU.add)
                    stage_project(core, lc, "out2", ring,
                                  [(out0 + i, "T", (lambda dve, view, j, i=i: put1(dve, view, 2 * i + j)), hp)
                                   for i in range(4)], carrier="vector")
            with ExitStack() as c2:
                xp = [c2.enter_context(nc.sbuf_tensor(f"x2_{n}", [P, KT, S], F32R)) for n in ("hi", "lo")]
                with ExitStack() as c3:
                    tmp = c3.enter_context(nc.sbuf_tensor("ln1_tmp", [P, 3, S], F32))
                    stage_layernorm(core, lc, "ln1", x, x, [list(range(KT))], 0, vec[:, 8:16], vec[:, 16:24], tmp)
                stage_split(core, lc, "x2", x, *xp, KT)

                def put(dve, n, view):
                    xn = x[:, bass.ds(n, 1), :] if not isinstance(n, int) else x[:, n:n + 1, :]
                    return dve.scalar_tensor_tensor(xn, xn, ALPHA, view, ALU.mult, ALU.add)
                stage_ffn(core, lc, "ffn2", l, args["w_up_2"], args["w_down_2"], ftaps, fbias, 2,
                          ACT.Gelu_apprx_tanh, put, ffn_buffers(nc, c2, "two"), xp)
            with ExitStack() as c2:
                tmp = c2.enter_context(nc.sbuf_tensor("ln2_tmp", [P, 3, S], F32))
                stage_layernorm(core, lc, "ln2", x, x, [list(range(KT))], 0, vec[:, 24:32], vec[:, 32:40], tmp)
            core.clear(core.sems[first_sem:])
            del core.sems[first_sem:]


def stage_finish(core, ctx, out):
    nc, ps = core.nc, core.ps
    xo = ctx.enter_context(nc.sbuf_tensor("x_out", [P, TT, D], F32))
    turned = core.sem(ctx, "finish_turned")
    kept = core.sem(ctx, "finish_kept")
    stored = core.sem(ctx, "finish_stored")
    with nc.Block() as block:
        @block.tensor
        def _(pe):
            for t in range(TT):
                for g in range(2):
                    for k in range(4):
                        ins = pe.transpose(ps[:, 2 * t + g, k * P:(k + 1) * P],
                                           core.x[:, 4 * g + k, t * P:(t + 1) * P], core.ident[:, :])
                    ins.then_inc(turned, 1)

        @block.scalar
        def _(act):
            for t in range(TT):
                for g in range(2):
                    act.wait_ge(turned, 2 * t + g + 1)
                    act.activation(xo[:, t, g * 512:(g + 1) * 512], ps[:, 2 * t + g, :], ACT.Copy).then_inc(kept, 1)

        @block.sync
        def _(sp):
            for t in range(TT):
                sp.wait_ge(kept, 2 * t + 2)
                sp.dma_start(out[0, t * P:(t + 1) * P, :], xo[:, t, :]).then_inc(stored, 16)
            sp.wait_ge(stored, 16 * TT)


def build(nc, args, out):
    with ExitStack() as ctx:
        core = Core(nc, ctx)
        with ExitStack() as c2:
            stage_start(core, c2, args)
            core.clear(core.sems)
            core.sems.clear()
        stack_one(core, nc, args)
        stack_two(core, nc, args)
        with ExitStack() as c2:
            stage_finish(core, c2, out)


def constants():
    f = np.zeros((P, 7 * P + 8), np.float32)
    f[:, 0:P] = np.eye(P)
    f[:, P:2 * P] = 1.0 / D
    f[:, 2 * P:3 * P] = 1.0 / 256
    f[0:HD, 3 * P:3 * P + HD] = f[HD:P, 3 * P + HD:4 * P] = 1.0 / HD
    for b in (0, HD):
        for i in range(8):
            f[b + i + 8, 4 * P + b + i] = -1.0
            f[b + i, 4 * P + b + i + 8] = 1.0
    f[0:HD, 5 * P:5 * P + HD] = f[0:HD, 5 * P + HD:6 * P] = np.eye(HD)
    f[0:HD, 6 * P:6 * P + HD] = f[0:HD, 6 * P + HD:7 * P] = f[0:HD, 4 * P:4 * P + HD]
    f[:, 7 * P:7 * P + 4] = [EPS, LN_EPS, 1.0, 0.0]
    inv = (np.float32(500000.0) ** (-np.arange(8, dtype=np.float32) * np.float32(2.0) / np.float32(16)))
    for b in (0, 8, HD, HD + 8):
        f[b:b + 8, 7 * P + 4] = inv
    f[:, 7 * P + 5] = np.pi / 2
    d = np.abs(np.arange(TABLE)[None, :] - 3 * P - np.arange(P)[:, None])
    times = (d <= 64) * 1 + ((d % 4 == 0) & (d <= 256)) * 1 + (d % 16 == 0) * 1
    attn = np.stack([d.astype(np.float64), np.where(times > 0, np.log(np.maximum(times, 1)), -BIG)], 1)
    t = np.arange(P)
    masks = np.stack([((t[:, None] // m) ^ (t[None, :] // m)) == 1 for m in LEVELS], 1)
    return {"const_f": f, "const_attn": attn.astype(np.float32).reshape(P, -1),
            "const_mask": masks.astype(np.int32).reshape(P, -1)}


_OUT = (1, S, D)


def kernel(**inputs):
    import concourse.bacc as _bacc
    from concourse.bass_utils import run_bass_kernel_spmd as _run

    nc = _bacc.Bacc("TRN2", target_bir_lowering=False, num_devices=1)
    arrays, args = {}, {}
    for name, a in {**inputs, **constants()}.items():
        a = np.ascontiguousarray(a)
        arrays[f"in_{name}"] = a
        args[name] = nc.dram_tensor(f"in_{name}", a.shape, mybir.dt.from_np(a.dtype), kind="ExternalInput").ap()
    out = nc.dram_tensor("out_x", _OUT, F32, kind="ExternalOutput").ap()
    build(nc, args, out)
    r = _run(nc, [arrays], core_ids=[0])
    return r.results[0]["out_x"]
```

```python
from contextlib import ExitStack

import numpy as np

import concourse.bass as bass
from concourse import mybir

F32 = mybir.dt.float32
F32R = mybir.dt.float32r
I32 = mybir.dt.int32
U8 = mybir.dt.uint8
ALU = mybir.AluOpType
ACT = mybir.ActivationFunctionType
AX = mybir.AxisListType

P = 128
D = 1024
S = 512
DEPTH = 2
KT = D // P
TT = S // P
EPS = 1e-6
LN_EPS = 1e-5
BIG = 1e30

CONV_CH, CONV_W = 256, 31
ATT_W = REC_W = 384
HD = 64
N_HEADS_1 = ATT_W // HD
RT = REC_W // P
D_FF = 2816
FT = D_FF // P
LEVELS = [1, 2, 4, 8, 16, 32, 64]
TABLE = S + 3 * P

N_HEADS_2 = 8
ATT_W2 = 512
TOPK = 128
CHUNK = 64
NCH = S // CHUNK
GLA_H, GLA_DK, GLA_DV = 4, 128, 256
GLA_RANK = 16
GLA_TAU = 16.0
ALPHA = (2.0 * DEPTH) ** 0.25

SLOT = 2048
NSLOT = 2


def cols(w, l, c0, n, kt=KT):
    return w[bass.ds(l, 1), 0:kt * P, c0:c0 + n].rearrange("o (k p) n -> p (o k) n", p=P)


def products(pe, out, w_hi, w_lo, x_hi, x_lo, first, last):
    pe.matmul(out, w_lo, x_hi, start=first, stop=False)
    pe.matmul(out, w_hi, x_hi, start=False, stop=False)
    return pe.matmul(out, w_hi, x_lo, start=False, stop=last)


class Ring:

    def __init__(self, core, ctx, name):
        nc = core.nc
        self.core = core
        self.loaded = [ctx.enter_context(nc.semaphore(f"{name}_slot{s}_loaded")) for s in range(NSLOT)]
        self.hi_ready = ctx.enter_context(nc.semaphore(f"{name}_hi_ready"))
        self.lo_ready = ctx.enter_context(nc.semaphore(f"{name}_lo_ready"))
        self.full = ctx.enter_context(nc.semaphore(f"{name}_tiles_multiplied"))
        core.sems += self.loaded + [self.hi_ready, self.lo_ready, self.full]
        self.units = []
        self.tiles = 0
        self.used_at = []
        self.issued = self.highs = self.lows = 0

    def plan(self, sources):
        first = len(self.units)
        self.units += sources
        return first

    def view(self, buf, i):
        _, kt, n = self.units[i]
        return buf[:, i % NSLOT, 0:kt * n].rearrange("p (k n) -> p k n", k=kt)

    def flat(self, buf, i):
        _, kt, n = self.units[i]
        return buf[:, i % NSLOT, 0:kt * n]

    def hi(self, i):
        return self.view(self.core.w_hi, i)

    def lo(self, i):
        return self.view(self.core.w_lo, i)

    def uses(self, unit, tiles):
        assert unit == len(self.used_at)
        before, self.tiles = self.tiles, self.tiles + tiles
        self.used_at.append(self.tiles)
        return before

    def load_to(self, sp, end):
        while self.issued < min(end, len(self.units)):
            i = self.issued
            if i >= NSLOT:
                sp.wait_ge(self.lo_ready, i - NSLOT + 1)
            sp.dma_start(self.view(self.core.w_raw, i), self.units[i][0]).then_inc(self.loaded[i % NSLOT], 16)
            self.issued += 1

    def high_to(self, act, end):
        while self.highs < min(end, len(self.units)):
            i = self.highs
            act.wait_ge(self.loaded[i % NSLOT], 16 * (i // NSLOT + 1))
            if i >= NSLOT:
                act.wait_ge(self.full, self.used_at[i - NSLOT])
            act.activation(self.flat(self.core.w_hi, i), self.flat(self.core.w_raw, i), ACT.Copy)\
                .then_inc(self.hi_ready, 1)
            self.highs += 1

    def low_to(self, dve, end):
        while self.lows < min(end, len(self.units)):
            i = self.lows
            dve.wait_ge(self.hi_ready, i + 1)
            dve.tensor_tensor(self.flat(self.core.w_lo, i), self.flat(self.core.w_raw, i),
                              self.flat(self.core.w_hi, i).bitcast(F32), ALU.subtract).then_inc(self.lo_ready, 1)
            self.lows += 1

    def load_ahead(self, sp):
        self.load_to(sp, NSLOT)

    def split_high(self, act):
        self.high_to(act, NSLOT)

    def split_low(self, dve):
        self.low_to(dve, NSLOT)

    def load_more(self, sp):
        self.load_to(sp, 2 * NSLOT)

    def arrived(self, pe, i):
        pe.wait_ge(self.lo_ready, i + 1)


class Chain:

    def __init__(self, eng, sem):
        self.eng, self.sem, self.n = eng, sem, 0

    def add(self, ins):
        self.n += 1
        ins.then_inc(self.sem, 1)
        return self.n

    def wait(self, n=None):
        self.eng.wait_ge(self.sem, self.n if n is None else n)

    def link(self, ins):
        self.add(ins)
        self.wait()


class Core:

    def __init__(self, nc, ctx):
        self.nc = nc
        sb = lambda name, shape, dt=F32: ctx.enter_context(nc.sbuf_tensor(name, shape, dt))
        self.ps = ctx.enter_context(nc.psum_tensor("ps", [P, 8, 512], F32))
        self.x = sb("x_res", [P, KT, S])
        self.w_raw = sb("weights_raw", [P, NSLOT, SLOT])
        self.w_hi = sb("weights_hi", [P, NSLOT, SLOT], F32R)
        self.w_lo = sb("weights_lo", [P, NSLOT, SLOT], F32R)
        self.ident = sb("ident", [P, P])
        self.ones = sb("ones", [P, 6, P])
        self.eps = sb("eps", [P, 8])
        self.sems = []

    def sem(self, ctx, name):
        s = ctx.enter_context(self.nc.semaphore(name))
        self.sems.append(s)
        return s

    def clear(self, sems):
        nums = sorted(s.num for s in sems)
        start = prev = nums[0]
        runs = []
        for n in nums[1:]:
            if n != prev + 1:
                runs.append((start, prev + 1))
                start = n
            prev = n
        runs.append((start, prev + 1))
        for a, b in runs:
            self.nc.gpsimd.sem_clear(range(a, b))
        self.nc.all_engine_barrier()


def stage_start(core, ctx, args):
    nc, ps = core.nc, core.ps
    const_in, x_in = args["const_f"], args["x"]
    xin = ctx.enter_context(nc.sbuf_tensor("x_tokens", [P, TT, D], F32))
    loaded = core.sem(ctx, "start_loaded")
    turned = core.sem(ctx, "start_turned")
    kept = core.sem(ctx, "start_kept")
    with nc.Block() as block:
        @block.sync
        def _(sp):
            sp.dma_start(core.ident[:, :], const_in[:, 0:P]).then_inc(loaded, 16)
            sp.dma_start(core.ones[:, :, :].rearrange("p a b -> p (a b)"), const_in[:, P:7 * P]).then_inc(loaded, 16)
            sp.dma_start(core.eps[:, :], const_in[:, 7 * P:7 * P + 8]).then_inc(loaded, 16)
            sp.dma_start(xin[:, :, :], x_in.rearrange("o (t p) d -> p (o t) d", p=P)).then_inc(loaded, 16)

        @block.tensor
        def _(pe):
            pe.wait_ge(loaded, 64)
            for k in range(KT):
                for t in range(TT):
                    ins = pe.transpose(ps[:, k, t * P:(t + 1) * P], xin[:, t, k * P:(k + 1) * P], core.ident[:, :])
                ins.then_inc(turned, 1)

        @block.scalar
        def _(act):
            for k in range(KT):
                act.wait_ge(turned, k + 1)
                act.activation(core.x[:, k, :], ps[:, k, :], ACT.Copy).then_inc(kept, 1)


def stage_columns(core, ctx, name, rows, outs, ahead=None, mod=None):
    nc, ps = core.nc, core.ps
    groups, g, n = [], [], 0
    for src, k in rows:
        if n + k > P:
            groups.append((g, n))
            g, n = [], 0
        g.append((src, k))
        n += k
    groups.append((g, n))
    stage = ctx.enter_context(nc.sbuf_tensor(f"{name}_rows", [P, len(groups), P], F32))
    loaded = core.sem(ctx, f"{name}_rows_loaded")
    turned = core.sem(ctx, f"{name}_rows_turned")
    kept = core.sem(ctx, f"{name}_columns_kept")
    with nc.Block() as block:
        @block.sync
        def _(sp):
            for i, (g, _) in enumerate(groups):
                r = 0
                for src, k in g:
                    sp.dma_start(stage[r:r + k, i, :], src).then_inc(loaded, 16)
                    r += k
            if mod is not None:
                mod.load_to(sp, mod.n)
            if ahead is not None:
                ahead.load_ahead(sp)

        @block.tensor
        def _(pe):
            pe.wait_ge(loaded, 16 * len(rows))
            for i, (_, n) in enumerate(groups):
                pe.transpose(ps[:, i, 0:n], stage[0:n, i, :], core.ident[0:n, 0:n]).then_inc(turned, 1)
            if mod is not None:
                mod.fold(pe, mod.n - 1)

        @block.scalar
        def _(act):
            todo, c = list(outs), 0
            for i, (_, n) in enumerate(groups):
                act.wait_ge(turned, i + 1)
                r = 0
                while r < n:
                    k = min(n - r, todo[0].shape[1] - c)
                    act.activation(todo[0][:, c:c + k], ps[:, i, r:r + k], ACT.Copy).then_inc(kept, 1)
                    r, c = r + k, c + k
                    if c == todo[0].shape[1]:
                        todo, c = todo[1:], 0

        if mod is not None:
            @block.vector
            def _(dve):
                for m in range(mod.n):
                    mod.sum(dve, m)
                mod.finish(dve)


class Split:

    def __init__(self, core, ctx, name, src, hi, lo, n):
        self.src, self.hi, self.lo, self.n = src, hi, lo, n
        self.high_done = core.sem(ctx, f"{name}_hi")
        self.low_done = core.sem(ctx, f"{name}_lo")

    def high(self, act):
        for k in range(self.n):
            act.activation(self.hi[:, k, :], self.src[:, k, :], ACT.Copy).then_inc(self.high_done, 1)

    def low(self, dve):
        for k in range(self.n):
            dve.wait_ge(self.high_done, k + 1)
            dve.tensor_tensor(self.lo[:, k, :], self.src[:, k, :], self.hi[:, k, :].bitcast(F32), ALU.subtract)\
                .then_inc(self.low_done, 1)


class Projection:

    def __init__(self, core, ctx, name, ring, jobs, carrier="scalar", mod=None, ahead=None, feed=None, rope=None, bank0=0, nbanks=7):
        self.core, self.ring, self.carrier, self.mod, self.ahead = core, ring, carrier, mod, ahead
        self.rope = rope
        self.feed, self.bank0, self.nbanks = feed, bank0, nbanks
        self.base = ring.tiles
        self.free = core.sem(ctx, f"{name}_bank_free")
        self.first, self.end = jobs[0][0], jobs[-1][0] + 1
        self.units, n = [], 0
        for unit, kind, put, src in jobs:
            _, kt, width = ring.units[unit]
            tiles = width // P if kind == "T" else TT
            assert kind == "tok" or width % P == 0
            ring.uses(unit, tiles)
            self.units.append((unit, kind, put, src, kt, width, tiles, n))
            n += tiles
        self.at = {"tensor": 0, "scalar": 0, "vector": 0}

    def todo(self, engine, upto):
        a = self.at[engine]
        b = len(self.units) if upto is None else min(upto, len(self.units))
        self.at[engine] = max(a, b)
        return self.units[a:b]

    def bank(self, b):
        return self.core.ps[:, self.bank0 + b % self.nbanks, :]

    def sync(self, sp):
        ring, mod, first, end = self.ring, self.mod, self.first, self.end
        if mod is not None:
            mod.load_to(sp, 2)
            for i in range(first, end):
                ring.load_to(sp, i + 1)
                mod.load_to(sp, i - first - 1)
            mod.load_to(sp, mod.n)
        ring.load_to(sp, end + 2 * NSLOT)
        if self.ahead is not None:
            sp.wait_ge(ring.lo_ready, end)
            self.ahead.load_ahead(sp)

    def tensor(self, pe, upto=None):
        ring = self.ring
        for unit, kind, put, (hi, lo), kt, width, tiles, b0 in self.todo("tensor", upto):
            ring.arrived(pe, unit)
            wh, wl = ring.hi(unit), ring.lo(unit)
            for j in range(tiles):
                b = b0 + j
                if b >= self.nbanks:
                    pe.wait_ge(self.free, b - self.nbanks + 1)
                bank = self.bank(b)
                for k in range(kt):
                    if b == 0 and self.feed is not None:
                        pe.wait_ge(self.feed.low_done, k + 1)
                    t = slice(j * P, (j + 1) * P)
                    if kind == "T":
                        ins = products(pe, bank, wh[:, k, t], wl[:, k, t], hi[:, k, :], lo[:, k, :],
                                       k == 0, k == kt - 1)
                    else:
                        ins = products(pe, bank[:, 0:width], hi[:, k, t], lo[:, k, t], wh[:, k, :], wl[:, k, :],
                                       k == 0, k == kt - 1)
                ins.then_inc(ring.full, 1)
            if self.mod is not None:
                self.mod.fold(pe, unit - self.first - 2)
            if self.rope is not None:
                self.rope.tensor(pe, unit - self.first, self)

    def carry(self, eng, job):
        unit, kind, put, src, kt, width, tiles, b0 = job
        for j in range(tiles):
            eng.wait_ge(self.ring.full, self.base + b0 + j + 1)
            put(eng, self.bank(b0 + j)[:, 0:width if kind == "tok" else S], j).then_inc(self.free, 1)

    def scalar(self, act, upto=None):
        for job in self.todo("scalar", upto):
            if self.carrier == "scalar":
                self.carry(act, job)
            self.ring.high_to(act, job[0] + NSLOT + 1)

    def vector(self, dve, upto=None):
        for job in self.todo("vector", upto):
            if self.carrier == "vector":
                self.carry(dve, job)
            self.ring.low_to(dve, job[0] + NSLOT + 1)
            if self.mod is not None:
                self.mod.sum(dve, job[0] - self.first)
            if self.rope is not None:
                self.rope.vector(dve, job[0] - self.first)


def stage_project(core, ctx, name, ring, jobs, **how):
    job = Projection(core, ctx, name, ring, jobs, **how)
    with core.nc.Block() as block:
        block.sync(job.sync)

        @block.tensor
        def _(pe):
            job.tensor(pe)
            if job.mod is not None:
                job.mod.fold(pe, job.mod.n - 1)

        @block.scalar
        def _(act):
            if job.feed is not None:
                job.feed.high(act)
            ring.high_to(act, job.first + NSLOT)
            job.scalar(act)

        @block.vector
        def _(dve):
            if job.feed is not None:
                job.feed.low(dve)
            ring.low_to(dve, job.first + NSLOT)
            job.vector(dve)
            if job.mod is not None:
                job.mod.finish(dve)


class ModJob:

    def __init__(self, core, ctx, name, w_ada, l, first, n, slots, acc, silu_c, b_cols, mod):
        self.core, self.n, self.first, self.l = core, n, first, l
        self.w_ada, self.silu_c, self.b_cols, self.mod = w_ada, silu_c, b_cols, mod
        self.slots = slots.rearrange("p a b -> p (a b)").rearrange("p (s k n) -> p s k n", s=2, k=KT)
        self.acc = acc
        self.loaded = [core.sem(ctx, f"{name}_slot{s}_loaded") for s in range(2)]
        self.chain = core.sem(ctx, f"{name}_partial_sums")
        self.folded = core.sem(ctx, f"{name}_folded")
        self.done = core.sem(ctx, f"{name}_done")
        self.issued = self.folds = 0

    def load_to(self, sp, end):
        while self.issued < min(end, self.n):
            m = self.issued
            if m >= 2:
                sp.wait_ge(self.chain, KT * (m - 1))
            sp.dma_start(self.slots[:, m % 2], cols(self.w_ada, self.l, 2 * P * (self.first + m), 2 * P))\
                .then_inc(self.loaded[m % 2], 16)
            self.issued += 1

    def sum(self, eng, m):
        if m >= self.n:
            return
        eng.wait_ge(self.loaded[m % 2], 16 * (m // 2 + 1))
        if m >= 2:
            eng.wait_ge(self.folded, m - 1)
        acc = self.acc[:, m % 2, :]
        for k in range(KT):
            w, c = self.slots[:, m % 2, k, :], self.silu_c[:, k:k + 1]
            if k == 0:
                eng.tensor_scalar(acc, w, c, None, ALU.mult).then_inc(self.chain, 1)
            else:
                eng.wait_ge(self.chain, KT * m + k)
                eng.scalar_tensor_tensor(acc, w, c, acc, ALU.mult, ALU.add).then_inc(self.chain, 1)

    def fold(self, pe, to):
        while self.folds <= min(to, self.n - 1):
            m = self.folds
            pe.wait_ge(self.chain, KT * (m + 1))
            for j in range(2):
                ins = pe.matmul(self.core.ps[:, 7, 2 * m + j:2 * m + j + 1], self.acc[:, m % 2, j * P:(j + 1) * P],
                                self.core.eps[:, 2:3], start=True, stop=True)
            ins.then_inc(self.folded, 1)
            self.folds += 1

    def finish(self, dve):
        dve.wait_ge(self.folded, self.n)
        a, b = 2 * self.first, 2 * (self.first + self.n)
        dve.tensor_tensor(self.mod[:, a:b], self.core.ps[:, 7, 0:b - a], self.b_cols[:, a:b], ALU.add)\
            .then_inc(self.done, 1)


class RmsNorm:

    def __init__(self, core, ctx, name, scale, shift, tmp, hi=None, lo=None):
        self.core, self.scale, self.shift, self.tmp, self.hi, self.lo = core, scale, shift, tmp, hi, lo
        self.squared = core.sem(ctx, f"{name}_squared")
        self.summed = core.sem(ctx, f"{name}_summed")
        self.rooted = core.sem(ctx, f"{name}_rooted")
        self.inverted = core.sem(ctx, f"{name}_inverted")
        self.scaled = core.sem(ctx, f"{name}_scaled")
        self.high_done = core.sem(ctx, f"{name}_hi")
        self.low_done = core.sem(ctx, f"{name}_lo")

    def stage(self, ahead=None):
        core, ps, tmp = self.core, self.core.ps, self.tmp
        with core.nc.Block() as block:
            @block.scalar
            def _(act):
                for k in range(KT):
                    if k >= 2:
                        act.wait_ge(self.summed, k - 1)
                    act.activation(tmp[:, k % 2, :], core.x[:, k, :], ACT.Square).then_inc(self.squared, 1)
                act.wait_ge(self.summed, KT)
                act.activation(tmp[:, 2, :], ps[:, 0, :], ACT.Sqrt, bias=core.eps[:, 0:1]).then_inc(self.rooted, 1)
                if ahead is not None:
                    ahead.split_high(act)

            @block.tensor
            def _(pe):
                for k in range(KT):
                    pe.wait_ge(self.squared, k + 1)
                    pe.matmul(ps[:, 0, :], core.ones[:, 0, :], tmp[:, k % 2, :],
                              start=(k == 0), stop=(k == KT - 1)).then_inc(self.summed, 1)

            @block.vector
            def _(dve):
                dve.wait_ge(self.rooted, 1)
                dve.reciprocal(tmp[:, 2, :], tmp[:, 2, :]).then_inc(self.inverted, 1)
                if self.shift is None:
                    dve.wait_ge(self.inverted, 1)
                    for k in range(KT):
                        self.scaling(dve, k, core.x[:, k, :])
                if ahead is not None:
                    ahead.split_low(dve)

            if ahead is not None:
                block.sync(ahead.load_more)

    def scaling(self, dve, k, dst):
        dve.scalar_tensor_tensor(dst, self.core.x[:, k, :], self.scale[:, k:k + 1], self.tmp[:, 2, :],
                                 ALU.mult, ALU.mult).then_inc(self.scaled, 1)

    def high(self, act):
        for k in range(KT):
            act.wait_ge(self.scaled, k + 1)
            act.activation(self.hi[:, k, :], self.tmp[:, k % 2, :], ACT.Identity,
                           bias=self.shift[:, k:k + 1]).then_inc(self.high_done, 1)

    def low(self, dve):
        for k in range(KT + 1):
            if k < KT:
                if k >= 2:
                    dve.wait_ge(self.low_done, k - 1)
                self.scaling(dve, k, self.tmp[:, k % 2, :])
            if k >= 1:
                j = k - 1
                dve.wait_ge(self.high_done, j + 1)
                dve.scalar_tensor_tensor(self.lo[:, j, :], self.tmp[:, j % 2, :], self.shift[:, j:j + 1],
                                         self.hi[:, j, :].bitcast(F32), ALU.add, ALU.subtract)\
                    .then_inc(self.low_done, 1)


class FfnStart:

    def __init__(self, core, ctx, name, l, w_up):
        self.core, self.l = core, l
        self.loaded = [core.sem(ctx, f"{name}_up_slot{s}_loaded") for s in range(2)]
        self.hi = core.sem(ctx, f"{name}_up_hi")
        self.lo = core.sem(ctx, f"{name}_up_lo")
        self.src = w_up.rearrange("d (k p) (h n) -> d p k h n", p=P, h=2)
        self.width = KT * 2 * P

    def view(self, buf, s):
        return buf[:, s, 0:self.width].rearrange("p (k h c) -> p k h c", k=KT, h=2)

    def load(self, sp, s, i):
        for h in range(2):
            sp.dma_start(self.view(self.core.w_raw, s)[:, :, h, :],
                         self.src[bass.ds(self.l, 1), :, :, h, bass.ds(2 * P * i + s * P, P)]
                         .rearrange("o p k n -> p (o k) n")).then_inc(self.loaded[s], 16)

    def load_ahead(self, sp):
        for s in range(2):
            self.load(sp, s, 0)

    def load_more(self, sp):
        pass

    def split_high(self, act):
        for s in range(2):
            act.wait_ge(self.loaded[s], 32)
            act.activation(self.core.w_hi[:, s, 0:self.width], self.core.w_raw[:, s, 0:self.width], ACT.Copy)\
                .then_inc(self.hi, 1)

    def split_low(self, dve):
        for s in range(2):
            dve.wait_ge(self.hi, s + 1)
            dve.tensor_tensor(self.core.w_lo[:, s, 0:self.width], self.core.w_raw[:, s, 0:self.width],
                              self.core.w_hi[:, s, 0:self.width].bitcast(F32), ALU.subtract).then_inc(self.lo, 1)


def stage_ffn(core, ctx, name, l, start, w_down, taps, bias, lead, gelu, put, bufs, src, feed):
    nc, ps = core.nc, core.ps
    gh, gl, u, c = bufs["gh"], bufs["gl"], bufs["u"], bufs["c"]
    sh, sl = src
    HK = FT // 2
    NP = FT // 2
    NO = KT // 2
    up_loaded, up_hi, up_lo, up_view = start.loaded, start.hi, start.lo, start.view
    up_full = core.sem(ctx, f"{name}_up_full")
    edge = core.sem(ctx, f"{name}_edges_zero")
    u_kept = core.sem(ctx, f"{name}_u_kept")
    tap0 = core.sem(ctx, f"{name}_tap0")
    tap1 = core.sem(ctx, f"{name}_tap1")
    conv = core.sem(ctx, f"{name}_conv")
    act_g = core.sem(ctx, f"{name}_gelu")
    prod = core.sem(ctx, f"{name}_gated")
    g_hi = core.sem(ctx, f"{name}_hidden_hi")
    g_lo = core.sem(ctx, f"{name}_hidden_lo")
    dn_loaded = [core.sem(ctx, f"{name}_down_slot{s}_loaded") for s in range(2)]
    dn_hi = core.sem(ctx, f"{name}_down_hi")
    dn_lo = core.sem(ctx, f"{name}_down_lo")
    dn_full = core.sem(ctx, f"{name}_down_units")
    dn_kept = core.sem(ctx, f"{name}_down_kept")
    UW, DW = KT * 2 * P, HK * P

    dn_view = lambda buf, s: buf[:, s, 0:DW].rearrange("p (k c) -> p k c", k=HK)
    dn_src = w_down.rearrange("d (k p) n -> d p k n", p=P)

    with nc.Block() as block:
        @block.sync
        def _(sp):
            def down(s, n, first=False):
                if first:
                    sp.wait_ge(up_lo, FT - 1 + s)
                else:
                    sp.wait_ge(dn_lo, 2 * n + s - 1)
                sp.dma_start(dn_view(core.w_raw, s), dn_src[bass.ds(l, 1), :, s * HK:(s + 1) * HK, bass.ds(P * n, P)]
                             .rearrange("o p k n -> p (o k) n")).then_inc(dn_loaded[s], 16)
            with sp.Fori(1, NP) as i:
                for s in range(2):
                    sp.wait_ge(up_lo, 2 * i + s - 1)
                    start.load(sp, s, i)
            for s in range(2):
                down(s, 0, first=True)
            with sp.Fori(1, KT) as n:
                for s in range(2):
                    down(s, n)

        @block.tensor
        def _(pe):
            def pair(s, i, peeled=False):
                pe.wait_ge(up_lo, 2 * i + s + 1)
                for h in range(2):
                    if not peeled:
                        pe.wait_ge(u_kept, 4 * i + 2 * s + h - 3)
                    for k in range(KT):
                        if peeled and s == 0 and h == 0:
                            pe.wait_ge(feed.low_done, k + 1)
                        ins = products(pe, ps[:, 2 * s + h, :], up_view(core.w_hi, s)[:, k, h, :],
                                       up_view(core.w_lo, s)[:, k, h, :], sh[:, k, :], sl[:, k, :],
                                       k == 0, k == KT - 1)
                    ins.then_inc(up_full, 1)
            for s in range(2):
                pair(s, 0, peeled=True)
            with pe.Fori(1, NP) as i:
                for s in range(2):
                    pair(s, i)

            def down(i, peeled=False):
                for b in range(2):
                    if not peeled:
                        pe.wait_ge(dn_kept, 2 * i + b - 1)
                    for s in range(2):
                        pe.wait_ge(dn_lo, 4 * i + 2 * b + s + 1)
                        if peeled and b == 0:
                            pe.wait_ge(g_lo, HK * (s + 1))
                        for k in range(HK):
                            j = s * HK + k
                            ins = products(pe, ps[:, 4 + b, :], dn_view(core.w_hi, s)[:, k, :],
                                           dn_view(core.w_lo, s)[:, k, :], gh[:, j, :], gl[:, j, :],
                                           j == 0, j == FT - 1)
                        ins.then_inc(dn_full, 1)
            down(0, peeled=True)
            with pe.Fori(1, NO) as i:
                down(i)

        @block.scalar
        def _(act):
            def high_up(s, i):
                act.wait_ge(up_loaded[s], 32 * i + 32)
                act.wait_ge(up_full, 4 * i + 2 * s - 2)
                act.activation(core.w_hi[:, s, 0:UW], core.w_raw[:, s, 0:UW], ACT.Copy).then_inc(up_hi, 1)

            def high_down(s, n, first=False):
                act.wait_ge(dn_loaded[s], 16 * n + 16)
                if first:
                    act.wait_ge(up_full, 2 * (FT - 1 + s))
                else:
                    act.wait_ge(dn_full, 2 * n + s - 1)
                act.activation(core.w_hi[:, s, 0:DW], core.w_raw[:, s, 0:DW], ACT.Copy).then_inc(dn_hi, 1)

            def pair(s, i, ahead, peeled=False):
                for h in range(2):
                    act.wait_ge(up_full, 4 * i + 2 * s + h + 1)
                    if not peeled:
                        act.wait_ge(conv, 4 * i + 2 * s + h - 3)
                    act.activation(u[:, 2 * s + h, lead:lead + S], ps[:, 2 * s + h, :], ACT.Copy)\
                        .then_inc(u_kept, 1)
                for h in range(2):
                    act.wait_ge(u_kept, 4 * i + 2 * s + h + 1)
                    if not peeled:
                        act.wait_ge(g_lo, 2 * i + s - 1)
                    j = 2 * i + s + h * FT
                    act.activation(c[:, 2 * s + h, :], u[:, 2 * s + h, 0:S], ACT.Identity,
                                   bias=(bias[:, bass.ds(j, 1)] if bias is not None else core.eps[:, 3:4]),
                                   scale=taps[:, bass.ds(j, 1)]).then_inc(tap0, 1)
                ahead()
                act.wait_ge(conv, 4 * i + 2 * s + 1)
                act.activation(c[:, 2 * s, :], c[:, 2 * s, :], gelu).then_inc(act_g, 1)
            feed.high(act)
            act.wait_ge(edge, 4)
            for s in range(2):
                pair(s, 0, lambda: high_up(s, 1), peeled=True)
            with act.Fori(1, NP - 1) as i:
                for s in range(2):
                    pair(s, i, lambda: high_up(s, i + 1))
            for s in range(2):
                pair(s, NP - 1, lambda: high_down(s, 0, first=True))
            with act.Fori(1, KT) as n:
                for s in range(2):
                    high_down(s, n)

        @block.vector
        def _(dve):
            def low_up(s, i):
                dve.wait_ge(up_hi, 2 * i + s + 1)
                dve.tensor_tensor(core.w_lo[:, s, 0:UW], core.w_raw[:, s, 0:UW],
                                  core.w_hi[:, s, 0:UW].bitcast(F32), ALU.subtract).then_inc(up_lo, 1)

            def low_down(s, n):
                dve.wait_ge(dn_hi, 2 * n + s + 1)
                dve.tensor_tensor(core.w_lo[:, s, 0:DW], core.w_raw[:, s, 0:DW],
                                  core.w_hi[:, s, 0:DW].bitcast(F32), ALU.subtract).then_inc(dn_lo, 1)

            def pair(s, i, ahead):
                j = 2 * i + s
                for h in range(2):
                    dve.wait_ge(tap0, 4 * i + 2 * s + h + 1)
                    cc = c[:, 2 * s + h, :]
                    uu = u[:, 2 * s + h, :]
                    t = [taps[:, bass.ds(j + h * FT + w * 2 * FT, 1)] for w in range(3)]
                    dve.scalar_tensor_tensor(cc, uu[:, 1:1 + S], t[1], cc, ALU.mult, ALU.add).then_inc(tap1, 1)
                    dve.wait_ge(tap1, 4 * i + 2 * s + h + 1)
                    dve.scalar_tensor_tensor(cc, uu[:, 2:2 + S], t[2], cc, ALU.mult, ALU.add).then_inc(conv, 1)
                ahead()
                dve.wait_ge(conv, 4 * i + 2 * s + 2)
                dve.wait_ge(act_g, 2 * i + s + 1)
                cg = c[:, 2 * s:2 * s + 1, :]
                dve.tensor_tensor(cg, cg, c[:, 2 * s + 1:2 * s + 2, :], ALU.mult).then_inc(prod, 1)
                dve.wait_ge(prod, 2 * i + s + 1)
                dve.tensor_copy(gh[:, bass.ds(j, 1), :], cg).then_inc(g_hi, 1)
                dve.wait_ge(g_hi, 2 * i + s + 1)
                dve.tensor_tensor(gl[:, bass.ds(j, 1), :], cg, gh[:, bass.ds(j, 1), :].bitcast(F32), ALU.subtract)\
                    .then_inc(g_lo, 1)
            feed.low(dve)
            for q in range(4):
                dve.memset(u[:, q, 0:S + 2], 0.0).then_inc(edge, 1)
            for s in range(2):
                pair(s, 0, lambda: low_up(s, 1))
            with dve.Fori(1, NP - 1) as i:
                for s in range(2):
                    pair(s, i, lambda: low_up(s, i + 1))
            for s in range(2):
                pair(s, NP - 1, lambda: low_down(s, 0))

            def out(i, last=False):
                for b in range(2):
                    n = 2 * i + b
                    if not (last and b == 1):
                        for s in range(2):
                            low_down(s, n + 1)
                    dve.wait_ge(dn_full, 2 * n + 2)
                    put(dve, n, ps[:, 4 + b:5 + b, :]).then_inc(dn_kept, 1)
            with dve.Fori(0, NO - 1) as i:
                out(i)
            out(NO - 1, last=True)


class ConvJob:

    def __init__(self, core, ctx, pad, acc, taps, cbias):
        self.core, self.pad, self.acc, self.taps, self.cbias = core, pad, acc, taps, cbias
        self.C2 = CONV_CH // P
        self.padded = core.sem(ctx, "conv_padded")
        self.tapped = core.sem(ctx, "conv_tapped")
        self.sem = lambda name: core.sem(ctx, f"conv_{name}")
        self.issued = 0

    def start(self, dve, a, gate):
        half = CONV_W // 2
        dve.memset(self.pad[:, :, :], 0.0).then_inc(self.padded, 1)
        dve.wait_ge(self.padded, 1)
        for k in range(self.C2):
            dve.tensor_tensor(self.pad[:, k, half:half + S], a[:, k, :], gate[:, k, :], ALU.mult)\
                .then_inc(self.padded, 1)

    def steps(self, dve, n):
        for i in range(self.issued, min(self.issued + n, CONV_W * self.C2)):
            w, k = i // self.C2, i % self.C2
            src, tap = self.pad[:, k, w:w + S], self.taps[:, i:i + 1]
            if w == 0:
                ins = dve.tensor_scalar(self.acc[:, k, :], src, tap, self.cbias[:, k:k + 1], ALU.mult, ALU.add)
            else:
                dve.wait_ge(self.tapped, i - self.C2 + 1)
                ins = dve.scalar_tensor_tensor(self.acc[:, k, :], src, tap, self.acc[:, k, :], ALU.mult, ALU.add)
            ins.then_inc(self.tapped, 1)
            self.issued += 1

    def norm(self, tmp, bank, ln_w, ln_b):
        core, ps, C2, acc = self.core, self.core.ps, self.C2, self.acc
        meaned, centred, squared = self.sem("mean"), self.sem("centred"), self.sem("squared")
        varied, rooted, inverted = self.sem("variance"), self.sem("rooted"), self.sem("inverted")
        normed = self.sem("normed")
        mean, var = ps[:, bank, :], ps[:, bank + 1, :]

        def tensor_mean(pe):
            for k in range(C2):
                pe.matmul(mean, core.ones[:, 1, :], acc[:, k, :], start=(k == 0), stop=(k == C2 - 1))\
                    .then_inc(meaned, 1)

        def tensor_variance(pe):
            for k in range(C2):
                pe.wait_ge(squared, k + 1)
                pe.matmul(var, core.ones[:, 1, :], tmp[:, 2 + k, :], start=(k == 0), stop=(k == C2 - 1))\
                    .then_inc(varied, 1)

        def scalar_squares(act):
            for k in range(C2):
                act.wait_ge(centred, k + 1)
                act.activation(tmp[:, 2 + k, :], tmp[:, k, :], ACT.Square).then_inc(squared, 1)

        def scalar_root(act):
            act.wait_ge(varied, C2)
            act.activation(tmp[:, 4, :], var, ACT.Sqrt, bias=core.eps[:, 0:1]).then_inc(rooted, 1)

        def scalar_silu(act):
            for k in range(C2):
                act.wait_ge(normed, k + 1)
                act.activation(acc[:, k, :], acc[:, k, :], ACT.Silu, bias=ln_b[:, k:k + 1]).then_inc(squared, 1)

        def vector_centre(dve):
            dve.wait_ge(meaned, C2)
            for k in range(C2):
                dve.tensor_tensor(tmp[:, k, :], acc[:, k, :], mean, ALU.subtract).then_inc(centred, 1)

        def vector_scale(dve):
            dve.wait_ge(rooted, 1)
            dve.reciprocal(tmp[:, 5, :], tmp[:, 4, :]).then_inc(inverted, 1)
            dve.wait_ge(inverted, 1)
            dve.wait_ge(centred, C2)
            for k in range(C2):
                dve.scalar_tensor_tensor(acc[:, k, :], tmp[:, k, :], ln_w[:, k:k + 1], tmp[:, 5, :],
                                         ALU.mult, ALU.mult).then_inc(normed, 1)
        return (tensor_mean, tensor_variance), (scalar_squares, scalar_root, scalar_silu), (vector_centre, vector_scale)


def stage_attention(core, ctx, name, heads, q, k, v, out, width, bias, prepare=None, preload=None, scratch=None):
    nc, ps = core.nc, core.ps
    NORM, TURN, MIX = 2, 4, 5
    SB = 6
    score_bank = lambda i: ps[:, i % 3, :]
    turned_bank = lambda i: ps[:, 3 + i % 2, :]
    mixed_bank = 5
    if scratch is None:
        scratch = ctx.enter_context(nc.sbuf_tensor(f"{name}_scratch", [P, SB + 2, S], F32))
    sp_, pt = scratch[:, 0:SB, :], scratch[:, SB:SB + 2, :]
    st = ctx.enter_context(nc.sbuf_tensor(f"{name}_stats", [P, SB, 4], F32))
    scored = core.sem(ctx, f"{name}_scored")
    biased = core.sem(ctx, f"{name}_biased")
    maxed = core.sem(ctx, f"{name}_maxed")
    probbed = core.sem(ctx, f"{name}_exponentials")
    inverted = core.sem(ctx, f"{name}_inverted")
    normed = core.sem(ctx, f"{name}_normed")
    turned = core.sem(ctx, f"{name}_turned")
    turned_kept = core.sem(ctx, f"{name}_turned_kept")
    mixed = core.sem(ctx, f"{name}_mixed")
    kept = core.sem(ctx, f"{name}_kept")
    steps = [(h, t) for h in range(heads) for t in range(TT)]
    with nc.Block() as block:
        if preload is not None:
            block.sync(preload)

        @block.tensor
        def _(pe):
            def scores(i):
                h, t = steps[i]
                w, r = width(t), HD * (h % 2)
                if i >= 3:
                    pe.wait_ge(biased, i - 2)
                pe.matmul(score_bank(i)[:, 0:w], q[r:r + HD, h // 2, t * P:(t + 1) * P], k[r:r + HD, h // 2, 0:w],
                          start=True, stop=True).then_inc(scored, 1)

            def values(i):
                h, t = steps[i]
                n, r = width(t) // P, HD * (h % 2)
                pe.wait_ge(normed, i + 1)
                if i >= 2:
                    pe.wait_ge(turned_kept, i - 1)
                for c in range(n):
                    ins = pe.transpose(turned_bank(i)[:, c * P:(c + 1) * P], sp_[:, i % SB, c * P:(c + 1) * P],
                                       core.ident[:, :])
                ins.then_inc(turned, 1)

            def mix(i):
                h, t = steps[i]
                n, r = width(t) // P, HD * (h % 2)
                pe.wait_ge(turned_kept, i + 1)
                if i >= 2:
                    pe.wait_ge(kept, i - 1)
                for c in range(n):
                    ins = pe.matmul(ps[r:r + HD, mixed_bank + i % 2, 0:P], v[:, c, h * HD:(h + 1) * HD],
                                    pt[:, i % 2, c * P:(c + 1) * P], start=(c == 0), stop=(c == n - 1))
                ins.then_inc(mixed, 1)
            for i in range(len(steps) + MIX):
                if i < len(steps):
                    scores(i)
                if TURN <= i < len(steps) + TURN:
                    values(i - TURN)
                if i >= MIX:
                    mix(i - MIX)

        @block.vector
        def _(dve):
            ch = Chain(dve, core.sem(ctx, f"{name}_chain"))

            def soft(i):
                h, t = steps[i]
                w = width(t)
                if t == 0 and prepare is not None:
                    prepare(dve, ch, h)
                dve.wait_ge(scored, i + 1)
                if i >= SB:
                    dve.wait_ge(turned, i - SB + 1)
                dve.scalar_tensor_tensor(sp_[:, i % SB, 0:w], score_bank(i)[:, 0:w], HD ** -0.5, bias(h, t),
                                         ALU.mult, ALU.add).then_inc(biased, 1)
                dve.wait_ge(biased, i + 1)
                dve.tensor_reduce(st[:, i % SB, 0:1], sp_[:, i % SB, 0:w], AX.X, ALU.max, negate=True)\
                    .then_inc(maxed, 1)

            def norm(i):
                h, t = steps[i]
                w = width(t)
                dve.wait_ge(probbed, i + 1)
                dve.reciprocal(st[:, i % SB, 2:3], st[:, i % SB, 1:2]).then_inc(inverted, 1)
                dve.wait_ge(inverted, i + 1)
                dve.tensor_scalar(sp_[:, i % SB, 0:w], sp_[:, i % SB, 0:w], st[:, i % SB, 2:3], None, ALU.mult)\
                    .then_inc(normed, 1)
            for i in range(len(steps) + NORM):
                if i < len(steps):
                    soft(i)
                if i >= NORM:
                    norm(i - NORM)

        @block.scalar
        def _(act):
            def exps(i):
                h, t = steps[i]
                w = width(t)
                act.wait_ge(maxed, i + 1)
                if i >= SB:
                    act.wait_ge(normed, i - SB + 1)
                act.activation(sp_[:, i % SB, 0:w], sp_[:, i % SB, 0:w], ACT.Exp, bias=st[:, i % SB, 0:1],
                               accum_out=st[:, i % SB, 1:2]).then_inc(probbed, 1)

            def turn(i):
                h, t = steps[i]
                w = width(t)
                act.wait_ge(turned, i + 1)
                if i >= 2:
                    act.wait_ge(mixed, i - 1)
                act.activation(pt[:, i % 2, 0:w], turned_bank(i)[:, 0:w], ACT.Copy).then_inc(turned_kept, 1)

            def keep(i):
                h, t = steps[i]
                r = HD * (h % 2)
                act.wait_ge(mixed, i + 1)
                act.activation(out[r:r + HD, h // 2, t * P:(t + 1) * P], ps[r:r + HD, mixed_bank + i % 2, 0:P], ACT.Copy)\
                    .then_inc(kept, 1)
            for i in range(len(steps) + MIX):
                if i < len(steps):
                    exps(i)
                if TURN <= i < len(steps) + TURN:
                    turn(i - TURN)
                if i >= MIX:
                    keep(i - MIX)


def stage_recurrence(core, ctx, qr, kf, kb, ff, fb, v, masks, orec, masks_src, conv):
    nc, ps = core.nc, core.ps
    qf = ctx.enter_context(nc.sbuf_tensor("rec_q_fwd", [P, RT, S], F32))
    qb = ctx.enter_context(nc.sbuf_tensor("rec_q_bwd", [P, RT, S], F32))
    tot = ctx.enter_context(nc.sbuf_tensor("rec_totals", [P, RT, 2, S], F32))
    HEAD = 10 * P
    close = ctx.enter_context(nc.sbuf_tensor("rec_close", [P, 2 * RT * HEAD + 2 * P], F32))
    own = lambda n: close[:, n * HEAD:n * HEAD + 12 * P].rearrange("p (i c) -> p i c", i=TT)[:, :, 0:P]
    near = lambda n: [close[:, n * HEAD + (1 + 6 * i) * P:n * HEAD + (3 + 6 * i) * P] for i in range(2)]
    both = lambda n, i: close[:, n * HEAD + (3 * i - i % 2) * P:n * HEAD + (3 * i - i % 2 + 2) * P]
    far = ctx.enter_context(nc.sbuf_tensor("rec_far", [P, 2, 2, S], F32))
    ks = lambda p: close[:, (2 * p + 1) * HEAD:(2 * p + 1) * HEAD + S]
    masks_wide = far[:, 0, :, :].rearrange("p a b -> p (a b)")[:, 0:len(LEVELS) * P].bitcast(I32)
    started = core.sem(ctx, "rec_started")
    multiplied = core.sem(ctx, "rec_multiplied")
    copied = core.sem(ctx, "rec_copied")
    decayed = core.sem(ctx, "rec_decayed")
    banked = core.sem(ctx, "rec_banked")
    taken = core.sem(ctx, "rec_taken")
    near_part = core.sem(ctx, "rec_near_part")
    NL = len(LEVELS)
    NB = 2 * RT * (NL + 1)
    uses = [("near", p, h, 0) for p in range(RT) for h in range(2)]
    for p in range(RT + 1):
        uses += [("far", p, h, half) for h in range(2) for half in range(2) if p < RT]
        uses += [("value", p - 1, h, 0) for h in range(2) if p >= 1]
    at_use = {u: n for n, u in enumerate(uses)}

    masks_in = core.sem(ctx, "rec_masks_loaded")
    with nc.Block() as block:
        @block.sync
        def _(sp):
            sp.dma_start(masks_wide, masks_src).then_inc(masks_in, 16)

        @block.tensor
        def _(pe):
            nb = 0
            for lv in range(NL + 1):
                for p in range(RT):
                    if lv == 0:
                        pe.wait_ge(started, p + 1)
                    if lv >= 2:
                        pe.wait_ge(decayed, 6 * ((lv - 2) * RT + p + 1))
                    for h in range(2):
                        r = h * HD
                        if nb >= 8:
                            pe.wait_ge(copied, nb - 7)
                        bank = ps[:, nb % 8, :]
                        for i in range(TT):
                            t = slice(i * P, (i + 1) * P)
                            if lv == 0:
                                ins = pe.matmul(bank[:, t], ks(p)[r:r + HD, t], qr[r:r + HD, p, t],
                                                start=True, stop=True)
                                continue
                            m = LEVELS[lv - 1]
                            tile_q = lambda a: a[r:r + HD, p, t].rearrange("k (n two m) -> k n two m", two=2, m=m)
                            pe.matmul(bank[:, i * P:i * P + P // 2], kf[r:r + HD, p, t],
                                      tile_q(qf)[:, :, 1, :], start=True, stop=True)
                            ins = pe.matmul(bank[:, i * P + P // 2:(i + 1) * P], kb[r:r + HD, p, t],
                                            tile_q(qb)[:, :, 0, :], start=True, stop=True)
                        ins.then_inc(multiplied, 1)
                        nb += 1
            for n, (what, p, h, half) in enumerate(uses):
                r = h * HD
                bank = ps[:, (NB + n) % 8, :]
                if n >= 8:
                    pe.wait_ge(taken, n - 7)
                else:
                    pe.wait_ge(copied, NB - 7 + n)
                if what == "near":
                    pe.wait_ge(decayed, 6 * ((NL - 1) * RT + p + 1))
                    for i in range(TT):
                        kk, qq = (kf, qf) if i % 2 == 0 else (kb, qb)
                        j = i ^ 1
                        ins = pe.matmul(bank[:, i * P:(i + 1) * P], kk[r:r + HD, p, i * P:(i + 1) * P],
                                        qq[r:r + HD, p, j * P:(j + 1) * P], start=True, stop=True)
                elif what == "far":
                    pe.wait_ge(decayed, 6 * NL * RT + 4 * (p + 1))
                    kk, qq = (kf, qf) if half == 0 else (kb, qb)
                    q0 = S // 2 * (1 - half)
                    for i in range(2):
                        s0 = (2 * half + i) * P
                        ins = pe.matmul(bank[:, i * 256:(i + 1) * 256], kk[r:r + HD, p, s0:s0 + P],
                                        qq[r:r + HD, p, q0:q0 + S // 2], start=True, stop=True)
                else:
                    pe.wait_ge(copied, NB)
                    pe.wait_ge(taken, at_use["far", p, h, 1] + 1)
                    head = slice((2 * p + h) * HD, (2 * p + h + 1) * HD)
                    for half in range(2):
                        to = bank[r:r + HD, half * 256:(half + 1) * 256]
                        for i in (2 * half, 2 * half + 1):
                            pe.matmul(to, v[:, i, head], both(2 * p + h, i), start=(i % 2 == 0), stop=False)
                        for i in (2 - 2 * half, 3 - 2 * half):
                            ins = pe.matmul(to, v[:, i, head], far[:, h, 1 - half, i % 2 * 256:i % 2 * 256 + 256],
                                            start=False, stop=(i % 2 == 1))
                ins.then_inc(banked, 1)

        @block.vector
        def _(dve):
            ch = Chain(dve, core.sem(ctx, "rec_chain"))
            for p in range(RT):
                ch.add(dve.tensor_tensor(ks(p), kf[:, p, :], kb[:, p, :], ALU.add))
                ch.add(dve.tensor_tensor(qf[:, p, :], qr[:, p, :], ff[:, p, :], ALU.mult))
                ch.add(dve.tensor_tensor(qb[:, p, :], qr[:, p, :], fb[:, p, :], ALU.mult))
                ch.wait()
                dve.sem_inc(started, 1)
            dve.wait_ge(masks_in, 16)
            for i in range(TT):
                ch.add(dve.tensor_copy(masks[:, :, i * P:(i + 1) * P],
                                       masks_wide.rearrange("p (a b) -> p a b", b=P)))
            ch.wait()

            def up(p, m, tf, tb):
                n = S // (2 * m)
                pairs = lambda a: a.rearrange("p (n two) -> p n two", two=2)
                wide = lambda a: a.unsqueeze(2).to_broadcast([P, n, m])
                tf, tb = pairs(tf), pairs(tb)
                for a, half, f in ((qf, 1, tf[:, :, 0]), (qb, 0, tb[:, :, 1]),
                                   (kf, 0, tf[:, :, 1]), (kb, 1, tb[:, :, 0])):
                    ap = a[:, p, :].rearrange("p (n two m) -> p n two m", two=2, m=m)[:, :, half, :]
                    dve.tensor_tensor(ap, ap, wide(f), ALU.mult).then_inc(decayed, 1)
                return tf, tb

            prev = [(ff[:, p, :], fb[:, p, :]) for p in range(RT)]
            nb, at = 0, 0
            for lv in range(NL + 1):
                n = S // 2 ** lv
                for p in range(RT):
                    if lv >= 1:
                        dve.wait_ge(multiplied, nb + 2)
                        if lv >= 2:
                            dve.wait_ge(decayed, 6 * ((lv - 2) * RT + p + 1))
                        tf, tb = up(p, LEVELS[lv - 1], *prev[p])
                        nf, nbk = tot[:, p, 0, at:at + n], tot[:, p, 1, at:at + n]
                        dve.tensor_tensor(nf, tf[:, :, 0], tf[:, :, 1], ALU.mult).then_inc(decayed, 1)
                        dve.tensor_tensor(nbk, tb[:, :, 0], tb[:, :, 1], ALU.mult).then_inc(decayed, 1)
                        prev[p] = (nf, nbk)
                    for h in range(2):
                        dve.wait_ge(multiplied, nb + 1)
                        bank = ps[:, nb % 8, :]
                        if lv == 0:
                            dve.tensor_copy(own(2 * p + h), bank.rearrange("p (i c) -> p i c", i=TT)).then_inc(copied, 1)
                        else:
                            m = LEVELS[lv - 1]
                            dve.wait_ge(copied, nb - 2 * RT + 1)
                            split = lambda a: a.rearrange("p i (n two m) -> p i n two m", two=2, m=m)
                            src = bank.rearrange("p (i two n m) -> p i two n m", i=TT, two=2, m=m)
                            for part, two in ((0, 1), (1, 0)):
                                ins = dve.copy_predicated(split(own(2 * p + h))[:, :, :, two, :],
                                                          split(masks[:, lv - 1, :].rearrange("p (i c) -> p i c", i=TT))[:, :, :, two, :],
                                                          src[:, :, part])
                            ins.then_inc(copied, 1)
                        nb += 1
                    if lv >= 1:
                        conv.steps(dve, 3)
                if lv >= 1:
                    at += n
            for p in range(RT):
                dve.wait_ge(banked, 2 * p + 2)
                dve.wait_ge(decayed, 6 * ((NL - 1) * RT + p + 1))
                up(p, P, *prev[p])

        @block.scalar
        def _(act):
            for n, (what, p, h, half) in enumerate(uses):
                act.wait_ge(banked, n + 1)
                bank = ps[:, (NB + n) % 8, :]
                if what == "near":
                    for i, to in enumerate(near(2 * p + h)):
                        ins = act.activation(to, bank[:, i * 256:(i + 1) * 256], ACT.Copy)
                        if i == 0:
                            ins.then_inc(near_part, 1)
                elif what == "far":
                    if p >= 1:
                        act.wait_ge(banked, at_use["value", p - 1, h, 0] + 1)
                    ins = act.activation(far[:, h, half, :], bank, ACT.Copy)
                else:
                    r = h * HD
                    ins = act.activation(orec[r:r + HD, p, :], bank[r:r + HD, :], ACT.Copy)
                ins.then_inc(taken, 1)


def stage_rec_norm(core, ctx, o, w, gate, out, tmp, conv_norm):
    (mean, variance), (squares, root, silu), (centre, scale) = conv_norm
    nc, ps = core.nc, core.ps
    squared = core.sem(ctx, "recn_squared")
    summed = core.sem(ctx, "recn_summed")
    rooted = core.sem(ctx, "recn_rooted")
    with nc.Block() as block:
        @block.scalar
        def _(act):
            for k in range(RT):
                act.activation(tmp[:, k, :], o[:, k, :], ACT.Square).then_inc(squared, 1)
            squares(act)
            for k in range(RT):
                act.wait_ge(summed, k + 1)
                act.activation(tmp[:, 3 + k, :], ps[:, k, :], ACT.Sqrt, bias=core.eps[:, 0:1]).then_inc(rooted, 1)
            root(act)
            silu(act)

        @block.tensor
        def _(pe):
            mean(pe)
            for k in range(RT):
                pe.wait_ge(squared, k + 1)
                pe.matmul(ps[:, k, :], core.ones[:, 2, :], tmp[:, k, :], start=True, stop=True).then_inc(summed, 1)
            variance(pe)

        @block.vector
        def _(dve):
            centre(dve)
            ch = Chain(dve, core.sem(ctx, "recn_chain"))
            for k in range(RT):
                dve.wait_ge(rooted, k + 1)
                ch.link(dve.reciprocal(tmp[:, 3 + k, :], tmp[:, 3 + k, :]))
                ch.link(dve.scalar_tensor_tensor(o[:, k, :], o[:, k, :], w[:, k:k + 1], tmp[:, 3 + k, :],
                                                 ALU.mult, ALU.mult))
                ch.add(dve.tensor_tensor(out[:, k, :], o[:, k, :], gate[:, k, :], ALU.mult))
            scale(dve)


def stage_gates(core, ctx, z_pos, z_neg, lb, one_minus, mod, vec, s2, also):
    nc = core.nc
    with nc.Block() as block:
        @block.vector
        def _(dve):
            ch = Chain(dve, core.sem(ctx, "gates_chain"))
            ch.add(dve.scalar_tensor_tensor(s2[:, :], mod[:, 32:40], 1.0, vec[:, 8:16], ALU.add, ALU.mult))
            for d in range(2):
                for k in range(RT):
                    j = d * RT + k
                    f, kk = z_pos[d][:, k, :], z_neg[d][:, k, :]
                    ch.add(dve.tensor_scalar(f, f, one_minus[:, j:j + 1], lb[:, j:j + 1], ALU.mult, ALU.add))
                    ch.add(dve.tensor_scalar(kk, kk, one_minus[:, j:j + 1], None, ALU.mult))
            ch.wait()
            for d in range(2):
                ch.add(dve.tensor_scalar(z_pos[d][:, :, :], z_pos[d][:, :, :], 1e-30, None, ALU.max))
            also(dve)


def stage_small_1(core, ctx, l_is_one, vec, mod, s1, lb, one_minus):
    nc = core.nc
    diff = core.sem(ctx, "bounds_difference")
    sig = core.sem(ctx, "bounds_sigmoid")
    with nc.Block() as block:
        @block.vector
        def _(dve):
            ch = Chain(dve, core.sem(ctx, "small1_chain"))
            dve.tensor_tensor(lb[:, :], vec[:, 28:34], vec[:, 22:28], ALU.subtract).then_inc(diff, 1)
            ch.add(dve.scalar_tensor_tensor(s1[:, :], mod[:, 8:16], 1.0, vec[:, 0:8], ALU.add, ALU.mult))
            dve.wait_ge(sig, 1)
            ch.link(dve.tensor_scalar(lb[:, :], lb[:, :], l_is_one, None, ALU.mult))
            ch.add(dve.tensor_scalar(one_minus[:, :], lb[:, :], -1.0, 1.0, ALU.mult, ALU.add))

        @block.scalar
        def _(act):
            act.wait_ge(diff, 1)
            act.activation(lb[:, :], lb[:, :], ACT.Sigmoid).then_inc(sig, 1)


def stack_one(core, nc, args):
    with ExitStack() as ctx:
        sb = lambda name, shape, dt=F32: ctx.enter_context(nc.sbuf_tensor(name, shape, dt))
        silu_c = sb("silu_c", [P, KT])
        layer_no = sb("layer_no", [P, 1])
        vec = sb("vec1", [P, 37])
        b_ada = sb("b_ada_cols", [P, 6 * KT])
        mod = sb("mod", [P, 6 * KT])
        ctaps = sb("conv_a_taps", [P, 2 * CONV_W])
        ftaps = sb("conv_f_taps", [P, 3 * 2 * FT])
        s1, s2 = sb("scale1", [P, KT]), sb("scale2", [P, KT])
        lb, om = sb("lower_bound", [P, 2 * RT]), sb("one_minus_lb", [P, 2 * RT])

        with ExitStack() as c2:
            cols_c = c2.enter_context(nc.sbuf_tensor("c_cols", [P, KT], F32))
            first_sem = len(core.sems)
            stage_columns(core, c2, "c", [(args["c"].rearrange("o (n p) -> (o n) p", p=P), KT)], (cols_c,))
            got = core.sem(c2, "silu_c_ready")
            with nc.Block() as block:
                @block.scalar
                def _(act):
                    act.activation(silu_c[:, :], cols_c[:, :], ACT.Silu).then_inc(got, 1)

                @block.vector
                def _(dve):
                    dve.memset(layer_no[:, :], 0.0).then_inc(got, 1)
            core.clear(core.sems[first_sem:])
            del core.sems[first_sem:]

        with nc.Fori(0, DEPTH) as l:
          with ExitStack() as lc:
            first_sem = len(core.sems)
            ring = Ring(core, lc, "ring1")
            w_in, w_out = args["w_in"], args["w_out"]
            plan = [(0, 256, "T"), (256, 256, "T")] + [(512 + 256 * i, 256, "T") for i in range(3)]
            plan += [(1280, 192, "tok"), (1472, 192, "tok")] + [(1664 + 256 * i, 256, "T") for i in range(4)]
            plan += [(2688, 128, "T"), (2816, 192, "tok"), (3008, 192, "tok"), (3200, 256, "T"), (3456, 128, "T")]
            in0 = ring.plan([(cols(w_in, l, c, n), KT, n) for c, n, _ in plan])
            out0 = ring.plan([(cols(w_out, l, 256 * i, 256), KT, 256) for i in range(4)])

            rows = lambda a, n: (a[bass.ds(l, 1), :].rearrange("o (n p) -> (o n) p", p=P), n)
            with ExitStack() as c2:
                stage_columns(core, c2, "vec1", [
                    rows(args["norm1_w"], 8), rows(args["norm2_w"], 8), rows(args["conv_a_b"], 2),
                    rows(args["ln_a_w"], 2), rows(args["ln_a_b"], 2),
                    (args["lb_gamma"].rearrange("d e (n p) -> (d e n) p", p=P), 12), rows(args["rec_norm_w"], 3),
                    rows(args["b_ada"], 48)], (vec, b_ada))
            with ExitStack() as mx:
                msb = lambda name, shape, dt=F32: mx.enter_context(nc.sbuf_tensor(name, shape, dt))
                orec = msb("rec_out", [P, RT, S])
                g_rec = msb("g_rec", [P, RT, S])
                mixed = msb("mixed", [P, KT, S])
                acc = msb("mod_partial", [P, 2, 2 * P])
                with ExitStack() as c2:
                    stage_columns(core, c2, "taps1", [(args["conv_a_w"][bass.ds(l, 1), :, :]
                                  .rearrange("o w (n p) -> (o w n) p", p=P), 2 * CONV_W)] +
                                  [(args["conv_f_w"][bass.ds(l, 1), w:w + 1, :]
                                    .rearrange("o w (n p) -> (o w n) p", p=P), 2 * FT) for w in range(3)], (ctaps, ftaps),
                                  ring, ModJob(core, lc, "mod_a", args["w_ada"], l, 0, 8, mixed[:, :, :], acc, silu_c,
                                               b_ada, mod))
                rx = ExitStack()
                rsb = lambda name, shape, dt=F32: rx.enter_context(nc.sbuf_tensor(name, shape, dt))
                qr, i_rec = rsb("q_rec", [P, RT, S]), rsb("i_rec", [P, TT, REC_W])
                ff, fb = rsb("f_fwd", [P, RT, S]), rsb("f_bwd", [P, RT, S])
                kf, kb = rsb("k_fwd", [P, RT, S]), rsb("k_bwd", [P, RT, S])
                pad = rsb("conv_pad", [P, CONV_CH // P, S + CONV_W - 1])
                ax = ExitStack()
                asb = lambda name, shape, dt=F32: ax.enter_context(nc.sbuf_tensor(name, shape, dt))
                q, k = asb("q_att", [P, 3, S]), asb("k_att", [P, 3, S])
                v = asb("v_att", [P, TT, ATT_W])
                a, gate = asb("a_val", [P, 2, S]), asb("a_gate", [P, 2, S])
                with ExitStack() as hx:
                    hi, lo = (hx.enter_context(nc.sbuf_tensor(f"h1_{n}", [P, KT, S], F32R)) for n in ("hi", "lo"))
                    stage_small_1(core, lc, layer_no[:, 0:1], vec, mod, s1, lb, om)
                    rms1 = RmsNorm(core, lc, "rms1", s1, mod[:, 0:8], orec, hi, lo)
                    rms1.stage(ring)
                    z_kept = core.sem(lc, "z_gates_kept")

                    def into(tiles):
                        def put(act, view, j):
                            dst, n, f = tiles[j]
                            if f is None:
                                act.activation(dst[0][:, n, :], view, ACT.Sigmoid).then_inc(z_kept, 1)
                                return act.activation(dst[1][:, n, :], view, ACT.Sigmoid, scale=-1.0)
                            return act.activation(dst[:, n, :], view, f)
                        return put
                    order = [(a, 0, ACT.Copy), (a, 1, ACT.Copy), (gate, 0, ACT.Sigmoid), (gate, 1, ACT.Sigmoid)]
                    order += [(q, n, ACT.Copy) for n in range(3)] + [(k, n, ACT.Copy) for n in range(3)]
                    order += [None] * 3 + [(qr, n, ACT.Silu) for n in range(3)]
                    order += [((ff, kf), n, None) for n in range(3)] + [((fb, kb), n, None) for n in range(3)]
                    order += [None] * 3 + [(g_rec, n, ACT.Silu) for n in range(3)]
                    tok = {5: (v, 0), 6: (v, 192), 12: (i_rec, 0), 13: (i_rec, 192)}
                    jobs = []
                    for i, (c, n, kind) in enumerate(plan):
                        if kind == "tok":
                            dst, c0 = tok[i]
                            put = lambda act, view, j, dst=dst, c0=c0: \
                                act.activation(dst[:, j, c0:c0 + 192], view, ACT.Copy)
                        else:
                            put = into(order[c // P:(c + n) // P])
                        jobs.append((in0 + i, kind, put, (hi, lo)))
                    stage_project(core, lc, "in1", ring, jobs, feed=rms1,
                                  mod=ModJob(core, lc, "mod_b", args["w_ada"], l, 8, 16, mixed[:, :, :], acc,
                                             silu_c, b_ada, mod))
                conv = ConvJob(core, lc, pad, mixed[:, 0:2, :], ctaps, vec[:, 16:18])
                counted = core.sem(lc, "layer_counted")

                def also(dve):
                    dve.tensor_scalar(layer_no[:, :], layer_no[:, :], 1.0, None, ALU.add).then_inc(counted, 1)
                    conv.start(dve, a, gate)
                stage_gates(core, lc, (ff, fb), (kf, kb), lb, om, mod, vec, s2, also)
                slopes = [2.0 ** (-8.0 * (h + 1) / N_HEADS_1) for h in range(N_HEADS_1)]
                with ax, ExitStack() as c2:
                    dist_ln = c2.enter_context(nc.sbuf_tensor("attn_tables", [P, 2, TABLE], F32))
                    tab = c2.enter_context(nc.sbuf_tensor("attn_bias", [P, 2, TABLE], F32))
                    tab_in = core.sem(lc, "attn_tables_loaded")

                    def prepare(dve, ch, h):
                        if h == 0:
                            dve.wait_ge(tab_in, 16)
                        ch.link(dve.scalar_tensor_tensor(tab[:, h % 2, :], dist_ln[:, 0, :], -slopes[h],
                                                         dist_ln[:, 1, :], ALU.mult, ALU.add))
                    stage_attention(core, c2, "att1", N_HEADS_1, q, k, v, mixed[:, 2:5, :], lambda t: S,
                                    lambda h, t: tab[:, h % 2, 3 * P - t * P:3 * P - t * P + S], prepare,
                                    lambda sp: sp.dma_start(dist_ln[:, :, :].rearrange("p a b -> p (a b)"),
                                                            args["const_attn"]).then_inc(tab_in, 16))
                with rx, ExitStack() as c2:
                    masks = c2.enter_context(nc.sbuf_tensor("rec_masks", [P, len(LEVELS), S], U8))
                    stage_recurrence(core, c2, qr, kf, kb, ff, fb, i_rec, masks, orec, args["const_mask"], conv)
                hi, lo = (msb(f"mixed_{n}", [P, KT, S], F32R) for n in ("hi", "lo"))
                with ExitStack() as c2:
                    scratch = c2.enter_context(nc.sbuf_tensor("rec_norm_scratch", [P, 12, S], F32))
                    stage_rec_norm(core, lc, orec, vec[:, 34:37], g_rec, mixed[:, 5:8, :], scratch,
                                   conv.norm(scratch[:, 6:12, :], 4, vec[:, 18:20], vec[:, 20:22]))
                split = Split(core, lc, "mixed", mixed, hi, lo, KT)

                def put1(dve, view, n):
                    return dve.scalar_tensor_tensor(core.x[:, n, :], view, mod[:, 16 + n:17 + n], core.x[:, n, :],
                                                    ALU.mult, ALU.add)
                ffn = FfnStart(core, lc, "ffn1", l, args["w_up"])
                stage_project(core, lc, "out1", ring,
                              [(out0 + i, "T", (lambda dve, view, j, i=i: put1(dve, view, 2 * i + j)), (hi, lo))
                               for i in range(4)], carrier="vector", ahead=ffn, feed=split)
            with ExitStack() as c2:
                hi, lo = (c2.enter_context(nc.sbuf_tensor(f"h2_{n}", [P, KT, S], F32R)) for n in ("hi", "lo"))
                bufs = ffn_buffers(nc, c2, "one")
                rms2 = RmsNorm(core, lc, "rms2", s2, mod[:, 24:32], bufs["c"], hi, lo)
                rms2.stage(ffn)

                def put(dve, n, view):
                    xn = core.x[:, bass.ds(n, 1), :]
                    return dve.scalar_tensor_tensor(xn, view, mod[:, bass.ds(n + 40, 1)], xn, ALU.mult, ALU.add)
                stage_ffn(core, lc, "ffn1", l, ffn, args["w_down"], ftaps, None, 1, ACT.Gelu, put,
                          bufs, (hi, lo), rms2)
            core.clear(core.sems[first_sem:])
            del core.sems[first_sem:]

        with ExitStack() as c2:
            first_sem = len(core.sems)
            fin = c2.enter_context(nc.sbuf_tensor("final_norm_cols", [P, KT], F32))
            stage_columns(core, c2, "fin", [(args["final_norm_w"].rearrange("(n p) -> n p", p=P), KT)], (fin,))
            tmp = c2.enter_context(nc.sbuf_tensor("rms3_tmp", [P, 3, S], F32))
            RmsNorm(core, c2, "rms3", fin, None, tmp).stage()
            core.clear(core.sems[first_sem:])
            del core.sems[first_sem:]


def ffn_buffers(nc, ctx, which):
    sb = lambda name, shape, dt=F32: ctx.enter_context(nc.sbuf_tensor(f"{name}_{which}", shape, dt))
    return {"gh": sb("hidden_hi", [P, FT, S], F32R), "gl": sb("hidden_lo", [P, FT, S], F32R),
            "u": sb("u_padded", [P, 4, S + 2]), "c": sb("u_convolved", [P, 4, S])}


def stage_layernorm(core, ctx, name, src, out, groups, avg, w, b, tmp, gate=None, ahead=None):
    nc, ps = core.nc, core.ps
    meaned = core.sem(ctx, f"{name}_mean")
    centred = core.sem(ctx, f"{name}_centred")
    squared = core.sem(ctx, f"{name}_squared")
    varied = core.sem(ctx, f"{name}_variance")
    rooted = core.sem(ctx, f"{name}_rooted")
    inverted = core.sem(ctx, f"{name}_inverted")
    normed = core.sem(ctx, f"{name}_normed")
    shifted = core.sem(ctx, f"{name}_shifted")
    flat = [(g, k, k == tiles[0], k == tiles[-1]) for g, tiles in enumerate(groups) for k in tiles]
    with nc.Block() as block:
        @block.tensor
        def _(pe):
            for g, k, first, last in flat:
                pe.matmul(ps[:, g, :], core.ones[:, avg, :], src[:, k, :], start=first, stop=last)\
                    .then_inc(meaned, 1)
            for i, (g, k, first, last) in enumerate(flat):
                pe.wait_ge(squared, i + 1)
                pe.matmul(ps[:, 4 + g, :], core.ones[:, avg, :], tmp[:, i % 2, :], start=first, stop=last)\
                    .then_inc(varied, 1)

        @block.vector
        def _(dve):
            for i, (g, k, first, last) in enumerate(flat):
                dve.wait_ge(meaned, (g + 1) * len(groups[0]))
                dve.tensor_tensor(src[:, k, :], src[:, k, :], ps[:, g, :], ALU.subtract).then_inc(centred, 1)
            for g in range(len(groups)):
                dve.wait_ge(rooted, g + 1)
                dve.reciprocal(tmp[:, 2 + g, :], tmp[:, 2 + g, :]).then_inc(inverted, 1)
            for i, (g, k, first, last) in enumerate(flat):
                dve.wait_ge(inverted, g + 1)
                dve.wait_ge(squared, i + 1)
                dve.scalar_tensor_tensor(out[:, k, :], src[:, k, :], w[:, k:k + 1], tmp[:, 2 + g, :],
                                         ALU.mult, ALU.mult).then_inc(normed, 1)
            if gate is not None:
                for i, (g, k, first, last) in enumerate(flat):
                    dve.wait_ge(normed, i + 1)
                    dve.tensor_tensor(out[:, k, :], out[:, k, :], gate[:, k, :], ALU.mult).then_inc(shifted, 1)
            if ahead is not None:
                ahead.split_low(dve)

        @block.scalar
        def _(act):
            for i, (g, k, first, last) in enumerate(flat):
                act.wait_ge(centred, i + 1)
                if i >= 2:
                    act.wait_ge(varied, i - 1)
                act.activation(tmp[:, i % 2, :], src[:, k, :], ACT.Square).then_inc(squared, 1)
            for g in range(len(groups)):
                act.wait_ge(varied, (g + 1) * len(groups[0]))
                act.activation(tmp[:, 2 + g, :], ps[:, 4 + g, :], ACT.Sqrt, bias=core.eps[:, 1:2])\
                    .then_inc(rooted, 1)
            if b is not None:
                for i, (g, k, first, last) in enumerate(flat):
                    act.wait_ge(normed, i + 1)
                    act.activation(out[:, k, :], out[:, k, :], ACT.Identity, bias=b[:, k:k + 1])\
                        .then_inc(shifted, 1)
            if ahead is not None:
                ahead.split_high(act)


def stage_angles(core, ctx, positions, cos, sin, pos_i, w, ahead):
    nc = core.nc
    loaded = core.sem(ctx, "positions_loaded")
    reduced = core.sem(ctx, "angle_reduced")
    absed = core.sem(ctx, "angle_abs")
    done = core.sem(ctx, "angle_done")
    C1 = 6.28125
    C2 = float(np.float32(np.floor((2 * np.pi - C1) * 2.0 ** 21) / 2.0 ** 21))
    C3 = float(2 * np.pi - C1 - C2)
    ROUND = 12582912.0
    with nc.Block() as block:
        @block.sync
        def _(sp):
            sp.dma_start(pos_i, positions.partition_broadcast(P)).then_inc(loaded, 16)
            ahead.load_more(sp)

        @block.vector
        def _(dve):
            ch = Chain(dve, core.sem(ctx, "angle_chain"))
            ahead.split_low(dve)
            dve.wait_ge(loaded, 16)
            ch.link(dve.tensor_copy(w[:, 0, :], pos_i))
            ch.link(dve.tensor_scalar(w[:, 1, :], w[:, 0, :], core.eps[:, 4:5], None, ALU.mult))
            ch.link(dve.tensor_scalar(w[:, 2, :], w[:, 1, :], 1.0 / (2 * np.pi), None, ALU.mult))
            ch.link(dve.tensor_scalar(w[:, 2, :], w[:, 2, :], ROUND, None, ALU.add))
            ch.link(dve.tensor_scalar(w[:, 2, :], w[:, 2, :], ROUND, None, ALU.subtract))
            for c in (C1, C2, C3):
                ch.link(dve.scalar_tensor_tensor(w[:, 1, :], w[:, 2, :], -c, w[:, 1, :], ALU.mult, ALU.add))
            dve.tensor_scalar(w[:, 1, :], w[:, 1, :], 3.1415925, -3.1415925, ALU.min, ALU.max).then_inc(reduced, 1)

        @block.scalar
        def _(act):
            ahead.split_high(act)
            act.wait_ge(reduced, 1)
            act.activation(w[:, 3, :], w[:, 1, :], ACT.Abs).then_inc(absed, 1)
            act.activation(sin[:, :], w[:, 1, :], ACT.Sin).then_inc(done, 1)
            act.wait_ge(absed, 1)
            act.activation(cos[:, :], w[:, 3, :], ACT.Sin, bias=core.eps[:, 5:6], scale=-1.0).then_inc(done, 1)


class Rope:

    def __init__(self, core, ctx, steps, ik_raw, ik, cos, sin, tmp):
        self.core, self.steps, self.ik_raw, self.ik = core, steps, ik_raw, ik
        self.cos, self.sin, self.tmp = cos, sin, tmp
        self.rotated = core.sem(ctx, "rope_rotated")
        self.multiplied = core.sem(ctx, "rope_multiplied")
        self.turned = core.sem(ctx, "rope_turned")
        self.first = [sum(len(t) for t in steps[:u]) for u in range(len(steps))]

    def tensor(self, pe, u, projection):
        if u < 1 or not self.steps[u - 1]:
            return
        ps, ones = self.core.ps, self.core.ones
        tiles, b0 = projection.units[u - 1][-2:]
        pe.wait_ge(projection.free, b0 + tiles)
        for n, x in enumerate(self.steps[u - 1], self.first[u - 1]):
            if n >= 2:
                pe.wait_ge(self.turned, n - 1)
            rot = ps[:, 5 + n % 2, :]
            if isinstance(x, str):
                pe.matmul(ps[:, 7, :], ones[0:HD, 4, :], self.ik_raw, start=True, stop=True)
                ins = pe.matmul(rot, ones[0:HD, 5, :], self.ik_raw, start=True, stop=True)
            else:
                ins = pe.matmul(rot, ones[:, 3, :], x, start=True, stop=True)
            ins.then_inc(self.rotated, 1)

    def vector(self, dve, u):
        if u < 1:
            return
        for n, x in enumerate(self.steps[u - 1], self.first[u - 1]):
            dve.wait_ge(self.rotated, n + 1)
            raw, out = (self.core.ps[:, 7, :], self.ik) if isinstance(x, str) else (x, x)
            t1, t2 = self.tmp[:, 2 * (n % 2), :], self.tmp[:, 2 * (n % 2) + 1, :]
            if n >= 2:
                dve.wait_ge(self.turned, n - 1)
            dve.tensor_tensor(t1, raw, self.cos, ALU.mult).then_inc(self.multiplied, 1)
            dve.tensor_tensor(t2, self.core.ps[:, 5 + n % 2, :], self.sin, ALU.mult).then_inc(self.multiplied, 1)
            dve.wait_ge(self.multiplied, 2 * n + 2)
            dve.tensor_tensor(out, t1, t2, ALU.add).then_inc(self.turned, 1)


NEG = -3.0e38


def stage_select(core, ctx, iq, ik, iw, bias, rl, sc, wk, beside, units):
    nc, ps = core.nc, core.ps
    m8 = ctx.enter_context(nc.sbuf_tensor("sel_max8", [P, 8], F32))
    cn = ctx.enter_context(nc.sbuf_tensor("sel_counts", [P, 2], F32))
    dotted = core.sem(ctx, "sel_dotted")
    relued = core.sem(ctx, "sel_relued")
    summed = core.sem(ctx, "sel_summed")
    steps = [(t, h) for t in range(1, TT) for h in range(N_HEADS_2)]
    with nc.Block() as block:
        block.sync(beside.sync)

        @block.tensor
        def _(pe):
            for i, (t, h) in enumerate(steps):
                w, r = P * (t + 1), HD * (h % 2)
                if i >= 4:
                    pe.wait_ge(relued, i - 3)
                pe.matmul(ps[:, i % 4, 0:w], iq[r:r + HD, h // 2, t * P:(t + 1) * P], ik[r:r + HD, 0:w],
                          start=True, stop=True).then_inc(dotted, 1)
                if h == N_HEADS_2 - 1:
                    beside.tensor(pe, units[t - 1])

        @block.scalar
        def _(act):
            beside.ring.high_to(act, beside.first + NSLOT)
            for i, (t, h) in enumerate(steps):
                w = P * (t + 1)
                act.wait_ge(dotted, i + 1)
                if i >= 4:
                    act.wait_ge(summed, i - 3)
                act.activation(rl[:, i % 4, 0:w], ps[:, i % 4, 0:w], ACT.Relu, scale=HD ** -0.5).then_inc(relued, 1)
                if h == N_HEADS_2 - 1:
                    beside.scalar(act, units[t - 1])

        @block.vector
        def _(dve):
            ch = Chain(dve, core.sem(ctx, "sel_chain"))
            beside.ring.low_to(dve, beside.first + NSLOT)
            ch.link(dve.memset(bias[:, 0, 0:P], 0.0))
            ch.add(dve.memset(bias[0:HD, 0, HD:P], -BIG))
            for i, (t, h) in enumerate(steps):
                w = P * (t + 1)
                acc = sc[:, t % 2, 0:w]
                dve.wait_ge(relued, i + 1)
                if h == 0:
                    dve.tensor_scalar(acc, rl[:, i % 4, 0:w], iw[:, t, h:h + 1], None, ALU.mult).then_inc(summed, 1)
                else:
                    dve.wait_ge(summed, i)
                    dve.scalar_tensor_tensor(acc, rl[:, i % 4, 0:w], iw[:, t, h:h + 1], acc, ALU.mult, ALU.add)\
                        .then_inc(summed, 1)
                if h < N_HEADS_2 - 1:
                    continue
                dve.wait_ge(summed, i + 1)
                ch.link(dve.memset(sc[0:HD, t % 2, w - CHUNK:w], NEG))
                work = wk[:, 0, 0:w]
                for r in range(TOPK // 8):
                    src = acc if r == 0 else work
                    ch.link(dve.max(m8[:, :], src))
                    if r < TOPK // 8 - 1:
                        ch.link(dve.match_replace(work, m8[:, :], src, NEG))
                    done, due = (units[t - 2] if t >= 2 else 0), units[t - 1]
                    beside.vector(dve, done + (due - done) * (r + 1) // (TOPK // 8))
                least = m8[:, 7:8]
                above, equal = wk[:, 0, 0:w], wk[:, 1, 0:w]
                ch.add(dve.tensor_scalar(equal, acc, least, None, ALU.is_equal))
                ch.link(dve.tensor_scalar(above, acc, least, 0.0, ALU.is_gt, ALU.add, accum_out=cn[:, 0:1]))
                ch.link(dve.tensor_scalar(cn[:, 1:2], cn[:, 0:1], -1.0, float(TOPK), ALU.mult, ALU.add))
                ch.link(dve.tensor_tensor_scan(wk[:, 2, 0:w], equal, equal, 0.0, ALU.add, ALU.max))
                ch.link(dve.scalar_tensor_tensor(equal, wk[:, 2, 0:w], cn[:, 1:2], equal, ALU.is_le, ALU.mult))
                ch.link(dve.tensor_tensor(above, above, equal, ALU.add))
                ch.link(dve.tensor_scalar(bias[:, t, 0:w], above, BIG, -BIG, ALU.mult, ALU.add))


def stage_gla_gates(core, ctx, glr, wg, wg_src, b, gk, la, etot, tmp, beside):
    nc, ps = core.nc, core.ps
    loaded = core.sem(ctx, "gla_w_loaded")
    full = core.sem(ctx, "gla_logits")
    logs = core.sem(ctx, "gla_log")
    steps = core.sem(ctx, "gla_act_chain")
    summed = core.sem(ctx, "gla_centred")
    decay = core.sem(ctx, "gla_decay")
    mask = tmp[:, 7, :]
    with nc.Block() as block:
        @block.sync
        def _(sp):
            sp.dma_start(wg[:, :], wg_src).then_inc(loaded, 16)
            beside.sync(sp)

        @block.tensor
        def _(pe):
            pe.wait_ge(loaded, 16)
            for h in range(GLA_H):
                pe.matmul(ps[:, h, :], wg[:, h * P:(h + 1) * P], glr[0:GLA_RANK, 0, :], start=True, stop=True)\
                    .then_inc(full, 1)
            beside.tensor(pe)

        @block.scalar
        def _(act):
            ch = Chain(act, steps)
            ring = beside.ring
            ring.high_to(act, beside.first + NSLOT)
            for h in range(GLA_H):
                act.wait_ge(full, h + 1)
                ch.link(act.activation(tmp[:, 2 + h, :], ps[:, h, :], ACT.Identity, bias=b[:, h:h + 1]))
                ch.link(act.activation(tmp[:, h % 2, :], tmp[:, 2 + h, :], ACT.Abs))
                ch.link(act.activation(tmp[:, h % 2, :], tmp[:, h % 2, :], ACT.Exp, scale=-1.0))
                act.activation(la[:, h, :], tmp[:, h % 2, :], ACT.Ln, bias=core.eps[:, 2:3]).then_inc(logs, 1)
            for h in range(GLA_H):
                act.wait_ge(summed, h + 1)
                act.activation(tmp[:, 2 + h, :], tmp[:, 2 + h, :], ACT.Exp, scale=-1.0 / GLA_TAU).then_inc(decay, 1)
                act.activation(etot[:, h, :], la[:, h, CHUNK - 1:S:CHUNK], ACT.Exp, scale=1.0 / GLA_TAU)\
                    .then_inc(decay, 1)
            beside.scalar(act)

        @block.vector
        def _(dve):
            ch = Chain(dve, core.sem(ctx, "gla_dve_chain"))
            beside.ring.low_to(dve, beside.first + NSLOT)
            ch.link(dve.memset(mask, 1.0))
            ch.add(dve.memset(mask.rearrange("p (n c) -> p n c", c=CHUNK)[:, :, 0:1], 0.0))
            for h in range(GLA_H):
                dve.wait_ge(logs, h + 1)
                ch.link(dve.tensor_scalar(tmp[:, 2 + h, :], tmp[:, 2 + h, :], 0.0, None, ALU.min))
                ch.link(dve.tensor_tensor(tmp[:, 6, :], tmp[:, 2 + h, :], la[:, h, :], ALU.subtract))
                ch.link(dve.tensor_tensor_scan(la[:, h, :], mask, tmp[:, 6, :], 0.0, ALU.mult, ALU.add))
                blk = lambda a: a.rearrange("p (n c) -> p n c", c=CHUNK)
                dve.tensor_tensor(blk(tmp[:, 2 + h, :]), blk(la[:, h, :]),
                                  blk(la[:, h, :])[:, :, CHUNK - 1:CHUNK].to_broadcast([P, NCH, CHUNK]),
                                  ALU.subtract).then_inc(summed, 1)
            for h in range(GLA_H):
                dve.wait_ge(decay, 2 * h + 2)
                ch.add(dve.tensor_tensor(gk[:, h, :], gk[:, h, :], tmp[:, 2 + h, :], ALU.mult))
            beside.vector(dve)


def stage_gla(core, ctx, gq, gk, gv, etot, out):
    nc, ps = core.nc, core.ps
    kt = ctx.enter_context(nc.sbuf_tensor("gla_k_tokens", [P, 2, S], F32))
    st = ctx.enter_context(nc.sbuf_tensor("gla_states", [P, 2, NCH, GLA_DV], F32))
    turned = core.sem(ctx, "gla_turned")
    turned_kept = core.sem(ctx, "gla_turned_kept")
    outer = core.sem(ctx, "gla_outer_products")
    stated = core.sem(ctx, "gla_stated")
    read = core.sem(ctx, "gla_read")
    kept = core.sem(ctx, "gla_kept")
    with nc.Block() as block:
        @block.tensor
        def _(pe):
            def turn(h):
                if h >= 2:
                    pe.wait_ge(turned_kept, h - 1)
                for t in range(TT):
                    ins = pe.transpose(ps[:, h % 2, t * P:(t + 1) * P], gk[:, h, t * P:(t + 1) * P], core.ident[:, :])
                ins.then_inc(turned, 1)

            def product(n):
                h, c = divmod(n, NCH)
                if c == 0:
                    pe.wait_ge(turned_kept, h + 1)
                if n >= 2:
                    pe.wait_ge(stated, n - 1)
                r, t = CHUNK * (c % 2), c // 2
                pe.matmul(ps[:, 2 + n % 2, 0:GLA_DV], kt[r:r + CHUNK, h % 2, t * P:(t + 1) * P],
                          gv[r:r + CHUNK, t, h * GLA_DV:(h + 1) * GLA_DV], start=True, stop=True).then_inc(outer, 1)

            def query(n):
                h, c = divmod(n, NCH)
                if c == 0 and h >= 2:
                    pe.wait_ge(kept, 2 * (h - 1))
                pe.wait_ge(stated, n + 1)
                for half in range(2):
                    ins = pe.matmul(ps[:, 4 + 2 * (h % 2) + half, c * CHUNK:(c + 1) * CHUNK],
                                    st[:, h % 2, c, half * P:(half + 1) * P], gq[:, h, c * CHUNK:(c + 1) * CHUNK],
                                    start=True, stop=True)
                ins.then_inc(read, 1)
            turn(0)
            for n in range(GLA_H * NCH + 1):
                if n < GLA_H * NCH:
                    if n % NCH == 4 and n // NCH + 1 < GLA_H:
                        turn(n // NCH + 1)
                    product(n)
                if n >= 1:
                    query(n - 1)

        @block.vector
        def _(dve):
            for n in range(GLA_H * NCH):
                h, c = divmod(n, NCH)
                dve.wait_ge(outer, n + 1)
                if h >= 2 and c == 0:
                    dve.wait_ge(read, NCH * (h - 1))
                if c == 0:
                    dve.tensor_copy(st[:, h % 2, c, :], ps[:, 2 + n % 2, 0:GLA_DV]).then_inc(stated, 1)
                else:
                    dve.wait_ge(stated, n)
                    dve.scalar_tensor_tensor(st[:, h % 2, c, :], st[:, h % 2, c - 1, :], etot[:, h, c:c + 1],
                                             ps[:, 2 + n % 2, 0:GLA_DV], ALU.mult, ALU.add).then_inc(stated, 1)

        @block.scalar
        def _(act):
            def keep_turned(h):
                act.wait_ge(turned, h + 1)
                if h >= 2:
                    act.wait_ge(outer, NCH * (h - 1))
                act.activation(kt[:, h % 2, :], ps[:, h % 2, :], ACT.Copy).then_inc(turned_kept, 1)
            keep_turned(0)
            for h in range(GLA_H):
                if h + 1 < GLA_H:
                    keep_turned(h + 1)
                act.wait_ge(read, NCH * (h + 1))
                for half in range(2):
                    act.activation(out[:, 2 * h + half, :], ps[:, 4 + 2 * (h % 2) + half, :], ACT.Copy,
                                   scale=GLA_DK ** -0.5).then_inc(kept, 1)


def stage_merge(core, ctx, ring, first, x, att, gla, out, split_att, split_gla):
    nc, ps = core.nc, core.ps
    sg = ctx.enter_context(nc.sbuf_tensor("merge_gates", [P, 4, S], F32))
    tm = ctx.enter_context(nc.sbuf_tensor("merge_part", [P, 2, S], F32))
    base = ring.tiles
    for u in range(16):
        ring.uses(first + u, 2)
    gated = core.sem(ctx, "merge_gated")
    half1 = core.sem(ctx, "merge_products")
    merged = core.sem(ctx, "merge_merged")
    srcs = [(x, KT), (att, ATT_W2 // P), (x, KT), (gla, KT)]
    with nc.Block() as block:
        @block.sync
        def _(sp):
            ring.load_to(sp, first + 16 + 2 * NSLOT)

        @block.tensor
        def _(pe):
            for n in range(4):
                for part, ((hi, lo), kt) in enumerate(srcs):
                    u = first + 4 * n + part
                    ring.arrived(pe, u)
                    if n >= 1:
                        pe.wait_ge(half1 if part % 2 else gated, 4 * (n - 1) + part // 2 * 2 + 2)
                    for j in range(2):
                        for k in range(kt):
                            if n == 0 and j == 0 and part % 2 == 1:
                                pe.wait_ge((split_att if part == 1 else split_gla).low_done, k + 1)
                            ins = products(pe, ps[:, 2 * part + j, :], ring.hi(u)[:, k, j * P:(j + 1) * P],
                                           ring.lo(u)[:, k, j * P:(j + 1) * P], hi[:, k, :], lo[:, k, :],
                                           k == 0, k == kt - 1)
                        ins.then_inc(ring.full, 1)

        @block.scalar
        def _(act):
            ring.high_to(act, first + NSLOT)
            split_att.high(act)
            split_gla.high(act)
            for n in range(4):
                for g in range(2):
                    for j in range(2):
                        act.wait_ge(ring.full, base + 8 * n + 4 * g + j + 1)
                        if n >= 1:
                            act.wait_ge(half1, 4 * (n - 1) + 2 * g + j + 1)
                        act.activation(sg[:, 2 * g + j, :], ps[:, 4 * g + j, :], ACT.Sigmoid).then_inc(gated, 1)
                    ring.high_to(act, first + 4 * n + 2 * g + 4)
            ring.high_to(act, first + 16 + NSLOT)

        @block.vector
        def _(dve):
            ring.low_to(dve, first + NSLOT)
            split_att.low(dve)
            split_gla.low(dve)
            dve.wait_ge(split_gla.low_done, KT)
            ring.low_to(dve, first + NSLOT + 1)
            for n in range(4):
                for g in range(2):
                    for j in range(2):
                        dve.wait_ge(ring.full, base + 8 * n + 4 * g + 2 + j + 1)
                        dve.wait_ge(gated, 4 * n + 2 * g + j + 1)
                        if g == 1 and n >= 1:
                            dve.wait_ge(merged, 2 * (n - 1) + j + 1)
                        dst = out[:, 2 * n + j, :] if g == 0 else tm[:, j, :]
                        dve.tensor_tensor(dst, ps[:, 4 * g + 2 + j, :], sg[:, 2 * g + j, :], ALU.mult)\
                            .then_inc(half1, 1)
                    ring.low_to(dve, first + min(4 * n + 2 * g + 5, 16 + NSLOT))
                for j in range(2):
                    dve.wait_ge(half1, 4 * n + 2 + j + 1)
                    dve.tensor_tensor(out[:, 2 * n + j, :], out[:, 2 * n + j, :], tm[:, j, :], ALU.add)\
                        .then_inc(merged, 1)
            ring.low_to(dve, first + 16 + NSLOT)


def stack_two(core, nc, args):
    with ExitStack() as ctx:
        sb = lambda name, shape, dt=F32: ctx.enter_context(nc.sbuf_tensor(name, shape, dt))
        vec = sb("vec2", [P, 52])
        fbias = sb("conv_2_bias", [P, 2 * FT])
        ftaps = sb("conv_2_taps", [P, 3 * 2 * FT])
        x = core.x

        with nc.Fori(0, DEPTH) as l:
          with ExitStack() as lc:
            first_sem = len(core.sems)
            ring = Ring(core, lc, "ring2")
            w_in = args["w_in_2"]
            at = dict(zip(("aq", "ak", "av", "iq", "ik", "iw", "gq", "gk", "gv", "glr", "g_r", "ga", "gb", "end"),
                          np.cumsum([0, 512, 512, 512, 512, 64, 8, 512, 512, 1024, 16, 1024, 1024, 1024]).tolist()))
            two = lambda name, n: [(cols(w_in, l, at[name] + 256 * i, 256), KT, 256) for i in range(n)]
            one = lambda name, n: [(cols(w_in, l, at[name], n), KT, n)]
            in0 = ring.plan(two("iq", 2) + one("ik", P) + one("iw", 8) + two("aq", 2) + two("ak", 2) + two("av", 2))
            gla0 = ring.plan(two("gq", 2) + two("gk", 2) + two("gv", 4) + one("glr", P))
            gr0 = ring.plan(two("g_r", 4))
            mg0 = ring.plan([u for n in range(4) for u in (
                (cols(w_in, l, at["ga"] + 256 * n, 256), KT, 256),
                (cols(args["p_attn_2"], l, 256 * n, 256, kt=4), 4, 256),
                (cols(w_in, l, at["gb"] + 256 * n, 256), KT, 256),
                (cols(args["p_gla_2"], l, 256 * n, 256), KT, 256))])
            out0 = ring.plan([(cols(args["w_mix_out_2"], l, 256 * i, 256), KT, 256) for i in range(4)])

            rows = lambda a, n: (a[bass.ds(l, 1), :].rearrange("o (n p) -> (o n) p", p=P), n)
            with ExitStack() as c2:
                stage_columns(core, c2, "vec2", [rows(args[k + "_2"], n) for k, n in (
                    ("b_mix_out", 8), ("ln1_g", 8), ("ln1_b", 8), ("ln2_g", 8), ("ln2_b", 8),
                    ("gla_b_gate", 4), ("gla_norm_g", 8), ("conv_b", 2 * FT))] + [
                        (args["conv_w_2"][bass.ds(l, 1), w:w + 1, :].rearrange("o w (n p) -> (o w n) p", p=P), 2 * FT)
                        for w in range(3)], (vec, fbias, ftaps), ring)

            keep = lambda dst, f=ACT.Copy, t0=0, **kw: (
                lambda act, view, j: act.activation(dst[:, t0 + j, :], view, f, **kw))
            tok = lambda dst, c0: (lambda act, view, j: act.activation(dst[:, j, c0:c0 + 256], view, ACT.Copy))
            with ExitStack() as mx:
                msb = lambda name, shape, dt=F32: mx.enter_context(nc.sbuf_tensor(name, shape, dt))
                xp = [msb(f"x_{n}", [P, KT, S], F32R) for n in ("hi", "lo")]
                att = msb("att_out2", [P, 4, S])
                gla = msb("gla_out", [P, KT, S])
                with ExitStack() as gx:
                    gsb = lambda name, shape, dt=F32: gx.enter_context(nc.sbuf_tensor(name, shape, dt))
                    gq, gk = gsb("gq", [P, 4, S]), gsb("gk", [P, 4, S])
                    gv = gsb("gv", [P, TT, GLA_H * GLA_DV])
                    etot = gsb("gla_chunk_decay", [P, GLA_H, NCH])
                    glr = gsb("glr", [GLA_RANK, 1, S])
                    with ExitStack() as ax:
                        asb = lambda name, shape, dt=F32: ax.enter_context(nc.sbuf_tensor(name, shape, dt))
                        aq, ak, iq = asb("aq", [P, 4, S]), asb("ak", [P, 4, S]), asb("iq", [P, 4, S])
                        av = asb("av", [P, TT, ATT_W2])
                        ik, iw = asb("ik", [P, S]), asb("iw", [P, TT, N_HEADS_2])
                        bias = asb("sel_bias", [P, TT, S])
                        ikr = bias[0:HD, TT - 1, :]
                        jobs = [(in0 + u, "T", keep(iq, t0=2 * u), xp) for u in range(2)]
                        jobs += [(in0 + 2, "T", lambda act, view, j: act.activation(ikr, view[0:HD, :], ACT.Copy), xp),
                                 (in0 + 3, "tok", keep(iw, scale=N_HEADS_2 ** -0.5), xp)]
                        for i, dst in enumerate((aq, ak)):
                            jobs += [(in0 + 4 + 2 * i + u, "T", keep(dst, t0=2 * u), xp) for u in range(2)]
                        jobs += [(in0 + 8 + u, "tok", tok(av, 256 * u), xp) for u in range(2)]
                        duo = lambda a: [[a[:, 0, :], a[:, 1, :]], [a[:, 2, :], a[:, 3, :]]]
                        turns = duo(iq) + [["key"], []] + duo(aq) + duo(ak) + [[], []]
                        cos, sin = att[:, 0, :], att[:, 1, :]
                        stage_angles(core, lc, args["positions_2"], cos, sin, att[:, 2, :].bitcast(I32),
                                     gla[:, 4:8, :], ring)
                        stage_project(core, lc, "in2", ring, jobs, feed=Split(core, lc, "x", x, *xp, KT), nbanks=5,
                                      rope=Rope(core, lc, turns, ikr, ik[:, :], cos, sin, gla[:, 0:4, :]))
                        jobs = []
                        for i, dst in enumerate((gq, gk)):
                            jobs += [(gla0 + 2 * i + u, "T", keep(dst, t0=2 * u), xp) for u in range(2)]
                        jobs += [(gla0 + 4 + u, "tok", tok(gv, 256 * u), xp) for u in range(4)]
                        jobs += [(gla0 + 8, "T", lambda act, view, j: act.activation(
                            glr[:, 0, :], view[0:GLA_RANK, :], ACT.Copy), xp)]
                        with ExitStack() as c2:
                            stage_select(core, c2, iq, ik, iw, bias, gla[:, 0:4, :], gla[:, 4:6, :], att[:, 0:3, :],
                                         Projection(core, lc, "gla_in", ring, jobs, bank0=4, nbanks=4), (2, 5, 9))
                        with ExitStack() as c2:
                            stage_attention(core, c2, "att2", N_HEADS_2, aq, ak, av, att, lambda t: P * (t + 1),
                                            lambda h, t: bias[:, t, 0:P * (t + 1)], scratch=gla)
                    gr = gsb("g_r", [P, KT, S])
                    with ExitStack() as c2:
                        csb = lambda name, shape: c2.enter_context(nc.sbuf_tensor(name, shape, F32))
                        jobs = [(gr0 + i, "T", keep(gr, ACT.Silu, t0=2 * i), xp) for i in range(4)]
                        stage_gla_gates(core, c2, glr, csb("gla_gate_w", [GLA_RANK, GLA_H * GLA_DK]),
                                        args["gla_w_gate_2"][bass.ds(l, 1), :, :].rearrange("o r n -> (o r) n"),
                                        vec[:, 40:44], gk, csb("gla_log_sums", [P, 4, S]), etot, gla,
                                        Projection(core, lc, "g_r", ring, jobs, bank0=4, nbanks=4))
                    with ExitStack() as c2:
                        stage_gla(core, c2, gq, gk, gv, etot, gla)
                    with ExitStack() as c2:
                        tmp = c2.enter_context(nc.sbuf_tensor("gla_ln_tmp", [P, 6, S], F32))
                        stage_layernorm(core, c2, "gla_ln", gla, gla, [[2 * h, 2 * h + 1] for h in range(GLA_H)], 1,
                                        vec[:, 44:52], None, tmp, gate=gr)
                with ExitStack() as c2:
                    csb = lambda name, n: c2.enter_context(nc.sbuf_tensor(name, [P, n, S], F32R))
                    ap = [csb(f"att_{n}", 4) for n in ("hi", "lo")]
                    gp = [csb(f"gla_{n}", KT) for n in ("hi", "lo")]
                    stage_merge(core, c2, ring, mg0, xp, ap, gp, gla, Split(core, lc, "att", att, *ap, 4),
                                Split(core, lc, "gla", gla, *gp, KT))
                with ExitStack() as c2:
                    csb = lambda name, n: c2.enter_context(nc.sbuf_tensor(name, [P, n, S], F32R))
                    hp = [csb(f"merged_{n}", KT) for n in ("hi", "lo")]
                    pre = core.sem(lc, "residual_scaled")

                    def put1(dve, view, n):
                        dve.tensor_scalar(x[:, n, :], x[:, n, :], ALPHA, vec[:, n:n + 1], ALU.mult, ALU.add)\
                            .then_inc(pre, 1)
                        dve.wait_ge(pre, n + 1)
                        return dve.tensor_tensor(x[:, n, :], view, x[:, n, :], ALU.add)
                    ffn = FfnStart(core, lc, "ffn2", l, args["w_up_2"])
                    stage_project(core, lc, "out2", ring,
                                  [(out0 + i, "T", (lambda dve, view, j, i=i: put1(dve, view, 2 * i + j)), hp)
                                   for i in range(4)], carrier="vector", ahead=ffn,
                                  feed=Split(core, lc, "merged", gla, *hp, KT))
            with ExitStack() as c2:
                xp = [c2.enter_context(nc.sbuf_tensor(f"x2_{n}", [P, KT, S], F32R)) for n in ("hi", "lo")]
                bufs = ffn_buffers(nc, c2, "two")
                stage_layernorm(core, lc, "ln1", x, x, [list(range(KT))], 0, vec[:, 8:16], vec[:, 16:24], bufs["c"],
                                ahead=ffn)

                def put(dve, n, view):
                    xn = x[:, bass.ds(n, 1), :] if not isinstance(n, int) else x[:, n:n + 1, :]
                    return dve.scalar_tensor_tensor(xn, xn, ALPHA, view, ALU.mult, ALU.add)
                stage_ffn(core, lc, "ffn2", l, ffn, args["w_down_2"], ftaps, fbias, 2,
                          ACT.Gelu_apprx_tanh, put, bufs, xp, Split(core, lc, "x2", x, *xp, KT))
            with ExitStack() as c2:
                tmp = c2.enter_context(nc.sbuf_tensor("ln2_tmp", [P, 3, S], F32))
                stage_layernorm(core, lc, "ln2", x, x, [list(range(KT))], 0, vec[:, 24:32], vec[:, 32:40], tmp)
            core.clear(core.sems[first_sem:])
            del core.sems[first_sem:]


def stage_finish(core, ctx, out):
    nc, ps = core.nc, core.ps
    xo = ctx.enter_context(nc.sbuf_tensor("x_out", [P, TT, D], F32))
    turned = core.sem(ctx, "finish_turned")
    kept = core.sem(ctx, "finish_kept")
    stored = core.sem(ctx, "finish_stored")
    with nc.Block() as block:
        @block.tensor
        def _(pe):
            for t in range(TT):
                for g in range(2):
                    for k in range(4):
                        ins = pe.transpose(ps[:, 2 * t + g, k * P:(k + 1) * P],
                                           core.x[:, 4 * g + k, t * P:(t + 1) * P], core.ident[:, :])
                    ins.then_inc(turned, 1)

        @block.scalar
        def _(act):
            for t in range(TT):
                for g in range(2):
                    act.wait_ge(turned, 2 * t + g + 1)
                    act.activation(xo[:, t, g * 512:(g + 1) * 512], ps[:, 2 * t + g, :], ACT.Copy).then_inc(kept, 1)

        @block.sync
        def _(sp):
            for t in range(TT):
                sp.wait_ge(kept, 2 * t + 2)
                sp.dma_start(out[0, t * P:(t + 1) * P, :], xo[:, t, :]).then_inc(stored, 16)
            sp.wait_ge(stored, 16 * TT)


def build(nc, args, out):
    with ExitStack() as ctx:
        core = Core(nc, ctx)
        with ExitStack() as c2:
            stage_start(core, c2, args)
            core.clear(core.sems)
            core.sems.clear()
        stack_one(core, nc, args)
        stack_two(core, nc, args)
        with ExitStack() as c2:
            stage_finish(core, c2, out)


def constants():
    f = np.zeros((P, 7 * P + 8), np.float32)
    f[:, 0:P] = np.eye(P)
    f[:, P:2 * P] = 1.0 / D
    f[:, 2 * P:3 * P] = 1.0 / 256
    f[0:HD, 3 * P:3 * P + HD] = f[HD:P, 3 * P + HD:4 * P] = 1.0 / HD
    for b in (0, HD):
        for i in range(8):
            f[b + i + 8, 4 * P + b + i] = -1.0
            f[b + i, 4 * P + b + i + 8] = 1.0
    f[0:HD, 5 * P:5 * P + HD] = f[0:HD, 5 * P + HD:6 * P] = np.eye(HD)
    f[0:HD, 6 * P:6 * P + HD] = f[0:HD, 6 * P + HD:7 * P] = f[0:HD, 4 * P:4 * P + HD]
    f[:, 7 * P:7 * P + 4] = [EPS, LN_EPS, 1.0, 0.0]
    inv = (np.float32(500000.0) ** (-np.arange(8, dtype=np.float32) * np.float32(2.0) / np.float32(16)))
    for b in (0, 8, HD, HD + 8):
        f[b:b + 8, 7 * P + 4] = inv
    f[:, 7 * P + 5] = np.pi / 2
    d = np.abs(np.arange(TABLE)[None, :] - 3 * P - np.arange(P)[:, None])
    times = (d <= 64) * 1 + ((d % 4 == 0) & (d <= 256)) * 1 + (d % 16 == 0) * 1
    attn = np.stack([d.astype(np.float64), np.where(times > 0, np.log(np.maximum(times, 1)), -BIG)], 1)
    t = np.arange(P)
    masks = np.stack([((t[:, None] // m) ^ (t[None, :] // m)) == 1 for m in LEVELS], 1)
    return {"const_f": f, "const_attn": attn.astype(np.float32).reshape(P, -1),
            "const_mask": masks.astype(np.int32).reshape(P, -1)}


_OUT = (1, S, D)


def kernel(**inputs):
    import concourse.bacc as _bacc
    from concourse.bass_utils import run_bass_kernel_spmd as _run

    nc = _bacc.Bacc("TRN2", target_bir_lowering=False, num_devices=1)
    arrays, args = {}, {}
    for name, a in {**inputs, **constants()}.items():
        a = np.ascontiguousarray(a)
        arrays[f"in_{name}"] = a
        args[name] = nc.dram_tensor(f"in_{name}", a.shape, mybir.dt.from_np(a.dtype), kind="ExternalInput").ap()
    out = nc.dram_tensor("out_x", _OUT, F32, kind="ExternalOutput").ap()
    build(nc, args, out)
    r = _run(nc, [arrays], core_ids=[0])
    return r.results[0]["out_x"]
```
